# Optimizing a Trainium2 kernel written in Bass

```python
import math
import jax, jax.numpy as jnp
from jax import lax
import numpy as np

D_MODEL = 1024
BATCH = 1
SEQ = 128
DEPTH = 1
DEC_BATCH = 1
DEC_SEQ = 512
PAST_LEN = 128

GRID_W = 64
M_INNER = 2 * D_MODEL
M_HEADDIM = 64
M_HEADS = M_INNER // M_HEADDIM
M_GROUPS = 4
M_HPG = M_HEADS // M_GROUPS
M_STATE = 128
M_CONV = 5
M_CHUNK = 128
M_XBC = M_INNER + 2 * M_GROUPS * M_STATE
R_WIDTH = D_MODEL
R_HEADSIZE = 64
R_HEADS = R_WIDTH // R_HEADSIZE
R_DECAY_RANK = 64
R_ICLR_RANK = 64
R_GATE_RANK = 128
R_COLS = 3 * R_WIDTH + 2 * R_DECAY_RANK + 2 * R_ICLR_RANK + R_GATE_RANK
IN_COLS = M_INNER + M_XBC + 2 * M_HEADS + R_COLS + 2 * D_MODEL
D_FF = -(-8 * D_MODEL // (3 * 256)) * 256

kernel_name = 'hybrid_ssd_rwkv7_diffusion_step'

def rmsnorm(x, w, eps=1e-6):
    xf = x.astype(jnp.float32)
    y = xf * lax.rsqrt(jnp.mean(xf * xf, axis=-1, keepdims=True) + eps)
    return (y * w).astype(x.dtype)

def centred_dwconv(x, w, b):
    pad = M_CONV // 2
    l = x.shape[1]
    xp = jnp.pad(x, ((0, 0), (pad, pad), (0, 0)))
    return b + sum(xp[:, i:i + l] * w[i] for i in range(M_CONV))

def qshift_seq(x):
    q = x.shape[-1] // 4
    prev = jnp.pad(x[:, :-1], ((0, 0), (1, 0), (0, 0)))
    nxt = jnp.pad(x[:, 1:], ((0, 0), (0, 1), (0, 0)))
    return jnp.concatenate([prev[..., :q], nxt[..., q:2 * q], prev[..., 2 * q:3 * q], nxt[..., 3 * q:]], axis=-1)

def qshift_grid(x):
    b, l, ch = x.shape
    rows = l // GRID_W
    g = x.reshape(b, rows, GRID_W, ch)
    q = ch // 4
    left = jnp.pad(g[:, :, :-1, :q], ((0, 0), (0, 0), (1, 0), (0, 0)))
    right = jnp.pad(g[:, :, 1:, q:2 * q], ((0, 0), (0, 0), (0, 1), (0, 0)))
    up = jnp.pad(g[:, :-1, :, 2 * q:3 * q], ((0, 0), (1, 0), (0, 0), (0, 0)))
    down = jnp.pad(g[:, 1:, :, 3 * q:], ((0, 0), (0, 1), (0, 0), (0, 0)))
    return jnp.concatenate([left, right, up, down], axis=-1).reshape(b, l, ch)

def segsum_exp(a):
    t = a.shape[-1]
    cs = jnp.cumsum(a, axis=-1)
    mask = jnp.tril(jnp.ones((t, t), dtype=bool))
    return jnp.exp(jnp.where(mask, cs[..., :, None] - cs[..., None, :], -jnp.inf))

def ssd_scan(x, dt, a, bm, cm, h0):
    b, l, _, p = x.shape
    nc = l // M_CHUNK
    xs = (x * dt[..., None]).reshape(b, nc, M_CHUNK, M_GROUPS, M_HPG, p)
    da = jnp.moveaxis((dt * a).reshape(b, nc, M_CHUNK, M_GROUPS, M_HPG), 2, -1)
    bc = bm.reshape(b, nc, M_CHUNK, M_GROUPS, M_STATE)
    cc = cm.reshape(b, nc, M_CHUNK, M_GROUPS, M_STATE)
    da_cs = jnp.cumsum(da, axis=-1)
    lmat = segsum_exp(da)
    cb = jnp.einsum('bclgn,bcsgn->bcgls', cc, bc)
    y_diag = jnp.einsum('bcgls,bcgels,bcsgep->bclgep', cb, lmat, xs)
    decay_states = jnp.exp(da_cs[..., -1:] - da_cs)
    states = jnp.einsum('bclgn,bcgel,bclgep->bcgepn', bc, decay_states, xs)
    h0g = h0.astype(jnp.float32).reshape(b, M_GROUPS, M_HPG, p, M_STATE)
    states = jnp.concatenate([h0g[:, None], states], axis=1)
    chunk_a = jnp.moveaxis(jnp.pad(da_cs[..., -1], ((0, 0), (1, 0), (0, 0), (0, 0))), 1, -1)
    decay_chunk = segsum_exp(chunk_a)
    new_states = jnp.einsum('bgezc,bcgepn->bzgepn', decay_chunk, states)
    prev_states, final = new_states[:, :-1], new_states[:, -1]
    y_off = jnp.einsum('bclgn,bcgepn,bcgel->bclgep', cc, prev_states, jnp.exp(da_cs))
    y = (y_diag + y_off).reshape(b, l, M_HEADS, p)
    return y, final.reshape(b, M_HEADS, p, M_STATE)

def mamba_branch(z, xbc, dt_raw, h0_f, h0_b, p):
    f32 = jnp.float32
    b, l, _ = z.shape
    xbc = jax.nn.silu(centred_dwconv(xbc, p['conv_w'], p['conv_b'])).astype(f32)
    xm, bm, cm = jnp.split(xbc, [M_INNER, M_INNER + M_GROUPS * M_STATE], axis=-1)
    xm = xm.reshape(b, l, M_HEADS, M_HEADDIM)
    bm = bm.reshape(b, l, M_GROUPS, M_STATE)
    cm = cm.reshape(b, l, M_GROUPS, M_STATE)
    dt = jax.nn.softplus(dt_raw.reshape(b, l, 2, M_HEADS).astype(f32) + p['dt_bias'].astype(f32))
    a = -jnp.exp(p['a_log'].astype(f32))
    y_f, hf = ssd_scan(xm, dt[:, :, 0], a[0], bm, cm, h0_f)
    y_b, hb = ssd_scan(xm[:, ::-1], dt[:, ::-1, 1], a[1], bm[:, ::-1], cm[:, ::-1], h0_b)
    y = y_f + y_b[:, ::-1] + p['d_skip'].astype(f32)[:, None] * xm
    y = y.reshape(b, l, M_INNER) * jax.nn.silu(z.astype(f32))
    yg = y.reshape(b, l, M_GROUPS, M_INNER // M_GROUPS)
    yg = yg * lax.rsqrt(jnp.mean(yg * yg, axis=-1, keepdims=True) + 1e-5)
    y = yg.reshape(b, l, M_INNER) * p['m_norm_w']
    return y.astype(z.dtype), hf, hb

def to_heads(t):
    return t.reshape(*t.shape[:-1], R_HEADS, R_HEADSIZE)

def wkv7_scan(r, w, k, v, kk, a, s0):
    def step(s, inp):
        rt, wt, kt, vt, kkt, at = inp
        sa = jnp.einsum('dbhij,dbhj->dbhi', s, -kkt)
        s = s * wt[..., None, :] + sa[..., None] * (kkt * at)[..., None, :] + vt[..., None] * kt[..., None, :]
        return s, jnp.einsum('dbhij,dbhj->dbhi', s, rt)
    xs = tuple(jnp.moveaxis(t, 2, 0) for t in (r, w, k, v, kk, a))
    s, y = lax.scan(step, s0, xs)
    return jnp.moveaxis(y, 0, 2), s

def rwkv_branch(rw, shifted, s0_f, s0_b, p):
    f32 = jnp.float32
    b, l, _ = rw.shape
    xx = (rw + p['mu_shift'] * (shifted - rw)).astype(f32)
    widths = [R_WIDTH, R_DECAY_RANK, R_DECAY_RANK, R_WIDTH, R_WIDTH, R_ICLR_RANK, R_ICLR_RANK, R_GATE_RANK]
    r, wlf, wlb, k, v, alf, alb, glo = jnp.split(xx, np.cumsum(widths)[:-1].tolist(), axis=-1)
    w_logit = p['w0'][:, None, None, :] + jnp.einsum('dblr,drc->dblc', jnp.tanh(jnp.stack([wlf, wlb])), p['w2'])
    decay = jnp.exp(-jnp.exp(-jax.nn.softplus(-w_logit.astype(f32)) - 0.5))
    a = jax.nn.sigmoid(p['a0'][:, None, None, :] + jnp.einsum('dblr,drc->dblc', jnp.stack([alf, alb]), p['a2'])).astype(f32)
    g = jax.nn.sigmoid(glo) @ p['g2']
    kk = to_heads(k * p['k_k'])
    kk = kk * lax.rsqrt(jnp.sum(kk * kk, axis=-1, keepdims=True) + 1e-12)
    k_dir = k[None] * (1 + (a - 1) * p['k_a'])
    rh, vh = to_heads(r), to_heads(v)
    both = lambda t: jnp.stack([t, t[:, ::-1]])
    per_dir = lambda t: jnp.stack([t[0], t[1][:, ::-1]])
    y, s = wkv7_scan(both(rh), to_heads(per_dir(decay)), to_heads(per_dir(k_dir)), both(vh), both(kk),
                     to_heads(per_dir(a)), jnp.stack([s0_f, s0_b]).astype(f32))
    y = y[0] + y[1][:, ::-1]
    mean = jnp.mean(y, axis=-1, keepdims=True)
    var = jnp.mean(jnp.square(y - mean), axis=-1, keepdims=True)
    yn = ((y - mean) * lax.rsqrt(var + 64e-5)).reshape(b, l, R_WIDTH) * p['lnx_w'] + p['lnx_b']
    k_mean = to_heads(0.5 * (k_dir[0] + k_dir[1]))
    bonus = jnp.sum(rh * k_mean * p['r_k'], axis=-1, keepdims=True) * vh
    out = (yn + bonus.reshape(b, l, R_WIDTH)) * g
    return out.astype(rw.dtype), s[0], s[1]

def trunk_layer(x, mod, on_grid, ssm_f, ssm_b, wkv_f, wkv_b, p):
    sh1, sc1, gt1, sh2, sc2, gt2 = jnp.split(mod, 6, axis=-1)
    h = rmsnorm(x, p['norm1_w']) * (1 + sc1) + sh1
    proj = h @ p['w_in']
    o1 = M_INNER
    o2 = o1 + M_XBC
    o3 = o2 + 2 * M_HEADS
    o4 = o3 + R_COLS
    z, xbc, dt_raw, rw, gates = jnp.split(proj, [o1, o2, o3, o4], axis=-1)
    y_m, ssm_f, ssm_b = mamba_branch(z, xbc, dt_raw, ssm_f, ssm_b, p)
    shifted = qshift_grid(rw) if on_grid else qshift_seq(rw)
    y_r, wkv_f, wkv_b = rwkv_branch(rw, shifted, wkv_f, wkv_b, p)
    g_m, g_r = jnp.split(jax.nn.sigmoid(gates), 2, axis=-1)
    mix = (g_m * (y_m @ p['w_m_out']) + g_r * (y_r @ p['w_r_out'])) @ p['w_o']
    x = x + gt1 * mix
    h = rmsnorm(x, p['norm2_w']) * (1 + sc2) + sh2
    gg, uu = jnp.split(h @ p['w_gu'], 2, axis=-1)
    x = x + gt2 * ((jax.nn.silu(gg) * uu) @ p['w_down'])
    return x, ssm_f, ssm_b, wkv_f, wkv_b

def setup_inputs(seed: int = 0) -> dict:
    key = jax.random.key(seed)
    ks = iter(jax.random.split(key, 48))
    D = D_MODEL

    def nrm(shape, scale):
        return scale * jax.random.normal(next(ks), shape, jnp.float32)

    def unif(shape, lo, hi):
        return jax.random.uniform(next(ks), shape, jnp.float32, lo, hi)

    dt0 = jnp.exp(unif((DEPTH, 2, M_HEADS), math.log(1e-3), math.log(1e-1)))
    dt_bias = dt0 + jnp.log(-jnp.expm1(-dt0))
    a_log = jnp.log(unif((DEPTH, 2, M_HEADS), 1.0, 16.0))
    return {
        'x_prompt': nrm((BATCH, SEQ, D), 1.0),
        'x_sample': nrm((DEC_BATCH, DEC_SEQ, D), 1.0),
        'state_ssm_fwd': nrm((DEC_BATCH, DEPTH, M_HEADS, M_HEADDIM, M_STATE), 0.1),
        'state_ssm_bwd': nrm((DEC_BATCH, DEPTH, M_HEADS, M_HEADDIM, M_STATE), 0.1),
        'state_wkv_fwd': nrm((DEC_BATCH, DEPTH, R_HEADS, R_HEADSIZE, R_HEADSIZE), 0.5),
        'state_wkv_bwd': nrm((DEC_BATCH, DEPTH, R_HEADS, R_HEADSIZE, R_HEADSIZE), 0.5),
        'c': nrm((DEC_BATCH, D), 1.0),
        'c_ctx': nrm((D,), 1.0),
        'norm1_w': 1.0 + nrm((DEPTH, D), 0.02),
        'norm2_w': 1.0 + nrm((DEPTH, D), 0.02),
        'w_ada': nrm((DEPTH, D, 6 * D), D ** -0.5),
        'b_ada': nrm((DEPTH, 6 * D), 0.02),
        'w_in': nrm((DEPTH, D, IN_COLS), D ** -0.5),
        'conv_w': nrm((DEPTH, M_CONV, M_XBC), M_CONV ** -0.5),
        'conv_b': nrm((DEPTH, M_XBC), 0.02),
        'dt_bias': dt_bias,
        'a_log': a_log,
        'd_skip': 1.0 + nrm((DEPTH, M_HEADS), 0.1),
        'm_norm_w': 1.0 + nrm((DEPTH, M_INNER), 0.02),
        'mu_shift': unif((DEPTH, R_COLS), 0.0, 1.0),
        'w0': -0.5 + nrm((DEPTH, 2, R_WIDTH), 0.5),
        'w2': nrm((DEPTH, 2, R_DECAY_RANK, R_WIDTH), R_DECAY_RANK ** -0.5),
        'a0': nrm((DEPTH, 2, R_WIDTH), 0.1),
        'a2': nrm((DEPTH, 2, R_ICLR_RANK, R_WIDTH), R_ICLR_RANK ** -0.5),
        'g2': nrm((DEPTH, R_GATE_RANK, R_WIDTH), R_GATE_RANK ** -0.5),
        'k_k': 0.85 + nrm((DEPTH, R_WIDTH), 0.05),
        'k_a': 1.0 + nrm((DEPTH, R_WIDTH), 0.05),
        'r_k': nrm((DEPTH, R_HEADS, R_HEADSIZE), 0.1),
        'lnx_w': 1.0 + nrm((DEPTH, R_WIDTH), 0.02),
        'lnx_b': nrm((DEPTH, R_WIDTH), 0.02),
        'w_m_out': nrm((DEPTH, M_INNER, D), M_INNER ** -0.5),
        'w_r_out': nrm((DEPTH, R_WIDTH, D), R_WIDTH ** -0.5),
        'w_o': nrm((DEPTH, D, D), D ** -0.5),
        'w_gu': nrm((DEPTH, D, 2 * D_FF), D ** -0.5),
        'w_down': nrm((DEPTH, D_FF, D), D_FF ** -0.5),
        'final_norm_w': 1.0 + nrm((D,), 0.02),
    }

def reference(x_prompt, x_sample, state_ssm_fwd, state_ssm_bwd, state_wkv_fwd, state_wkv_bwd,
              c, c_ctx, norm1_w, norm2_w, w_ada, b_ada, w_in, conv_w, conv_b, dt_bias, a_log,
              d_skip, m_norm_w, mu_shift, w0, w2, a0, a2, g2, k_k, k_a, r_k, lnx_w, lnx_b,
              w_m_out, w_r_out, w_o, w_gu, w_down, final_norm_w):
    f32 = jnp.float32
    bp = x_prompt.shape[0]
    ctx, lat = x_prompt, x_sample
    new_sf, new_sb, new_wf, new_wb = [], [], [], []
    for l in range(DEPTH):
        p = dict(norm1_w=norm1_w[l], norm2_w=norm2_w[l], w_in=w_in[l], conv_w=conv_w[l], conv_b=conv_b[l],
                 dt_bias=dt_bias[l], a_log=a_log[l], d_skip=d_skip[l], m_norm_w=m_norm_w[l],
                 mu_shift=mu_shift[l], w0=w0[l], w2=w2[l], a0=a0[l], a2=a2[l], g2=g2[l], k_k=k_k[l],
                 k_a=k_a[l], r_k=r_k[l], lnx_w=lnx_w[l], lnx_b=lnx_b[l], w_m_out=w_m_out[l],
                 w_r_out=w_r_out[l], w_o=w_o[l], w_gu=w_gu[l], w_down=w_down[l])
        mod_ctx = (jax.nn.silu(c_ctx) @ w_ada[l] + b_ada[l])[None, None, :]
        mod_lat = (jax.nn.silu(c) @ w_ada[l] + b_ada[l])[:, None, :]
        z_ssm = jnp.zeros((bp, M_HEADS, M_HEADDIM, M_STATE), f32)
        z_wkv = jnp.zeros((bp, R_HEADS, R_HEADSIZE, R_HEADSIZE), f32)
        ctx, sf, sb, wf, wb = trunk_layer(ctx, mod_ctx, False, z_ssm, z_ssm, z_wkv, z_wkv, p)
        new_sf.append(sf)
        new_sb.append(sb)
        new_wf.append(wf)
        new_wb.append(wb)
        lat, _, _, _, _ = trunk_layer(lat, mod_lat, True, state_ssm_fwd[:, l], state_ssm_bwd[:, l],
                                      state_wkv_fwd[:, l], state_wkv_bwd[:, l], p)
    y_prompt = rmsnorm(ctx, final_norm_w)
    y_sample = rmsnorm(lat, final_norm_w)
    new_ssm_fwd = jnp.stack(new_sf, axis=1).astype(x_prompt.dtype)
    new_ssm_bwd = jnp.stack(new_sb, axis=1).astype(x_prompt.dtype)
    new_wkv_fwd = jnp.stack(new_wf, axis=1).astype(x_prompt.dtype)
    new_wkv_bwd = jnp.stack(new_wb, axis=1).astype(x_prompt.dtype)
    return (y_prompt, y_sample, new_ssm_fwd, new_ssm_bwd, new_wkv_fwd, new_wkv_bwd)


_drawn_inputs = setup_inputs


def setup_inputs(seed=0):
    import zlib

    import numpy as np

    out = dict(_drawn_inputs(seed))
    spreads = {}
    factors = {'state_ssm_fwd': 3.854,
     'state_ssm_bwd': 4.651,
     'state_wkv_fwd': 8.0,
     'state_wkv_bwd': 8.0,
     'norm2_w': 4.224,
     'd_skip': 8.0,
     'm_norm_w': 8.0,
     'lnx_w': 8.0,
     'lnx_b': 8.0,
     'final_norm_w': 2.926}
    for name, (base, spread) in spreads.items():
        noise = np.random.default_rng([zlib.crc32(name.encode()), seed]).standard_normal(out[name].shape)
        drawn = base * np.exp(spread * noise) if base else spread * noise
        out[name] = __import__('jax').numpy.asarray(drawn.astype(out[name].dtype))
    for name, factor in factors.items():
        out[name] = (out[name] * factor).astype(out[name].dtype)
    return out
```

```python
from contextlib import ExitStack

import numpy as np
import concourse.bass as bass
import concourse.mybir as mybir

P = 128
D = 1024
KD = D // P
CTX, LAT = 128, 512
T = CTX + LAT
SEG = ((0, 0, CTX), (1, CTX, T))
BANKS = ((0, 512), (512, T))
GRID_W = 64
M_INNER, M_HEADS, M_GROUPS, M_STATE, M_CONV = 2048, 32, 4, 128, 5
HPG = M_HEADS // M_GROUPS
HD = 64
GI = M_INNER // M_GROUPS
KI = M_INNER // P
NCH = T // P
R_HEADS = 16
PAIRS = R_HEADS // 2
WC = 64
NWC = T // WC
D_FF = 2816
KF = D_FF // P
R_COLS = 3 * D + 2 * 64 + 2 * 64 + 128
QUARTER = R_COLS // 4
LOG_DECAY = float(np.exp(-0.5))

F32 = mybir.dt.float32
ACT = mybir.ActivationFunctionType
ALU = mybir.AluOpType
AX = mybir.AxisListType

VEC = dict(norm1=KD, norm2=KD, final=KD, b_ada=96, conv_w=24 * M_CONV, conv_b=24, m_norm=KI, mu=27,
           w0=16, a0=16, k_k=KD, k_a=KD, r_k=KD, lnx_w=KD, lnx_b=KD)
ROW = dict(dt_bias=64, a_log=64, d_skip=32)
LEVELS = 6
STRICT, UPTO, LEVEL = 0, 1, 2
CST = dict(ident=P, ones=P, head_ones=P, tri=2 * P, wmask=2 * (2 + LEVELS) * WC, reset=2 * T,
           qmask=27 * 4, ident_w=WC)


class Resident:
    pass


def offsets(widths):
    at, out = 0, {}
    for name, n in widths.items():
        out[name] = (at, at + n)
        at += n
    return out, at


VEC_AT, VEC_N = offsets(VEC)
ROW_AT, ROW_N = offsets(ROW)
CST_AT, CST_N = offsets(CST)


def project(pe, psum, w, rhs, k_tiles):
    for lo, hi in BANKS:
        for k in range(k_tiles):
            last = pe.matmul(psum[:, lo:hi], w[:, k, :], rhs[:, k, lo:hi],
                             start=(k == 0), stop=(k == k_tiles - 1))
    return last


def stream(sp, n, load, used):
    load(0, 0)
    load(0, 1)
    if n > 2:
        with sp.Fori(1, n // 2) as it:
            for s in (0, 1):
                sp.wait_ge(used, 2 * it + s - 1)
                load(it, s)


def tiles_of(w):
    return w.rearrange("p (k m) -> p k m", m=P)


def phase_load(nc, sem, io, g):
    cst_in, vec_in, row_in = sem("cst_in"), sem("vec_in"), sem("row_in")
    derived = sem("derived")
    with nc.Block() as block:
        @block.sync
        def _(sp):
            sp.dma_start(g.cst[:, :], io["cst"]).then_inc(cst_in, 16)
            sp.dma_start(g.vec[:, :], io["vec"]).then_inc(vec_in, 16)
            sp.dma_start(g.row[:, :], io["row"]).then_inc(row_in, 16)

        @block.vector
        def _(dve):
            dve.wait_ge(vec_in, 16)
            dve.wait_ge(cst_in, 16)
            dve.tensor_tensor(g.mu_q[:, :, :], g.qmask, g.v("mu").unsqueeze(2).to_broadcast([P, 27, 4]),
                              ALU.mult).then_inc(derived, 1)
            dve.tensor_scalar(g.mu_own[:, :], g.v("mu"), -1.0, 1.0, ALU.mult, ALU.add).then_inc(derived, 1)
            dve.tensor_scalar(g.k_a_c[:, :], g.v("k_a"), -1.0, 1.0, ALU.mult, ALU.add).then_inc(derived, 1)

        @block.scalar
        def _(act):
            act.wait_ge(row_in, 16)
            act.activation(g.neg_a[:, :], g.r("a_log"), ACT.Exp).then_inc(derived, 1)
            act.wait_ge(derived, 4)
            act.mul(g.neg_a[:, :], g.neg_a[:, :], -1.0).then_inc(derived, 1)


def phase_modulation(nc, sem, io, g):
    PER, GROUPS = 3, 16
    cond_in, cond_ready = sem("cond_in"), sem("cond_ready")
    w_in = [sem("ada_w_in0"), sem("ada_w_in1")]
    psum_full, psum_free = sem("ada_psum_full"), sem("ada_psum_free")
    mod_done = sem("mod_done")
    with ExitStack() as ctx:
        cond = ctx.enter_context(nc.sbuf_tensor("cond", [P, KD, 2], F32))
        w = ctx.enter_context(nc.sbuf_tensor("ada_w", [P, 2, PER * KD * P], F32))
        ps = ctx.enter_context(nc.psum_tensor("ada_ps", [P, 2, 512], F32))
        block = ctx.enter_context(nc.Block())

        @block.sync
        def _(sp):
            sp.dma_start(cond[:, :, :], io["cond"]).then_inc(cond_in, 16)
            stream(sp, GROUPS, lambda it, s: sp.dma_start(w[:, s, :], io["w_ada"][2 * it + s])
                   .then_inc(w_in[s], 16), used=psum_full)

        @block.scalar
        def _(act):
            act.wait_ge(cond_in, 16)
            act.activation(cond[:, :, :], cond[:, :, :], ACT.Silu).then_inc(cond_ready, 1)

        @block.tensor
        def _(pe):
            pe.wait_ge(cond_ready, 1)
            with pe.Fori(0, GROUPS // 2) as it:
                for s in (0, 1):
                    wt = tiles_of(w[:, s, :])
                    pe.wait_ge(w_in[s], 16 * it + 16)
                    pe.wait_ge(psum_free, 2 * it + s + 1)
                    for m in range(PER):
                        for k in range(KD):
                            last = pe.matmul(ps[:, s, 2 * m:2 * m + 2], wt[:, m * KD + k, :], cond[:, k, :],
                                             start=(k == 0), stop=(k == KD - 1))
                    last.then_inc(psum_full, 1)

        @block.vector
        def _(dve):
            dve.sem_inc(psum_free, 2)
            b_ada = g.v("b_ada").rearrange("p (g n) -> p g n", n=2 * PER)
            mod = g.mod[:, :, :].rearrange("p (g m) c -> p g (m c)", m=PER)
            with dve.Fori(0, GROUPS // 2) as it:
                for s in (0, 1):
                    dve.wait_ge(psum_full, 2 * it + s + 1)
                    dve.tensor_tensor(mod[:, bass.ds(2 * it + s, 1), :].squeeze(1), ps[:, s, 0:2 * PER],
                                      b_ada[:, bass.ds(2 * it + s, 1), :].squeeze(1),
                                      ALU.add).then_inc(psum_free, 1)


def phase_norm(nc, sem, g, tag, weight, shift_at, out):
    squared, square_free = sem(tag + "_squared"), sem(tag + "_square_free")
    inv_done, rstd_done, chain = sem(tag + "_inv_done"), sem(tag + "_rstd_done"), sem(tag + "_norm_chain")
    with ExitStack() as ctx:
        sq = ctx.enter_context(nc.sbuf_tensor(tag + "_sq", [P, 2, T], F32))
        rstd = ctx.enter_context(nc.sbuf_tensor(tag + "_rstd", [P, T], F32))
        gain = ctx.enter_context(nc.sbuf_tensor(tag + "_gain", [P, KD, 2], F32))
        ps = ctx.enter_context(nc.psum_tensor(tag + "_ps", [P, 1024], F32))
        block = ctx.enter_context(nc.Block())

        @block.scalar
        def _(act):
            for k in range(KD):
                if k >= 2:
                    act.wait_ge(square_free, k - 1)
                act.activation(sq[:, k % 2, :], g.x[:, k, :], ACT.Square).then_inc(squared, 1)
            act.wait_ge(inv_done, 2)
            act.activation(rstd[:, :], rstd[:, :], ACT.Sqrt).then_inc(rstd_done, 1)

        @block.tensor
        def _(pe):
            for k in range(KD):
                pe.wait_ge(squared, k + 1)
                for lo, hi in BANKS:
                    last = pe.matmul(ps[:, lo:hi], g.ones, sq[:, k % 2, lo:hi],
                                     start=(k == 0), stop=(k == KD - 1))
                last.then_inc(square_free, 1)
        @block.vector
        def _(dve):
            if shift_at is not None:
                scale = g.mod[:, shift_at + KD:shift_at + 2 * KD, :]
                dve.scalar_tensor_tensor(out=gain[:, :, :], in0=scale, scalar=1.0,
                                         in1=weight.unsqueeze(2).to_broadcast([P, KD, 2]),
                                         op0=ALU.add, op1=ALU.mult).then_inc(chain, 1)
            else:
                dve.tensor_copy(gain[:, :, :], weight.unsqueeze(2).to_broadcast([P, KD, 2])).then_inc(chain, 1)
            dve.wait_ge(square_free, KD)
            dve.tensor_scalar(rstd[:, :], ps[:, 0:T], 1.0 / D, 1e-6, ALU.mult, ALU.add).then_inc(inv_done, 1)
            dve.wait_ge(inv_done, 1)
            dve.reciprocal(rstd[:, :], rstd[:, :]).then_inc(inv_done, 1)
            dve.wait_ge(rstd_done, 1)
            dve.wait_ge(chain, 1)
            for k in range(KD):
                dve.tensor_tensor(out[:, k, :], g.x[:, k, :], rstd[:, :], ALU.mult).then_inc(chain, 1)
            for k in range(KD):
                dve.wait_ge(chain, k + 2)
                for c, lo, hi in SEG:
                    if shift_at is not None:
                        dve.tensor_scalar(out[:, k, lo:hi], out[:, k, lo:hi], gain[:, k, c:c + 1],
                                          g.mod[:, shift_at + k, c:c + 1], ALU.mult, ALU.add)
                    else:
                        dve.tensor_scalar(out[:, k, lo:hi], out[:, k, lo:hi], gain[:, k, c:c + 1], None,
                                          ALU.mult)


def phase_conv(nc, sem, io, g, tag, first, n, keep, tok):
    w_in = [sem(tag + "_w_in0"), sem(tag + "_w_in1")]
    psum_full, psum_free = sem(tag + "_psum_full"), sem(tag + "_psum_free")
    padded, pad_free, conv = sem(tag + "_padded"), sem(tag + "_pad_free"), sem(tag + "_conv_chain")
    conv_free, act_done, act_free = sem(tag + "_conv_free"), sem(tag + "_act_done"), sem(tag + "_act_free")
    tr_full, tr_free, kept = sem(tag + "_tr_full"), sem(tag + "_tr_free"), sem(tag + "_kept")
    PAD = M_CONV // 2
    W_PAD = T + 3 * PAD
    W_OUT = T + PAD
    PARTS = ((0, 0, CTX), (CTX + PAD, CTX, T))
    with ExitStack() as ctx:
        w = ctx.enter_context(nc.sbuf_tensor(tag + "_w", [P, 2, KD * P], F32))
        pad = ctx.enter_context(nc.sbuf_tensor(tag + "_pad", [P, 2, W_PAD], F32))
        acc = ctx.enter_context(nc.sbuf_tensor(tag + "_acc", [P, 2, W_OUT], F32))
        res = ctx.enter_context(nc.sbuf_tensor(tag + "_res", [P, 2, T], F32))
        ps = ctx.enter_context(nc.psum_tensor(tag + "_ps", [P, 2, 1024], F32))
        pt = ctx.enter_context(nc.psum_tensor(tag + "_pt", [P, 2, 1024], F32))
        zeroed = sem(tag + "_pad_zeroed")
        block = ctx.enter_context(nc.Block())
        cw = g.v("conv_w").rearrange("p (j i) -> p j i", i=M_CONV)

        @block.sync
        def _(sp):
            stream(sp, n, lambda it, s: sp.dma_start(w[:, s, :], io["w_xbc"][2 * it + s + first])
                   .then_inc(w_in[s], 16), used=psum_full)

        @block.gpsimd
        def _(pool):
            pool.memset(pad[:, :, :], 0.0).then_inc(zeroed, 1)

        @block.tensor
        def _(pe):
            def tile(it, s):
                pe.wait_ge(w_in[s], 16 * it + 16)
                pe.wait_ge(psum_free, 2 * it + s + 1)
                project(pe, ps[:, s, :], tiles_of(w[:, s, :]), g.h, KD).then_inc(psum_full, 1)

            def turn(it, s):
                if tok is None:
                    return
                pe.wait_ge(act_done, 2 * it + s + 1)
                pe.wait_ge(tr_free, 2 * it + s + 1)
                for c in range(NCH):
                    last = pe.transpose(pt[:, s, P * c:P * c + P], res[:, s, P * c:P * c + P], g.ident)
                last.then_inc(tr_full, 1)

            tile(0, 0)
            if n > 2:
                with pe.Fori(0, n // 2 - 1) as it:
                    tile(it, 1)
                    turn(it, 0)
                    tile(it + 1, 0)
                    turn(it, 1)
            tile(n // 2 - 1, 1)
            turn(n // 2 - 1, 0)
            turn(n // 2 - 1, 1)

        @block.scalar
        def _(act):
            act.sem_inc(psum_free, 2)
            act.sem_inc(conv_free, 2)
            act.wait_ge(zeroed, 1)
            with act.Fori(0, n // 2) as it:
                for s in (0, 1):
                    act.wait_ge(psum_full, 2 * it + s + 1)
                    act.wait_ge(pad_free, 2 * it + s + 1)
                    act.activation(pad[:, s, PAD:PAD + CTX], ps[:, s, 0:CTX], ACT.Copy)
                    act.activation(pad[:, s, 2 * PAD + CTX:2 * PAD + T], ps[:, s, CTX:T],
                                   ACT.Copy).then_inc(padded, 1)
                    act.wait_ge(padded, 2 * it + s + 1)
                    act.sem_inc(psum_free, 1)
                for s in (0, 1):
                    act.wait_ge(conv, 2 * M_CONV * it + M_CONV * s + M_CONV)
                    act.wait_ge(act_free, 2 * it + s + 1)
                    for at, lo, hi in PARTS:
                        last = act.activation(res[:, s, lo:hi], acc[:, s, at:at + hi - lo], ACT.Silu,
                                              bias=g.v("conv_b")[:, bass.ds(2 * it + s + first, 1)])
                    last.then_inc(act_done, 1)
                    act.wait_ge(act_done, 2 * it + s + 1)
                    act.sem_inc(conv_free, 1)

        @block.vector
        def _(dve):
            dve.sem_inc(pad_free, 2)
            dve.sem_inc(tr_free, 2)
            dve.sem_inc(act_free, 2)
            with dve.Fori(0, n // 2) as it:
                for s in (0, 1):
                    dve.wait_ge(padded, 2 * it + s + 1)
                    dve.wait_ge(conv_free, 2 * it + s + 1)
                    for i in range(M_CONV):
                        src, wi = pad[:, s, i:i + W_OUT], cw[:, bass.ds(2 * it + s + first, 1), i]
                        if i == 0:
                            dve.tensor_scalar(acc[:, s, :], src, wi, None, ALU.mult).then_inc(conv, 1)
                        else:
                            dve.wait_ge(conv, 2 * M_CONV * it + M_CONV * s + i)
                            dve.scalar_tensor_tensor(out=acc[:, s, :], in0=src, scalar=wi, in1=acc[:, s, :],
                                                     op0=ALU.mult, op1=ALU.add).then_inc(conv, 1)
                    dve.wait_ge(conv, 2 * M_CONV * it + M_CONV * s + M_CONV)
                    dve.sem_inc(pad_free, 1)
                for s in (0, 1):
                    if keep is not None:
                        dve.wait_ge(act_done, 2 * it + s + 1)
                        dve.tensor_copy(keep[:, bass.ds(2 * it + s, 1), :].squeeze(1),
                                        res[:, s, :]).then_inc(kept, 1)
                        dve.wait_ge(kept, 2 * it + s + 1)
                    if tok is not None:
                        dve.wait_ge(tr_full, 2 * it + s + 1)
                        dve.tensor_copy(tok[:, :, bass.ds((2 * it + s) * P, P)],
                                        pt[:, s, 0:T].rearrange("p (c m) -> p c m", m=P)).then_inc(tr_free, 1)
                    dve.sem_inc(act_free, 1)


DT_PARTS = ("dt", "da", "cs", "ecs", "edec", "etot")


def phase_dt(nc, sem, io, g, dts):
    w_in, raw_full, cum_full = sem("dt_w_in"), sem("dt_raw_full"), sem("dt_cum_full")
    vec, act_done = sem("dt_vec"), sem("dt_act")
    N = NCH * 64
    SERIES = [1.0 / n for n in (13, 11, 9, 7, 5, 3)]
    with ExitStack() as ctx:
        w = ctx.enter_context(nc.sbuf_tensor("dt_w", [P, KD, 64], F32))
        raw = ctx.enter_context(nc.sbuf_tensor("dt_raw", [P, NCH, 64], F32))
        e = ctx.enter_context(nc.sbuf_tensor("dt_e", [P, NCH, 64], F32))
        s2 = ctx.enter_context(nc.sbuf_tensor("dt_s2", [P, NCH, 64], F32))
        q = ctx.enter_context(nc.sbuf_tensor("dt_q", [P, NCH, 64], F32))
        pr = ctx.enter_context(nc.psum_tensor("dt_pr", [P, 512], F32))
        pc = ctx.enter_context(nc.psum_tensor("dt_pc", [P, 512], F32))
        pt = ctx.enter_context(nc.psum_tensor("dt_pt", [P, 512], F32))
        block = ctx.enter_context(nc.Block())
        view = lambda p: p[:, 0:N].rearrange("p (c n) -> p c n", n=64)
        over_chunks = lambda r: r.unsqueeze(1).to_broadcast([P, NCH, 64])

        @block.sync
        def _(sp):
            sp.dma_start(w[:, :, :], io["w_dt"].rearrange("p (k n) -> p k n", n=64)).then_inc(w_in, 16)

        @block.tensor
        def _(pe):
            pe.wait_ge(w_in, 16)
            for c in range(NCH):
                for k in range(KD):
                    last = pe.matmul(pr[:, 64 * c:64 * c + 64], g.h[:, k, P * c:P * c + P], w[:, k, :],
                                     start=(k == 0), stop=(k == KD - 1))
            last.then_inc(raw_full, 1)
            pe.wait_ge(vec, DA_DONE)
            for d in (0, 1):
                half = slice(32 * d, 32 * d + 32)
                pe.matmul(view(pc)[:, :, half], g.tri[:, d, :], dts["da"][:, :, half], start=True, stop=True)
            pe.matmul(view(pt), g.ones, dts["da"][:, :, :], start=True, stop=True).then_inc(cum_full, 1)

        steps = [0]

        @block.vector
        def _(dve):
            def then(ins):
                steps[0] += 1
                ins.then_inc(vec, 1)
                dve.wait_ge(vec, steps[0])

            dve.wait_ge(raw_full, 1)
            then(dve.tensor_tensor(raw[:, :, :], view(pr), over_chunks(g.r("dt_bias")), ALU.add))
            dve.wait_ge(act_done, 2)
            then(dve.tensor_scalar(q[:, :, :], e[:, :, :], 2.0, None, ALU.add))
            then(dve.reciprocal(q[:, :, :], q[:, :, :]))
            then(dve.tensor_tensor(e[:, :, :], e[:, :, :], q[:, :, :], ALU.mult))
            then(dve.tensor_tensor(s2[:, :, :], e[:, :, :], e[:, :, :], ALU.mult))
            then(dve.tensor_scalar(q[:, :, :], s2[:, :, :], SERIES[0], None, ALU.mult))
            for c in SERIES[1:]:
                then(dve.scalar_tensor_tensor(out=q[:, :, :], in0=q[:, :, :], scalar=c, in1=s2[:, :, :],
                                              op0=ALU.add, op1=ALU.mult))
            then(dve.scalar_tensor_tensor(out=q[:, :, :], in0=q[:, :, :], scalar=1.0, in1=e[:, :, :],
                                          op0=ALU.add, op1=ALU.mult))
            then(dve.tensor_scalar(q[:, :, :], q[:, :, :], 2.0, None, ALU.mult))
            then(dve.scalar_tensor_tensor(out=dts["dt"][:, :, :], in0=raw[:, :, :], scalar=0.0, in1=q[:, :, :],
                                          op0=ALU.max, op1=ALU.add))
            then(dve.tensor_tensor(dts["da"][:, :, :], dts["dt"][:, :, :], over_chunks(g.neg_a[:, :]), ALU.mult))
            assert steps[0] == DA_DONE
            dve.wait_ge(cum_full, 1)
            then(dve.tensor_copy(dts["cs"][:, :, :], view(pc)))
            then(dve.tensor_copy(dts["etot"][:, :, :], view(pt)))
            then(dve.tensor_tensor(dts["edec"][:, :, :], dts["etot"][:, :, :], dts["cs"][:, :, :], ALU.subtract))

        @block.scalar
        def _(act):
            act.wait_ge(vec, 1)
            act.activation(e[:, :, :], raw[:, :, :], ACT.Abs).then_inc(act_done, 1)
            act.wait_ge(act_done, 1)
            act.activation(e[:, :, :], e[:, :, :], ACT.Exp, scale=-1.0).then_inc(act_done, 1)
            act.wait_ge(vec, DA_DONE + 3)
            act.activation(dts["ecs"][:, :, :], dts["cs"][:, :, :], ACT.Exp)
            act.activation(dts["etot"][:, :, :], dts["etot"][:, :, :], ACT.Exp)
            act.activation(dts["edec"][:, :, :], dts["edec"][:, :, :], ACT.Exp).then_inc(act_done, 1)


DA_DONE = 15


def phase_ssd(nc, sem, io, g, dts, x_tok, b_chan, c_chan, b_tok, y_tok):
    UNITS = 2 * NCH
    chunk = lambda u: 0 if u < 2 else (u // 2 if u % 2 == 0 else NCH - u // 2)
    with_state = lambda u: u >= 2
    makes_state = lambda u: u < UNITS - 2
    s_in, s_out = [sem("s_in0"), sem("s_in1")], [sem("s_out0"), sem("s_out1")]
    parts_ready, mats_ready, y_init = sem("ssd_parts_ready"), sem("ssd_mats_ready"), sem("ssd_y_init")
    cum_full, dist_done, decay_done = sem("ssd_cum_full"), sem("ssd_dist_done"), sem("ssd_decay_done")
    cb_full, cb_done, m_done = sem("ssd_cb_full"), sem("ssd_cb_done"), sem("ssd_m_done")
    xdt_done, xdec_done, sdec_done = sem("ssd_xdt_done"), sem("ssd_xdec_done"), sem("ssd_sdec_done")
    st_full, s_done = sem("ssd_st_full"), sem("ssd_s_done")
    off_full, off_done, diag_full, y_new = (sem("ssd_off_full"), sem("ssd_off_done"), sem("ssd_diag_full"),
                                            sem("ssd_y_new"))
    y_added, pool_go = sem("ssd_y_added"), sem("ssd_pool_go")
    with ExitStack() as ctx:
        sb = lambda n, shape: ctx.enter_context(nc.sbuf_tensor("ssd_" + n, shape, F32))
        pb = lambda n, shape: ctx.enter_context(nc.psum_tensor("ssd_" + n, shape, F32))
        part = {n: sb(n, [P, NCH, 2, HPG]) for n in DT_PARTS}
        ct, bt, bk = sb("ct", [P, T]), sb("bt", [P, T]), sb("bk", [P, NCH, M_STATE])
        m = sb("m", [P, 2, HPG, P])
        cb = sb("cb", [P, P])
        xdt, xdec, yn = sb("xdt", [P, 2, GI]), sb("xdec", [P, 2, GI]), sb("yn", [P, 2, GI])
        off, sdec = sb("off", [P, GI]), sb("sdec", [P, GI])
        s_ctx, s_lat = sb("s_ctx", [P, 2, GI]), sb("s_lat", [P, 2, GI])
        p_cum = pb("p_cum", [P, 2, HPG, P])
        p_cb, p_diag, p_off, p_st = (pb("p_cb", [P, 512]), pb("p_diag", [P, 512]), pb("p_off", [P, 512]),
                                     pb("p_st", [P, 512]))
        block = ctx.enter_context(nc.Block())
        heads = lambda a: a.rearrange("p (e f) -> p e f", f=HD)
        per_head = lambda n, u: part[n][:, chunk(u), u % 2, :].unsqueeze(2).to_broadcast([P, HPG, HD])
        ONE, TWO = 1, 2

        @block.sync
        def _(sp):
            for d in (0, 1):
                sp.dma_start(s_lat[:, d, :], io["ssm_in"][d, 0]).then_inc(s_in[d], 16)
            with sp.Fori(0, M_GROUPS - 1) as gi:
                for d in (0, 1):
                    sp.wait_ge(s_done, 8 * gi + d + 1 + ONE)
                    sp.dma_start(io["ssm_out"][d, bass.ds(gi, 1)].squeeze(0), s_ctx[:, d, :]).then_inc(s_out[d], 16)
                sp.wait_ge(off_full, 8 * gi + 8)
                for d in (0, 1):
                    sp.dma_start(s_lat[:, d, :], io["ssm_in"][d, bass.ds(gi + 1, 1)].squeeze(0)).then_inc(s_in[d], 16)
            last = M_GROUPS - 1
            for d in (0, 1):
                sp.wait_ge(s_done, 8 * last + d + 1 + ONE)
                sp.dma_start(io["ssm_out"][d, last], s_ctx[:, d, :]).then_inc(s_out[d], 16)
            for d in (0, 1):
                sp.wait_ge(s_out[d], 16 * M_GROUPS + 16)

        @block.gpsimd
        def _(pool):
            pool.sem_inc(y_added, TWO)
            with pool.Fori(0, M_GROUPS) as gi:
                pool.wait_ge(diag_full, UNITS * gi + TWO)
                pool.wait_ge(y_new, UNITS * gi + ONE)
                for n in DT_PARTS:
                    src = dts[n][:, :, :].rearrange("p c (d q e) -> p c d q e", d=2, e=HPG)
                    for d in (0, 1):
                        last = pool.tensor_copy(part[n][:, :, d, :], src[:, :, d, bass.ds(gi, 1), :].squeeze(2))
                last.then_inc(parts_ready, 1)
                for c in range(NCH):
                    last = pool.tensor_tensor(
                        heads(y_tok[:, c, bass.ds(gi * GI, GI)]), heads(x_tok[:, c, bass.ds(gi * GI, GI)]),
                        g.r("d_skip")[:, bass.ds(gi * HPG, HPG)].unsqueeze(2).to_broadcast([P, HPG, HD]), ALU.mult)
                last.then_inc(y_init, 1)
                pool.wait_ge(parts_ready, gi + 1)

                def add_y(u):
                    n = UNITS * gi + u
                    pool.wait_ge(y_init, gi + 1)
                    pool.wait_ge(y_new, n + 1 + ONE)
                    pool.wait_ge(y_added, n + TWO)
                    pool.sem_inc(pool_go, 1)
                    y = y_tok[:, chunk(u), bass.ds(gi * GI, GI)]
                    pool.tensor_tensor(y, y, yn[:, u % 2, :], ALU.add).then_inc(y_added, 1)

                for u in range(UNITS):
                    n, d, i = UNITS * gi + u, u % 2, 8 * gi + u
                    pool.wait_ge(diag_full, n + 1)
                    pool.sem_inc(pool_go, 1)
                    x = heads(x_tok[:, chunk(u), bass.ds(gi * GI, GI)])
                    pool.tensor_tensor(heads(xdt[:, d, :]), x, per_head("dt", u), ALU.mult).then_inc(xdt_done, 1)
                    if makes_state(u):
                        pool.wait_ge(xdt_done, n + 1)
                        pool.tensor_tensor(heads(xdec[:, d, :]), heads(xdt[:, d, :]), per_head("edec", u),
                                           ALU.mult).then_inc(xdec_done, 1)
                        if with_state(u):
                            if u < 4:
                                pool.wait_ge(s_in[d], 16 * gi + 16)
                            pool.wait_ge(s_done, i + ONE)
                            pool.tensor_tensor(heads(sdec[:, :]), heads(s_lat[:, d, :]), per_head("etot", u),
                                               ALU.mult).then_inc(sdec_done, 1)
                    if u:
                        add_y(u - 1)
                add_y(UNITS - 1)

        @block.scalar
        def _(act):
            act.sem_inc(dist_done, TWO)
            with act.Fori(0, M_GROUPS) as gi:
                act.wait_ge(diag_full, UNITS * gi + TWO)
                act.activation(ct[:, :], c_chan[:, bass.ds(gi, 1), :].squeeze(1), ACT.Copy)
                act.activation(bt[:, :], b_chan[:, bass.ds(gi, 1), :].squeeze(1), ACT.Copy)
                act.activation(bk[:, :, :], b_tok[:, :, bass.ds(gi * M_STATE, M_STATE)], ACT.Copy)\
                   .then_inc(mats_ready, 1)
                act.wait_ge(parts_ready, gi + 1)
                for u in range(UNITS):
                    n = UNITS * gi + u
                    act.wait_ge(cum_full, n + 1)
                    act.wait_ge(diag_full, n + 1)
                    for e in range(HPG):
                        last = act.activation(m[:, u % 2, e, :], p_cum[:, u % 2, e, :], ACT.Relu, scale=-1.0,
                                              bias=part["cs"][:, chunk(u), u % 2, e:e + 1])
                    last.then_inc(dist_done, 1)
                    act.wait_ge(dist_done, n + 1 + TWO)
                    act.activation(m[:, u % 2, :, :], m[:, u % 2, :, :], ACT.Exp, scale=-1.0)\
                       .then_inc(decay_done, 1)

        @block.tensor
        def _(pe):
            pe.sem_inc(diag_full, TWO)
            with pe.Fori(0, M_GROUPS) as gi:
                pe.wait_ge(parts_ready, gi + 1)
                pe.wait_ge(mats_ready, gi + 1)

                def cum(u):
                    pe.wait_ge(dist_done, UNITS * gi + u + 1)
                    for e in range(HPG):
                        da = part["da"][:, chunk(u), u % 2, e:e + 1].to_broadcast([P, P])
                        last = pe.matmul(p_cum[:, u % 2, e, :], da, g.tri[:, u % 2, :], start=True, stop=True)
                    last.then_inc(cum_full, 1)

                cum(0)
                for u in range(UNITS):
                    n, d, i = UNITS * gi + u, u % 2, 8 * gi + u
                    span = slice(P * chunk(u), P * chunk(u) + P)
                    if u + 1 < UNITS:
                        cum(u + 1)
                    pe.wait_ge(cb_done, n + ONE)
                    pe.matmul(p_cb[:, 0:P], bt[:, span], ct[:, span], start=True, stop=True).then_inc(cb_full, 1)
                    if with_state(u):
                        if u < 4:
                            pe.wait_ge(s_in[d], 16 * gi + 16)
                        else:
                            pe.wait_ge(s_done, i - 1 + ONE)
                        pe.wait_ge(off_done, 8 * gi + u - 2 + ONE)
                        pe.matmul(p_off[:, :], ct[:, span], s_lat[:, d, :], start=True, stop=True)\
                          .then_inc(off_full, 1)
                    if makes_state(u):
                        pe.wait_ge(xdec_done, i + 1)
                        pe.wait_ge(s_done, i + ONE)
                        pe.matmul(p_st[:, :], bk[:, chunk(u), :], xdec[:, d, :], start=True, stop=True)\
                          .then_inc(st_full, 1)
                    pe.wait_ge(xdt_done, n + 1)
                    pe.wait_ge(m_done, n + 1)
                    pe.wait_ge(y_new, n + ONE)
                    for e in range(HPG):
                        last = pe.matmul(p_diag[:, HD * e:HD * e + HD], m[:, d, e, :],
                                         xdt[:, d, HD * e:HD * e + HD], start=True, stop=True)
                    last.then_inc(diag_full, 1)

        @block.vector
        def _(dve):
            dve.sem_inc(cb_done, ONE)
            dve.sem_inc(off_done, ONE)
            dve.sem_inc(s_done, ONE)
            dve.sem_inc(y_new, ONE)
            for d in (0, 1):
                dve.sem_inc(s_out[d], 16)
            with dve.Fori(0, M_GROUPS) as gi:
                dve.wait_ge(parts_ready, gi + 1)
                for u in range(UNITS):
                    n, d, i = UNITS * gi + u, u % 2, 8 * gi + u
                    dve.wait_ge(y_new, n + ONE)
                    dve.wait_ge(cb_full, n + 1)
                    dve.tensor_tensor(cb[:, :], p_cb[:, 0:P], g.tri[:, d, :], ALU.mult).then_inc(cb_done, 1)
                    if with_state(u):
                        dve.wait_ge(off_full, 8 * gi + u - 1)
                        dve.tensor_tensor(heads(off[:, :]), heads(p_off[:, :]), per_head("ecs", u),
                                          ALU.mult).then_inc(off_done, 1)
                    if makes_state(u):
                        dve.wait_ge(st_full, i + 1)
                        if with_state(u):
                            dve.wait_ge(sdec_done, 6 * gi + u - 1)
                            dve.tensor_tensor(s_lat[:, d, :], sdec[:, :], p_st[:, :], ALU.add).then_inc(s_done, 1)
                        else:
                            dve.wait_ge(s_out[d], 16 * gi + 16)
                            dve.tensor_copy(s_ctx[:, d, :], p_st[:, :]).then_inc(s_done, 1)
                    dve.wait_ge(cb_done, n + 1 + ONE)
                    dve.wait_ge(decay_done, n + 1)
                    dve.tensor_tensor(m[:, d, :, :], m[:, d, :, :],
                                      cb[:, :].unsqueeze(1).to_broadcast([P, HPG, P]), ALU.mult).then_inc(m_done, 1)
                    dve.wait_ge(diag_full, n + 1 + TWO)
                    dve.wait_ge(y_added, n + 1)
                    if with_state(u):
                        dve.wait_ge(off_done, 8 * gi + u - 1 + ONE)
                        dve.tensor_tensor(yn[:, d, :], off[:, :], p_diag[:, :], ALU.add).then_inc(y_new, 1)
                    else:
                        dve.tensor_copy(yn[:, d, :], p_diag[:, :]).then_inc(y_new, 1)


def phase_m_gate(nc, sem, io, g, y_tok, y_chan):
    w_in = [sem("z_w_in0"), sem("z_w_in1")]
    z_full, z_done, gated = sem("z_full"), sem("z_done"), sem("z_gated")
    sum_done, mean_done, root_done, inv_done = sem("z_sum_done"), sem("z_mean_done"), sem("z_root_done"), sem("z_inv")
    normed, tr_full, tr_done = sem("z_normed"), sem("z_tr_full"), sem("z_tr_done")
    SUB = GI // P
    with ExitStack() as ctx:
        sb = lambda n, shape: ctx.enter_context(nc.sbuf_tensor("z_" + n, shape, F32))
        w = sb("w", [P, 2, KD * GI])
        z, sq = sb("z", [P, 2, GI]), sb("sq", [P, GI])
        ms = sb("ms", [P, 2, 1])
        pz = ctx.enter_context(nc.psum_tensor("z_pz", [P, 2, 512], F32))
        pt = ctx.enter_context(nc.psum_tensor("z_pt", [P, 2, 512], F32))
        block = ctx.enter_context(nc.Block())
        units = [(q, c) for q in range(M_GROUPS) for c in range(NCH)]

        @block.sync
        def _(sp):
            for q in range(M_GROUPS):
                if q >= 2:
                    sp.wait_ge(z_full, NCH * (q - 1))
                sp.dma_start(w[:, q % 2, :], io["w_z"][q]).then_inc(w_in[q % 2], 16)

        @block.tensor
        def _(pe):
            def turn(n):
                q, c = units[n]
                pe.wait_ge(normed, n + 1)
                if n >= 2:
                    pe.wait_ge(tr_done, n - 1)
                for j in range(SUB):
                    at = GI * q + P * j
                    last = pe.transpose(pt[:, n % 2, P * j:P * j + P], y_tok[:, c, at:at + P], g.ident)
                last.then_inc(tr_full, 1)

            for n, (q, c) in enumerate(units):
                pe.wait_ge(w_in[q % 2], 16 * (q // 2 + 1))
                if n >= 2:
                    pe.wait_ge(z_done, n - 1)
                for k in range(KD):
                    last = pe.matmul(pz[:, n % 2, :], g.h[:, k, P * c:P * c + P],
                                     w[:, q % 2, GI * k:GI * k + GI], start=(k == 0), stop=(k == KD - 1))
                last.then_inc(z_full, 1)
                if n >= 1:
                    turn(n - 1)
            turn(len(units) - 1)

        @block.scalar
        def _(act):
            for n in range(len(units)):
                act.wait_ge(z_full, n + 1)
                if n >= 2:
                    act.wait_ge(gated, n - 1)
                act.activation(z[:, n % 2, :], pz[:, n % 2, :], ACT.Silu).then_inc(z_done, 1)
                act.wait_ge(inv_done, n + 1)
                act.activation(ms[:, n % 2, :], ms[:, n % 2, :], ACT.Sqrt).then_inc(root_done, 1)

        @block.vector
        def _(dve):
            for n, (q, c) in enumerate(units):
                y = y_tok[:, c, GI * q:GI * q + GI]
                dve.wait_ge(z_done, n + 1)
                dve.tensor_tensor(y, y, z[:, n % 2, :], ALU.mult).then_inc(gated, 1)
                dve.wait_ge(gated, n + 1)
                dve.tensor_tensor_reduce(out=sq[:, :], in0=y, in1=y, scale=1.0, scalar=0.0, op0=ALU.mult,
                                         op1=ALU.add, accum_out=ms[:, n % 2, :]).then_inc(sum_done, 1)
                dve.wait_ge(sum_done, n + 1)
                dve.tensor_scalar(ms[:, n % 2, :], ms[:, n % 2, :], 1.0 / GI, 1e-5, ALU.mult, ALU.add)\
                   .then_inc(mean_done, 1)
                dve.wait_ge(mean_done, n + 1)
                dve.reciprocal(ms[:, n % 2, :], ms[:, n % 2, :]).then_inc(inv_done, 1)
                dve.wait_ge(root_done, n + 1)
                dve.tensor_scalar(y, y, ms[:, n % 2, :], None, ALU.mult).then_inc(normed, 1)
                dve.wait_ge(tr_full, n + 1)
                dve.tensor_tensor(y_chan[:, SUB * q:SUB * q + SUB, P * c:P * c + P],
                                  pt[:, n % 2, :].rearrange("p (j t) -> p j t", t=P),
                                  g.v("m_norm")[:, SUB * q:SUB * q + SUB].unsqueeze(2).to_broadcast([P, SUB, P]),
                                  ALU.mult).then_inc(tr_done, 1)


def phase_mix_out(nc, sem, g, tag, w_dram, y, k_tiles, add):
    w_in = [sem(tag + "_w_in0"), sem(tag + "_w_in1")]
    out_full, gate_full, gate_done, done = (sem(tag + "_out_full"), sem(tag + "_gate_full"),
                                            sem(tag + "_gate_done"), sem(tag + "_done"))
    scaled = sem(tag + "_scaled")
    KW = k_tiles + KD
    with ExitStack() as ctx:
        w = ctx.enter_context(nc.sbuf_tensor(tag + "_w", [P, 2, KW * P], F32))
        gate = ctx.enter_context(nc.sbuf_tensor(tag + "_gate", [P, 2, T], F32))
        po = ctx.enter_context(nc.psum_tensor(tag + "_po", [P, 2, 1024], F32))
        pg = ctx.enter_context(nc.psum_tensor(tag + "_pg", [P, 2, 1024], F32))
        block = ctx.enter_context(nc.Block())

        @block.sync
        def _(sp):
            stream(sp, KD, lambda it, s: sp.dma_start(w[:, s, :], w_dram[2 * it + s]).then_inc(w_in[s], 16),
                   used=out_full)

        @block.tensor
        def _(pe):
            with pe.Fori(0, KD // 2) as it:
                for s in (0, 1):
                    n = 2 * it + s
                    wt = tiles_of(w[:, s, :])
                    pe.wait_ge(w_in[s], 16 * it + 16)
                    pe.wait_ge(gate_done, n + 1)
                    project(pe, pg[:, s, :], wt[:, k_tiles:, :], g.h, KD).then_inc(gate_full, 1)
                    pe.wait_ge(done, n + 1)
                    project(pe, po[:, s, :], wt[:, :k_tiles, :], y, k_tiles).then_inc(out_full, 1)

        @block.scalar
        def _(act):
            act.sem_inc(gate_done, 2)
            with act.Fori(0, KD // 2) as it:
                for s in (0, 1):
                    n = 2 * it + s
                    act.wait_ge(gate_full, n + 1)
                    act.wait_ge(done, n + 1)
                    act.activation(gate[:, s, :], pg[:, s, 0:T], ACT.Sigmoid).then_inc(gate_done, 1)

        @block.vector
        def _(dve):
            dve.sem_inc(done, 2)
            with dve.Fori(0, KD // 2) as it:
                for s in (0, 1):
                    n = 2 * it + s
                    dve.wait_ge(gate_done, n + 3)
                    dve.wait_ge(out_full, n + 1)
                    mix = g.mix[:, bass.ds(n, 1), :].squeeze(1)
                    if not add:
                        dve.tensor_tensor(mix, gate[:, s, :], po[:, s, 0:T], ALU.mult).then_inc(done, 1)
                    else:
                        dve.tensor_tensor(gate[:, s, :], gate[:, s, :], po[:, s, 0:T], ALU.mult).then_inc(scaled, 1)
                        dve.wait_ge(scaled, n + 1)
                        dve.tensor_tensor(mix, mix, gate[:, s, :], ALU.add).then_inc(done, 1)


def phase_residual(nc, sem, g, tag, w_dram, rhs, k_tiles, gate_at):
    w_in = [sem(tag + "_w_in0"), sem(tag + "_w_in1")]
    full, done = sem(tag + "_full"), sem(tag + "_done")
    with ExitStack() as ctx:
        w = ctx.enter_context(nc.sbuf_tensor(tag + "_w", [P, 2, k_tiles * P], F32))
        ps = ctx.enter_context(nc.psum_tensor(tag + "_ps", [P, 2, 1024], F32))
        block = ctx.enter_context(nc.Block())

        @block.sync
        def _(sp):
            stream(sp, KD, lambda it, s: sp.dma_start(w[:, s, :], w_dram[2 * it + s]).then_inc(w_in[s], 16),
                   used=full)

        @block.tensor
        def _(pe):
            with pe.Fori(0, KD // 2) as it:
                for s in (0, 1):
                    pe.wait_ge(w_in[s], 16 * it + 16)
                    pe.wait_ge(done, 2 * it + s + 1)
                    project(pe, ps[:, s, :], tiles_of(w[:, s, :]), rhs, k_tiles).then_inc(full, 1)

        @block.vector
        def _(dve):
            dve.sem_inc(done, 2)
            with dve.Fori(0, KD // 2) as it:
                for s in (0, 1):
                    dve.wait_ge(full, 2 * it + s + 1)
                    for c, lo, hi in SEG:
                        x = g.x[:, bass.ds(2 * it + s, 1), lo:hi].squeeze(1)
                        last = dve.scalar_tensor_tensor(
                            out=x, in0=ps[:, s, lo:hi], in1=x, op0=ALU.mult, op1=ALU.add,
                            scalar=g.mod[:, bass.ds(2 * it + s + gate_at, 1), c])
                    last.then_inc(done, 1)


def phase_up(nc, sem, io, g, hidden):
    w_in = [sem("up_w_in0"), sem("up_w_in1")]
    g_full, u_full, silu_done, done = sem("up_g_full"), sem("up_u_full"), sem("up_silu_done"), sem("up_done")
    with ExitStack() as ctx:
        w = ctx.enter_context(nc.sbuf_tensor("up_w", [P, 2, 2 * KD * P], F32))
        act_g = ctx.enter_context(nc.sbuf_tensor("up_silu", [P, 2, T], F32))
        pg = ctx.enter_context(nc.psum_tensor("up_pg", [P, 2, 1024], F32))
        pu = ctx.enter_context(nc.psum_tensor("up_pu", [P, 2, 1024], F32))
        block = ctx.enter_context(nc.Block())

        @block.sync
        def _(sp):
            stream(sp, KF, lambda it, s: sp.dma_start(w[:, s, :], io["w_gu"][2 * it + s]).then_inc(w_in[s], 16),
                   used=u_full)

        @block.tensor
        def _(pe):
            with pe.Fori(0, KF // 2) as it:
                for s in (0, 1):
                    n = 2 * it + s
                    wt = tiles_of(w[:, s, :])
                    pe.wait_ge(w_in[s], 16 * it + 16)
                    pe.wait_ge(silu_done, n + 1)
                    project(pe, pg[:, s, :], wt[:, :KD, :], g.h, KD).then_inc(g_full, 1)
                    pe.wait_ge(done, n + 1)
                    project(pe, pu[:, s, :], wt[:, KD:, :], g.h, KD).then_inc(u_full, 1)

        @block.scalar
        def _(act):
            act.sem_inc(silu_done, 2)
            with act.Fori(0, KF // 2) as it:
                for s in (0, 1):
                    n = 2 * it + s
                    act.wait_ge(g_full, n + 1)
                    act.wait_ge(done, n + 1)
                    act.activation(act_g[:, s, :], pg[:, s, 0:T], ACT.Silu).then_inc(silu_done, 1)

        @block.vector
        def _(dve):
            dve.sem_inc(done, 2)
            with dve.Fori(0, KF // 2) as it:
                for s in (0, 1):
                    n = 2 * it + s
                    dve.wait_ge(silu_done, n + 3)
                    dve.wait_ge(u_full, n + 1)
                    dve.tensor_tensor(hidden[:, bass.ds(n, 1), :].squeeze(1), act_g[:, s, :], pu[:, s, 0:T],
                                      ALU.mult).then_inc(done, 1)


def phase_store(nc, sem, io, g):
    stored = sem("stored")
    with nc.Block() as block:
        @block.sync
        def _(sp):
            sp.dma_start(io["y"].rearrange("k p t -> p k t"), g.h[:, :, :]).then_inc(stored, 16)
            sp.wait_ge(stored, 16)


def phase_load_x(nc, sem, io, g):
    x_in = sem("x_again")
    with nc.Block() as block:
        @block.sync
        def _(sp):
            sp.dma_start(g.x[:, :, :], io["x_t"].rearrange("k p t -> p k t")).then_inc(x_in, 16)
            sp.wait_ge(x_in, 16)


R_TILES, W_TILE, K_TILES, V_TILES, A_TILE, G_TILE = range(0, 8), 8, range(9, 17), range(17, 25), 25, 26


def quarters_of(tiles):
    return sorted({ch // QUARTER for m in tiles for ch in (P * m, P * m + P - 1)})


def shifted_views(q, dst, src):
    before = q % 2 == 0
    far, near = slice(1, CTX), slice(0, CTX - 1)
    context = (dst[:, far], src[:, near]) if before else (dst[:, near], src[:, far])
    if q < 2:
        grid = lambda a: a[:, CTX:T].rearrange("p (r w) -> p r w", w=GRID_W)
        far, near = slice(1, GRID_W), slice(0, GRID_W - 1)
        latent = (grid(dst)[:, :, far], grid(src)[:, :, near]) if before else \
                 (grid(dst)[:, :, near], grid(src)[:, :, far])
    else:
        far, near = slice(CTX + GRID_W, T), slice(CTX, T - GRID_W)
        latent = (dst[:, far], src[:, near]) if before else (dst[:, near], src[:, far])
    return context, latent


def phase_low(nc, sem, io, g, low):
    w_in = [sem(f"low_w_in{m}") for m in range(3)]
    full, own, mixed, ready = sem("low_full"), sem("low_own"), sem("low_mixed"), sem("low_ready")
    tiles = (W_TILE, A_TILE, G_TILE)
    with ExitStack() as ctx:
        w = ctx.enter_context(nc.sbuf_tensor("low_w", [P, 3, KD * P], F32))
        ps = ctx.enter_context(nc.psum_tensor("low_ps", [P, 3, 1024], F32))
        block = ctx.enter_context(nc.Block())

        @block.sync
        def _(sp):
            for m in range(3):
                sp.dma_start(w[:, m, :], io["w_low"][m]).then_inc(w_in[m], 16)

        @block.tensor
        def _(pe):
            for m in range(3):
                pe.wait_ge(w_in[m], 16)
                project(pe, ps[:, m, :], tiles_of(w[:, m, :]), g.h, KD).then_inc(full, 1)

        @block.scalar
        def _(act):
            for m, tile in enumerate(tiles):
                act.wait_ge(full, m + 1)
                act.activation(low[:, m, :], ps[:, m, 0:T], ACT.Copy,
                               scale=g.mu_own[:, tile:tile + 1]).then_inc(own, 1)
            act.wait_ge(mixed, 1)
            act.activation(low[:, 0, :], low[:, 0, :], ACT.Tanh)
            act.wait_ge(mixed, 3)
            act.activation(low[:, 2, :], low[:, 2, :], ACT.Sigmoid)

        @block.vector
        def _(dve):
            for m, tile in enumerate(tiles):
                dve.wait_ge(own, m + 1)
                (q,) = quarters_of([tile])
                for dst, src in shifted_views(q, low[:, m, :], ps[:, m, 0:T]):
                    last = dve.scalar_tensor_tensor(out=dst, in0=src, scalar=g.mu_q[:, tile, q:q + 1],
                                                    in1=dst, op0=ALU.mult, op1=ALU.add)
                last.then_inc(mixed, 1)


A_HAT, R_HAT, B_HAT, K_HAT = range(4)


def phase_rwkv_in(nc, sem, io, g, low, bonus, carry):
    w_in = [sem("rw_w_in0"), sem("rw_w_in1")]
    a_full, a_done = [sem("rw_a_full0"), sem("rw_a_full1")], [sem("rw_a_done0"), sem("rw_a_done1")]
    b_full, b_done = [sem("rw_b_full0"), sem("rw_b_full1")], [sem("rw_b_done0"), sem("rw_b_done1")]
    own, half_mixed = sem("rw_own"), sem("rw_half_mixed")
    sq_done, inv_chain, root_done, kk_done = (sem("rw_sq_done"), sem("rw_inv_chain"), sem("rw_root_done"),
                                              sem("rw_kk_done"))
    cum_done, before_done, g_done, ginv_done, gbef_done = (sem("rw_cum_done"), sem("rw_before_done"),
                                                           sem("rw_g_done"), sem("rw_ginv_done"),
                                                           sem("rw_gbef_done"))
    rate_done, kd_done, kd_sum, kk_a, rk_done = (sem("rw_rate_done"), sem("rw_kd_done"), sem("rw_kd_sum"),
                                                 sem("rw_kk_a"), sem("rw_rk_done"))
    ahat, rhat, bhat, khat = sem("rw_ahat"), sem("rw_rhat"), sem("rw_bhat"), sem("rw_khat")
    turned = sem("rw_turned")
    chan_out, tok_out = sem("rw_chan_out"), sem("rw_tok_out")
    vec_tile, pool_tile, act_tile = sem("rw_vec_tile"), sem("rw_pool_tile"), sem("rw_act_tile")
    roles = (R_TILES, K_TILES, V_TILES)
    TURNS = ((0, B_HAT), (0, K_HAT), (1, B_HAT), (1, K_HAT), None)
    A_USES, B_USES = 3, 6 + len(TURNS)
    TWO = 2

    def a_use(it, s, x):
        return (A_USES * s + x) % 2, A_USES * it + (A_USES * s + x) // 2

    def b_use(it, s, x):
        return (B_USES * s + x) % 2, B_USES * it + (B_USES * s + x) // 2

    with ExitStack() as ctx:
        sb = lambda n, shape: ctx.enter_context(nc.sbuf_tensor("rw_" + n, shape, F32))
        KW = 3 * KD + 2
        w = sb("w", [P, 2, KW * P])
        rkv = sb("rkv", [P, 2, 3, T])
        dec, rate = sb("dec", [P, 2, T]), sb("rate", [P, 2, T])
        cum, gg = sb("cum", [P, 2, T]), sb("gg", [P, 2, T])
        kd = sb("kd", [P, 2, T])
        kk, inv, kds = sb("kk", [P, T]), sb("inv", [P, T]), sb("kds", [P, T])
        hat = sb("hat", [P, 2, 4, T])
        tb = sb("tb", [P, len(TURNS), T])
        pa = ctx.enter_context(nc.psum_tensor("rw_pa", [P, 2, 1024], F32))
        pb = ctx.enter_context(nc.psum_tensor("rw_pb", [P, 2, 1024], F32))
        block = ctx.enter_context(nc.Block())
        one = lambda base, n: bass.ds(n + base, 1)

        @block.sync
        def _(sp):
            def load(it, s):
                sp.dma_start(w[:, s, :], io["w_rkv"][2 * it + s]).then_inc(w_in[s], 16)

            def store(it, s):
                n = 2 * it + s
                chan = io["chan"].rearrange("d c p (q j t) -> d q j p c t", q=4, j=PAIRS)
                for d in (0, 1):
                    for q, made in ((A_HAT, ahat), (R_HAT, rhat), (B_HAT, bhat), (K_HAT, khat)):
                        sp.wait_ge(made, 2 * n + d + 1)
                        sp.dma_start(chan[d, q, bass.ds(n, 1)].squeeze(0),
                                     hat[:, d, q, :].rearrange("p (c t) -> p c t", t=WC)).then_inc(chan_out, 16)
                tok = io["tok"].rearrange("d (c p) (q j m) -> d q j p c m", p=P, q=2, m=P)
                val = io["val"].rearrange("(c p) (j m) -> j p c m", p=P, m=P)
                for x, turn in enumerate(TURNS):
                    sp.wait_ge(turned, len(TURNS) * n + x + 1)
                    dst = val[bass.ds(n, 1)] if turn is None else tok[turn[0], turn[1] - B_HAT, bass.ds(n, 1)]
                    sp.dma_start(dst.squeeze(0), tb[:, x, :].rearrange("p (c m) -> p c m", m=P)).then_inc(tok_out, 16)

            load(0, 0)
            load(0, 1)
            with sp.Fori(0, PAIRS // 2 - 1) as it:
                for s in (0, 1):
                    store(it, s)
                    load(it + 1, s)
            for s in (0, 1):
                store(PAIRS // 2 - 1, s)
            sp.wait_ge(chan_out, 16 * 8 * (PAIRS + 1))
            sp.wait_ge(tok_out, 16 * len(TURNS) * (PAIRS + 1))

        @block.tensor
        def _(pe):
            def proj(it, s, x):
                slot, before = a_use(it, s, x)
                if x == 0:
                    pe.wait_ge(w_in[s], 16 * it + 16)
                pe.wait_ge(a_done[slot], before + 1)
                wt = tiles_of(w[:, s, :])
                project(pe, pa[:, slot, :], wt[:, KD * x:KD * x + KD, :], g.h, KD).then_inc(a_full[slot], 1)

            def small(it, s, x, lhs, rhs, ready=None):
                slot, before = b_use(it, s, x)
                if ready is not None:
                    pe.wait_ge(*ready)
                pe.wait_ge(b_done[slot], before + 1)
                for lo, hi in BANKS:
                    last = pe.matmul(pb[:, slot, lo:hi], lhs, rhs[:, lo:hi], start=True, stop=True)
                last.then_inc(b_full[slot], 1)

            def finish(it, s, ahead):
                n = 2 * it + s
                wt = tiles_of(w[:, s, :])
                proj(it, s, 2)
                for x, tile in ((0, 0), (2, 1)):
                    for d in (0, 1):
                        rows = slice(64 * d, 64 * d + 64)
                        small(it, s, x + d, wt[rows, 3 * KD + tile, :], low[rows, tile, :])
                if ahead is not None:
                    proj(*ahead, 0)
                    proj(*ahead, 1)
                small(it, s, 4, g.head_ones, inv, (sq_done, n + 1))
                small(it, s, 5, g.head_ones, kds, (rk_done, n + 1))
                for x, turn in enumerate(TURNS):
                    slot, before = b_use(it, s, 6 + x)
                    if turn is None:
                        src = rkv[:, s, 2, :]
                    else:
                        src = hat[:, turn[0], turn[1], :]
                        pe.wait_ge(bhat if turn[1] == B_HAT else khat, 2 * n + turn[0] + 1)
                    pe.wait_ge(b_done[slot], before + 1)
                    for c in range(NCH):
                        last = pe.transpose(pb[:, slot, P * c:P * c + P], src[:, P * c:P * c + P], g.ident)
                    last.then_inc(b_full[slot], 1)

            proj(0, 0, 0)
            proj(0, 0, 1)
            with pe.Fori(0, PAIRS // 2 - 1) as it:
                finish(it, 0, (it, 1))
                finish(it, 1, (it + 1, 0))
            finish(PAIRS // 2 - 1, 0, (PAIRS // 2 - 1, 1))
            finish(PAIRS // 2 - 1, 1, None)

        def mixed(eng, it, s, x):
            slot, before = a_use(it, s, x)
            eng.wait_ge(a_done[slot], before + 2)

        @block.scalar
        def _(act):
            act.sem_inc(act_tile, TWO)
            with act.Fori(0, PAIRS // 2) as it:
                for s in (0, 1):
                    n = 2 * it + s
                    act.wait_ge(vec_tile, n + 1)
                    act.wait_ge(pool_tile, n + 1)
                    for x, role in enumerate(roles):
                        slot, before = a_use(it, s, x)
                        act.wait_ge(a_full[slot], before + 1)
                        act.activation(rkv[:, s, x, :], pa[:, slot, 0:T], ACT.Copy,
                                       scale=g.mu_own[:, one(role[0], n)]).then_inc(own, 1)
                    act.wait_ge(vec_tile, n + 2)
                    act.wait_ge(pool_tile, n + 2)
                    act.wait_ge(chan_out, 16 * 8 * n + 16 * 8)
                    for x, bias, dst in ((0, "w0", dec), (2, "a0", rate)):
                        for d in (0, 1):
                            slot, before = b_use(it, s, x + d)
                            act.wait_ge(b_full[slot], before + 1)
                            act.activation(dst[:, d, :], pb[:, slot, 0:T], ACT.Sigmoid,
                                           bias=g.v(bias)[:, one(KD * d, n)]).then_inc(b_done[slot], 1)
                    mixed(act, it, s, 1)
                    act.activation(inv[:, :], rkv[:, s, 1, :], ACT.Square,
                                   scale=g.v("k_k")[:, one(0, n)]).then_inc(sq_done, 1)
                    for d in (0, 1):
                        act.wait_ge(before_done, 2 * n + d + 1)
                        act.activation(gg[:, d, :], cum[:, d, :], ACT.Exp, scale=-LOG_DECAY).then_inc(g_done, 1)
                        act.activation(dec[:, d, :], dec[:, d, :], ACT.Exp, scale=-LOG_DECAY).then_inc(gbef_done, 1)
                        act.activation(cum[:, d, :], cum[:, d, :], ACT.Exp, scale=LOG_DECAY).then_inc(ginv_done, 1)
                    act.wait_ge(inv_chain, 2 * n + 2)
                    act.activation(inv[:, :], inv[:, :], ACT.Sqrt).then_inc(root_done, 1)
                    for d in (0, 1):
                        end = WC - 1 if d == 0 else 0
                        act.wait_ge(g_done, 2 * n + d + 1)
                        act.activation(carry[:, d, :, one(0, n)].squeeze(2), gg[:, d, end:T:WC], ACT.Copy)
                    act.wait_ge(tok_out, 16 * len(TURNS) * n + 16 * len(TURNS))
                    for x in range(len(TURNS)):
                        slot, before = b_use(it, s, 6 + x)
                        act.wait_ge(b_full[slot], before + 1)
                        act.activation(tb[:, x, :], pb[:, slot, 0:T], ACT.Copy).then_inc(turned, 1)
                        act.wait_ge(turned, len(TURNS) * n + x + 1)
                        act.sem_inc(b_done[slot], 1)

        @block.gpsimd
        def _(pool):
            pool.sem_inc(pool_tile, TWO)
            with pool.Fori(0, PAIRS // 2) as it:
                for s in (0, 1):
                    n = 2 * it + s
                    r, k = rkv[:, s, 0, :], rkv[:, s, 1, :]
                    for d in (0, 1):
                        pool.wait_ge(cum_done, 2 * n + d + 1)
                        pool.tensor_tensor(dec[:, d, :], cum[:, d, :], dec[:, d, :], ALU.subtract)\
                            .then_inc(before_done, 1)
                    for d in (0, 1):
                        pool.wait_ge(rate_done, 2 * n + d + 1)
                        if d == 0:
                            mixed(pool, it, s, 1)
                        pool.tensor_tensor(kd[:, d, :], kd[:, d, :], k, ALU.mult).then_inc(kd_done, 1)
                    pool.wait_ge(kd_done, 2 * n + 2)
                    pool.wait_ge(vec_tile, n + 2)
                    pool.tensor_tensor(kds[:, :], kd[:, 0, :], kd[:, 1, :], ALU.add).then_inc(kd_sum, 1)
                    for d in (0, 1):
                        pool.wait_ge(kk_done, n + 1)
                        pool.tensor_tensor(rate[:, d, :], rate[:, d, :], kk[:, :], ALU.mult).then_inc(kk_a, 1)
                    mixed(pool, it, s, 0)
                    for d in (0, 1):
                        pool.wait_ge(g_done, 2 * n + d + 1)
                        pool.tensor_tensor(hat[:, d, R_HAT, :], gg[:, d, :], r, ALU.mult).then_inc(rhat, 1)
                    pool.wait_ge(rhat, 2 * n + 2)
                    pool.sem_inc(pool_tile, 1)

        @block.vector
        def _(dve):
            dve.sem_inc(vec_tile, TWO)
            dve.sem_inc(a_done[0], 1)
            dve.sem_inc(a_done[1], 1)
            dve.sem_inc(b_done[0], 1)
            dve.sem_inc(b_done[1], 1)
            dve.sem_inc(chan_out, 16 * 8)
            dve.sem_inc(tok_out, 16 * len(TURNS))
            with dve.Fori(0, PAIRS // 2) as it:
                for s in (0, 1):
                    n = 2 * it + s
                    r, k, v = (rkv[:, s, x, :] for x in range(3))
                    for x, role in enumerate(roles):
                        slot, before = a_use(it, s, x)
                        dve.wait_ge(own, 3 * n + x + 1)
                        qa, qb = quarters_of(role)
                        for q in (qa, qb):
                            for dst, src in shifted_views(q, rkv[:, s, x, :], pa[:, slot, 0:T]):
                                last = dve.scalar_tensor_tensor(
                                    out=dst, in0=src, scalar=g.mu_q[:, one(role[0], n), q], in1=dst,
                                    op0=ALU.mult, op1=ALU.add)
                            if q == qa:
                                last.then_inc(half_mixed, 1)
                                dve.wait_ge(half_mixed, 3 * n + x + 1)
                        last.then_inc(a_done[slot], 1)
                    for d in (0, 1):
                        slot, before = b_use(it, s, d)
                        dve.wait_ge(b_done[slot], before + 2)
                        flow = (lambda a: a) if d == 0 else (lambda a: a[:, ::-1])
                        dve.tensor_tensor_scan(flow(cum[:, d, :]), flow(g.reset[:, d, :]), flow(dec[:, d, :]),
                                               0.0, ALU.mult, ALU.add).then_inc(cum_done, 1)
                    for d in (0, 1):
                        slot, before = b_use(it, s, 2 + d)
                        dve.wait_ge(b_done[slot], before + 2)
                        dve.tensor_scalar(kd[:, d, :], rate[:, d, :], g.v("k_a")[:, one(0, n)],
                                          g.k_a_c[:, one(0, n)], ALU.mult, ALU.add).then_inc(rate_done, 1)
                    slot, before = b_use(it, s, 4)
                    dve.wait_ge(b_full[slot], before + 1)
                    dve.tensor_scalar(inv[:, :], pb[:, slot, 0:T], 1e-12, None, ALU.add).then_inc(inv_chain, 1)
                    dve.wait_ge(inv_chain, 2 * n + 1)
                    dve.sem_inc(b_done[slot], 1)
                    dve.reciprocal(inv[:, :], inv[:, :]).then_inc(inv_chain, 1)
                    mixed(dve, it, s, 0)
                    dve.wait_ge(kd_sum, n + 1)
                    dve.scalar_tensor_tensor(out=kds[:, :], in0=r, scalar=g.v("r_k")[:, one(0, n)], in1=kds[:, :],
                                             op0=ALU.mult, op1=ALU.mult).then_inc(rk_done, 1)
                    dve.wait_ge(root_done, n + 1)
                    dve.scalar_tensor_tensor(out=kk[:, :], in0=k, scalar=g.v("k_k")[:, one(0, n)], in1=inv[:, :],
                                             op0=ALU.mult, op1=ALU.mult).then_inc(kk_done, 1)
                    for d in (0, 1):
                        dve.wait_ge(ginv_done, 2 * n + d + 1)
                        dve.tensor_tensor(hat[:, d, K_HAT, :], kd[:, d, :], cum[:, d, :], ALU.mult).then_inc(khat, 1)
                    dve.wait_ge(kk_done, n + 1)
                    for d in (0, 1):
                        dve.wait_ge(gbef_done, 2 * n + d + 1)
                        dve.scalar_tensor_tensor(out=hat[:, d, A_HAT, :], in0=kk[:, :], scalar=-1.0,
                                                 in1=dec[:, d, :], op0=ALU.mult, op1=ALU.mult).then_inc(ahat, 1)
                    for d in (0, 1):
                        dve.wait_ge(kk_a, 2 * n + d + 1)
                        dve.tensor_tensor(hat[:, d, B_HAT, :], rate[:, d, :], cum[:, d, :], ALU.mult).then_inc(bhat, 1)
                    slot, before = b_use(it, s, 5)
                    dve.wait_ge(b_full[slot], before + 1)
                    mixed(dve, it, s, 2)
                    dve.scalar_tensor_tensor(out=bonus[:, one(0, n), :].squeeze(1), in0=pb[:, slot, 0:T],
                                             scalar=0.5, in1=v, op0=ALU.mult, op1=ALU.mult)\
                       .then_inc(b_done[slot], 1)
                    dve.wait_ge(b_done[slot], before + 2)
                    dve.sem_inc(vec_tile, 1)


PE_STEPS = ["MB", "MK", "MM"] + [f"{x}{n}" for n in range(1, LEVELS) for x in "ZT"] + ["X", "U", "Y", "S"]
DVE_STEPS = ["MB", "MK", "T0"] + [f"{x}{n}" for n in range(1, LEVELS) for x in "ZT"] + ["S"]
ACT_STEPS = ["X", "U", "Y"]


def phase_wkv(nc, sem, io, g, carry, first, n_chunks, state_in, state_out, tag):
    count = lambda steps, i, name: len(steps) * i + steps.index(name) + 1
    loaded = [[sem(f"{tag}_in{d}{s}") for s in (0, 1)] for d in (0, 1)]
    y_out = [[sem(f"{tag}_y_out{d}{s}") for s in (0, 1)] for d in (0, 1)]
    pe_done, dve_done, act_done = ([sem(f"{tag}_{e}_done{d}") for d in (0, 1)] for e in ("pe", "dve", "act"))
    chain, summed = ([sem(f"{tag}_{e}{d}") for d in (0, 1)] for e in ("t0_parts", "summed"))
    pe_ready, dve_ready, sp_ready = sem(tag + "_pe_go"), sem(tag + "_dve_go"), sem(tag + "_sp_go")
    state_ready, state_stored = sem(tag + "_state_ready"), sem(tag + "_state_stored")
    with ExitStack() as ctx:
        sb = lambda n, shape: ctx.enter_context(nc.sbuf_tensor(f"{tag}_{n}", shape, F32))
        cm = sb("cm", [P, 2, 2, 4, PAIRS, WC])
        tk = sb("tk", [P, 2, 2, 2, PAIRS, HD])
        vv = sb("vv", [P, 2, 2, PAIRS, HD])
        mb, mk = sb("mb", [P, 2, PAIRS, 2, WC]), sb("mk", [P, 2, PAIRS, 2, WC])
        tt = sb("tt", [P, 2, 2, PAIRS, WC])
        z = sb("z", [P, 2, PAIRS, WC])
        x_, u_, st = sb("x", [P, 2, PAIRS, HD]), sb("u", [P, 2, PAIRS, HD]), sb("st", [P, 2, PAIRS, HD])
        y_ = sb("y", [P, 2, 2, PAIRS, HD])
        p0 = ctx.enter_context(nc.psum_tensor(tag + "_p0", [P, 2, 2, 512], F32))
        p1 = ctx.enter_context(nc.psum_tensor(tag + "_p1", [P, 2, 2, 512], F32))
        block = ctx.enter_context(nc.Block())
        narrow = lambda p: p.rearrange("p (j w) -> p j w", w=WC)
        wide = lambda p: p.rearrange("p b (j q w) -> p (b j) q w", q=2, w=WC)
        over_heads = lambda m: m.unsqueeze(1).to_broadcast([P, PAIRS, WC])
        chunk = lambda d, i: i + first if d == 0 else first + n_chunks - 1 - i
        ITERS = n_chunks // 2

        @block.sync
        def _(sp):
            if state_in is not None:
                sp.dma_start(st[:, :, :, :], state_in.rearrange("d p (j w) -> p d j w", w=HD)).then_inc(state_ready, 16)

            def load(it, s):
                for d in (0, 1):
                    c = chunk(d, 2 * it + s)
                    sp.dma_start(cm[:, s, d, :, :, :], io["chan"][d, bass.ds(c, 1)].squeeze(0)
                                 .rearrange("p (q j t) -> p q j t", q=4, t=WC)).then_inc(loaded[d][s], 16)
                    for h in (0, 1):
                        rows = slice(64 * h, 64 * h + 64)
                        tok = io["tok"][d, bass.ds(c * WC, WC), :].rearrange("t (n h m) -> h t n m", h=2, m=HD)
                        val = io["val"][bass.ds(c * WC, WC), :].rearrange("t (n h m) -> h t n m", h=2, m=HD)
                        sp.dma_start(tk[rows, s, d, :, :, :].rearrange("p q j m -> p (q j) m"), tok[h])\
                          .then_inc(loaded[d][s], 16)
                        sp.dma_start(vv[rows, s, d, :, :], val[h]).then_inc(loaded[d][s], 16)

            def store(it, s):
                for d in (0, 1):
                    i = 2 * it + s
                    sp.wait_ge(act_done[d], count(ACT_STEPS, i, "Y") + 1)
                    sp.sem_inc(sp_ready, 1)
                    dst = io["wkv_y"][d, bass.ds(chunk(d, i), 1)].squeeze(0).rearrange("p (j w) -> p j w", w=HD)
                    sp.dma_start(dst, y_[:, s, d, :, :]).then_inc(y_out[d][s], 16)

            load(0, 0)
            load(0, 1)
            if ITERS > 1:
                with sp.Fori(0, ITERS - 1) as it:
                    for s in (0, 1):
                        store(it, s)
                        for d in (0, 1):
                            sp.wait_ge(pe_done[d], len(PE_STEPS) * (2 * it + s + 1))
                        sp.sem_inc(sp_ready, 1)
                        load(it + 1, s)
            for s in (0, 1):
                store(ITERS - 1, s)
            for d in (0, 1):
                for s in (0, 1):
                    sp.wait_ge(y_out[d][s], 16 * ITERS + 16)
            if state_out is not None:
                for d in (0, 1):
                    sp.wait_ge(dve_done[d], len(DVE_STEPS) * n_chunks + 1)
                sp.dma_start(state_out.rearrange("d p (j w) -> p d j w", w=HD), st[:, :, :, :]).then_inc(state_stored, 16)
                sp.wait_ge(state_stored, 16)

        @block.gpsimd
        def _(pool):
            if state_in is None:
                pool.memset(st[:, :, :, :], 0.0).then_inc(state_ready, 16)
            for d in (0, 1):
                for s in (0, 1):
                    pool.sem_inc(y_out[d][s], 16)

        @block.tensor
        def _(pe):
            pe.wait_ge(state_ready, 16)
            halves = (slice(0, 64), slice(64, 128))

            def stage(d, i, name, products, waits):
                for s, v in waits:
                    pe.wait_ge(s, v)
                pe.sem_inc(pe_ready, 1)
                for j in range(PAIRS):
                    for rows in halves:
                        group = products(j, rows)
                        for n, (out, lhs, rhs, starts, stops) in enumerate(group):
                            last = pe.matmul(out[rows], lhs[rows], rhs[rows], start=starts, stop=stops)
                last.then_inc(pe_done[d], 1)

            def alone(out, lhs, rhs):
                return [(out, lhs, rhs, True, True)]

            def total(out, *pairs):
                return [(out, l, r, n == 0, n == len(pairs) - 1) for n, (l, r) in enumerate(pairs)]

            def step(it, s):
                i = 2 * it + s
                hat = [cm[:, s, d] for d in (0, 1)]
                dve = lambda d, name, at=i: (dve_done[d], count(DVE_STEPS, at, name) + 1)
                act = lambda d, name, at=i: (act_done[d], count(ACT_STEPS, at, name) + 1)
                for d in (0, 1):
                    h = hat[d]
                    stage(d, i, "MB", lambda j, r: alone(wide(p0[:, d])[:, j], h[:, B_HAT, j, :],
                                                         h[:, A_HAT:R_HAT + 1, j, :]),
                          [(loaded[d][s], 80 * it + 80), (act_done[d], len(ACT_STEPS) * i + 1)])
                for d in (0, 1):
                    h = hat[d]
                    stage(d, i, "MK", lambda j, r: alone(wide(p1[:, d])[:, j], h[:, K_HAT, j, :],
                                                         h[:, A_HAT:R_HAT + 1, j, :]),
                          [(dve_done[d], len(DVE_STEPS) * i + 1)])
                for d in (0, 1):
                    h = hat[d]
                    stage(d, i, "MM", lambda j, r: alone(narrow(p0[:, d, 0])[:, j], h[:, A_HAT, j, :],
                                                         h[:, B_HAT, j, :]), [dve(d, "MB")])
                for n in range(1, LEVELS):
                    for d in (0, 1):
                        stage(d, i, f"Z{n}", lambda j, r: alone(narrow(p0[:, d, 0])[:, j], mb[:, d, j, 0, :],
                                                                tt[:, d, 0, j, :]), [dve(d, f"T{n - 1}")])
                    for d in (0, 1):
                        both = n < LEVELS - 1
                        stage(d, i, f"T{n}", lambda j, r: (
                            alone(narrow(p1[:, d, 0])[:, j], tt[:, d, 1, j, :], z[:, d, j, :]) if both else [])
                            + alone(narrow(p1[:, d, 1])[:, j], z[:, d, j, :], tt[:, d, 1, j, :]),
                            [dve(d, f"Z{n}")])
                for d in (0, 1):
                    h = hat[d]
                    stage(d, i, "X", lambda j, r: total(narrow(p0[:, d, 0])[:, j], (h[:, A_HAT, j, :], st[:, d, j, :]),
                                                        (mk[:, d, j, 0, :], vv[:, s, d, j, :])), [])
                for d in (0, 1):
                    stage(d, i, "U", lambda j, r: alone(narrow(p0[:, d, 1])[:, j], tt[:, d, 1, j, :], x_[:, d, j, :]),
                          [act(d, "X"), dve(d, f"T{LEVELS - 1}")])
                for d in (0, 1):
                    h = hat[d]
                    stage(d, i, "Y", lambda j, r: total(narrow(p1[:, d, 0])[:, j], (h[:, R_HAT, j, :], st[:, d, j, :]),
                                                        (mb[:, d, j, 1, :], u_[:, d, j, :]),
                                                        (mk[:, d, j, 1, :], vv[:, s, d, j, :])), [act(d, "U")])
                    stage(d, i, "S", lambda j, r: total(narrow(p1[:, d, 1])[:, j], (tk[:, s, d, 0, j, :], u_[:, d, j, :]),
                                                        (tk[:, s, d, 1, j, :], vv[:, s, d, j, :])), [])

            with pe.Fori(0, ITERS) as it:
                step(it, 0)
                step(it, 1)

        @block.scalar
        def _(act):
            for d in (0, 1):
                act.sem_inc(act_done[d], 1)
            with act.Fori(0, ITERS) as it:
                for s in (0, 1):
                    i = 2 * it + s
                    for name, src, dst in (("X", lambda d: p0[:, d, 0, :], lambda d: x_[:, d]),
                                           ("U", lambda d: p0[:, d, 1, :], lambda d: u_[:, d]),
                                           ("Y", lambda d: p1[:, d, 0, :], lambda d: y_[:, s, d])):
                        for d in (0, 1):
                            act.wait_ge(pe_done[d], count(PE_STEPS, i, name))
                            if name == "Y":
                                act.wait_ge(y_out[d][s], 16 * it + 16)
                            act.activation(dst(d), narrow(src(d)), ACT.Copy).then_inc(act_done[d], 1)

        @block.vector
        def _(dve):
            for d in (0, 1):
                dve.sem_inc(dve_done[d], 1)
            mask = lambda d, level: g.wmask[:, d, level, :]
            with dve.Fori(0, ITERS) as it:
                for s in (0, 1):
                    i = 2 * it + s
                    pairs = lambda d: g.wmask[:, d, STRICT:UPTO + 1, :].unsqueeze(1).to_broadcast([P, PAIRS, 2, WC])
                    for d in (0, 1):
                        dve.wait_ge(pe_done[d], count(PE_STEPS, i, "MB"))
                        dve.tensor_tensor(mb[:, d], wide(p0[:, d]), pairs(d), ALU.mult).then_inc(dve_done[d], 1)
                    for d in (0, 1):
                        dve.wait_ge(pe_done[d], count(PE_STEPS, i, "MK"))
                        dve.tensor_tensor(mk[:, d], wide(p1[:, d]), pairs(d), ALU.mult).then_inc(dve_done[d], 1)
                    for d in (0, 1):
                        dve.wait_ge(pe_done[d], count(PE_STEPS, i, "MM"))
                        dve.tensor_tensor(tt[:, d, 0], narrow(p0[:, d, 0]), over_heads(mask(d, LEVEL)), ALU.mult)
                        dve.wait_ge(dve_done[d], count(DVE_STEPS, i, "MB") + 1)
                        dve.tensor_tensor(tt[:, d, 1], mb[:, d, :, 0, :], over_heads(mask(1 - d, LEVEL)),
                                          ALU.mult).then_inc(chain[d], 1)
                        dve.wait_ge(chain[d], i + 1)
                        dve.tensor_tensor(tt[:, d], tt[:, d], g.ident_w.unsqueeze(1).unsqueeze(1)
                                          .to_broadcast([P, 2, PAIRS, WC]), ALU.add).then_inc(dve_done[d], 1)
                    for n in range(1, LEVELS):
                        for d in (0, 1):
                            dve.wait_ge(pe_done[d], count(PE_STEPS, i, f"Z{n}"))
                            dve.tensor_tensor(z[:, d], narrow(p0[:, d, 0]), over_heads(mask(d, LEVEL + n)),
                                              ALU.mult).then_inc(dve_done[d], 1)
                        for d in (0, 1):
                            lo = 0 if n < LEVELS - 1 else 1
                            dve.wait_ge(pe_done[d], count(PE_STEPS, i, f"T{n}"))
                            t = tt[:, d, lo:2].rearrange("p k j w -> p k (j w)")
                            dve.tensor_tensor(t, t, p1[:, d, lo:2, :], ALU.add).then_inc(dve_done[d], 1)
                    for d in (0, 1):
                        dve.wait_ge(pe_done[d], count(PE_STEPS, i, "S"))
                        dve.tensor_tensor(st[:, d], st[:, d], narrow(p1[:, d, 1]), ALU.add).then_inc(summed[d], 1)
                        dve.wait_ge(summed[d], i + 1)
                        dve.sem_inc(dve_ready, 1)
                        end = carry[:, d, bass.ds(chunk(d, i), 1), :].squeeze(1)
                        dve.tensor_tensor(st[:, d], st[:, d], end.unsqueeze(2).to_broadcast([P, PAIRS, HD]),
                                          ALU.mult).then_inc(dve_done[d], 1)


def phase_wkv_out(nc, sem, io, g, low, bonus, y_r):
    y_in = [sem("wo_y_in0"), sem("wo_y_in1")]
    norm_chain, sq_done, root_done = sem("wo_norm_chain"), sem("wo_sq_done"), sem("wo_root_done")
    normed, go, tr_full, tr_chain, tr_done = (sem("wo_normed"), sem("wo_go"), sem("wo_tr_full"),
                                              sem("wo_tr_chain"), sem("wo_tr_done"))
    g_in, g_full, g_done = sem("wo_g_in"), sem("wo_g_full"), sem("wo_g_done")
    CHAIN = 6
    with ExitStack() as ctx:
        sb = lambda n, shape: ctx.enter_context(nc.sbuf_tensor("wo_" + n, shape, F32))
        y = sb("y", [P, 2, 2, PAIRS, HD])
        sq = sb("sq", [P, PAIRS, HD])
        mean, var = sb("mean", [P, PAIRS]), sb("var", [P, PAIRS])
        g2 = sb("g2", [P, D])
        ps = ctx.enter_context(nc.psum_tensor("wo_ps", [P, 2, 512], F32))
        pg = ctx.enter_context(nc.psum_tensor("wo_pg", [P, 2, 1024], F32))
        block = ctx.enter_context(nc.Block())
        per_head = lambda a: a.unsqueeze(2).to_broadcast([P, PAIRS, HD])

        @block.sync
        def _(sp):
            sp.dma_start(g2[:, :], io["g2"]).then_inc(g_in, 16)

            def load(it, s):
                for d in (0, 1):
                    src = io["wkv_y"][d, bass.ds(2 * it + s, 1)].squeeze(0).rearrange("p (j w) -> p j w", w=HD)
                    sp.dma_start(y[:, s, d, :, :], src).then_inc(y_in[s], 16)

            stream(sp, NWC, load, used=tr_full)

        @block.tensor
        def _(pe):
            with pe.Fori(0, NWC // 2) as it:
                for s in (0, 1):
                    n = 2 * it + s
                    pe.wait_ge(normed, n + 1)
                    pe.wait_ge(tr_done, n + 1)
                    pe.sem_inc(go, 1)
                    for j in range(PAIRS):
                        for rows in (slice(0, 64), slice(64, 128)):
                            last = pe.matmul(ps[rows, s, WC * j:WC * j + WC], y[rows, s, 0, j, :],
                                             g.ident_w[rows], start=True, stop=True)
                    last.then_inc(tr_full, 1)
            pe.wait_ge(g_in, 16)
            for j in range(PAIRS):
                if j >= 2:
                    pe.wait_ge(g_done, j - 1)
                for lo, hi in BANKS:
                    last = pe.matmul(pg[:, j % 2, lo:hi], g2[:, P * j:P * j + P], low[:, 2, lo:hi],
                                     start=True, stop=True)
                last.then_inc(g_full, 1)

        @block.scalar
        def _(act):
            with act.Fori(0, NWC // 2) as it:
                for s in (0, 1):
                    n = 2 * it + s
                    act.wait_ge(norm_chain, CHAIN * n + 3)
                    act.activation(sq[:, :, :], y[:, s, 0, :, :], ACT.Square).then_inc(sq_done, 1)
                    act.wait_ge(norm_chain, CHAIN * n + 6)
                    act.activation(var[:, :], var[:, :], ACT.Sqrt).then_inc(root_done, 1)

        @block.vector
        def _(dve):
            dve.sem_inc(tr_done, 2)
            with dve.Fori(0, NWC // 2) as it:
                for s in (0, 1):
                    n = 2 * it + s
                    yy = y[:, s, 0, :, :]

                    def then(ins, at):
                        ins.then_inc(norm_chain, 1)
                        dve.wait_ge(norm_chain, CHAIN * n + at)

                    dve.wait_ge(y_in[s], 32 * it + 32)
                    then(dve.tensor_tensor(yy, yy, y[:, s, 1, :, :], ALU.add), 1)
                    then(dve.tensor_reduce(mean[:, :], yy, AX.X, ALU.add), 2)
                    dve.tensor_scalar(mean[:, :], mean[:, :], 1.0 / HD, None, ALU.mult).then_inc(tr_chain, 1)
                    dve.wait_ge(tr_chain, 3 * n + 1)
                    then(dve.tensor_tensor(yy, yy, per_head(mean[:, :]), ALU.subtract), 3)
                    dve.wait_ge(sq_done, n + 1)
                    then(dve.tensor_reduce(var[:, :], sq[:, :, :], AX.X, ALU.add), 4)
                    then(dve.tensor_scalar(var[:, :], var[:, :], 1.0 / HD, 64e-5, ALU.mult, ALU.add), 5)
                    then(dve.reciprocal(var[:, :], var[:, :]), 6)
                    dve.wait_ge(root_done, n + 1)
                    dve.tensor_tensor(yy, yy, per_head(var[:, :]), ALU.mult).then_inc(normed, 1)
                    dve.wait_ge(tr_full, n + 1)
                    out = y_r[:, :, bass.ds(WC * n, WC)]
                    dve.tensor_tensor(out, ps[:, s, :].rearrange("p (j t) -> p j t", t=WC),
                                      per_head(g.v("lnx_w")), ALU.mult).then_inc(tr_chain, 1)
                    dve.wait_ge(tr_chain, 3 * n + 2)
                    dve.tensor_tensor(out, out, per_head(g.v("lnx_b")), ALU.add).then_inc(tr_chain, 1)
                    dve.wait_ge(tr_chain, 3 * n + 3)
                    dve.tensor_tensor(out, out, bonus[:, :, bass.ds(WC * n, WC)], ALU.add).then_inc(tr_done, 1)
            dve.wait_ge(tr_done, NWC + 2)
            for j in range(PAIRS):
                dve.wait_ge(g_full, j + 1)
                dve.tensor_tensor(y_r[:, j, :], y_r[:, j, :], pg[:, j % 2, 0:T], ALU.mult).then_inc(g_done, 1)


def build(nc, io):
    with ExitStack() as ctx:
        serial = [0]

        def run(phase, *args, **kw):
            used = []
            serial[0] += 1

            def sem(name):
                used.append(nc.alloc_semaphore(f"p{serial[0]}_{name}"))
                return used[-1]

            phase(nc, sem, *args, **kw)
            nc.all_engine_barrier()
            nc.clear_and_free_semaphores(used)
            nc.all_engine_barrier()

        def sb(scope, name, shape):
            return scope.enter_context(nc.sbuf_tensor(name, shape, F32))

        g = Resident()
        g.h = sb(ctx, "h", [P, KD, T])
        g.mod = sb(ctx, "mod", [P, 6 * KD, 2])
        g.cst, g.vec, g.row = sb(ctx, "cst", [P, CST_N]), sb(ctx, "vec", [P, VEC_N]), sb(ctx, "row", [P, ROW_N])
        g.mu_q, g.mu_own = sb(ctx, "mu_q", [P, 27, 4]), sb(ctx, "mu_own", [P, 27])
        g.k_a_c, g.neg_a = sb(ctx, "k_a_c", [P, KD]), sb(ctx, "neg_a", [P, 64])
        g.v = lambda name: g.vec[:, VEC_AT[name][0]:VEC_AT[name][1]]
        g.r = lambda name: g.row[:, ROW_AT[name][0]:ROW_AT[name][1]]
        c = lambda name: g.cst[:, CST_AT[name][0]:CST_AT[name][1]]
        g.ident, g.ones, g.head_ones, g.ident_w = c("ident"), c("ones"), c("head_ones"), c("ident_w")
        g.tri = c("tri").rearrange("p (d f) -> p d f", d=2)
        g.wmask = c("wmask").rearrange("p (d l f) -> p d l f", d=2, f=WC)
        g.reset = c("reset").rearrange("p (d t) -> p d t", d=2)
        g.qmask = c("qmask").rearrange("p (m q) -> p m q", q=4)

        run(phase_load, io, g)
        run(phase_modulation, io, g)
        with ExitStack() as scope:
            g.x = sb(scope, "x", [P, KD, T])
            run(phase_load_x, io, g)
            run(phase_norm, g, "norm1", g.v("norm1"), 0, g.h)
        with ExitStack() as mixers:
            g.mix = sb(mixers, "mix", [P, KD, T])
            with ExitStack() as mamba:
                y_tok = sb(mamba, "y_tok", [P, NCH, M_INNER])
                with ExitStack() as scan:
                    x_tok = sb(scan, "x_tok", [P, NCH, M_INNER])
                    b_chan, c_chan = g.mix[:, 0:M_GROUPS, :], g.mix[:, M_GROUPS:2 * M_GROUPS, :]
                    b_tok = sb(scan, "b_tok", [P, NCH, M_GROUPS * M_STATE])
                    dts = {n: sb(scan, n, [P, NCH, 64]) for n in DT_PARTS}
                    run(phase_conv, io, g, "xin", 0, KI, None, x_tok)
                    run(phase_conv, io, g, "bin", KI, M_GROUPS, b_chan, b_tok)
                    run(phase_conv, io, g, "cin", KI + M_GROUPS, M_GROUPS, c_chan, None)
                    run(phase_dt, io, g, dts)
                    run(phase_ssd, io, g, dts, x_tok, b_chan, c_chan, b_tok, y_tok)
                y_chan = sb(mamba, "y_chan", [P, KI, T])
                run(phase_m_gate, io, g, y_tok, y_chan)
                run(phase_mix_out, g, "m_out", io["w_m"], y_chan, KI, add=False)
            with ExitStack() as rwkv:
                low = sb(rwkv, "low", [P, 3, T])
                bonus = sb(rwkv, "bonus", [P, KD, T])
                carry = sb(rwkv, "carry", [P, 2, NWC, PAIRS])
                run(phase_low, io, g, low)
                run(phase_rwkv_in, io, g, low, bonus, carry)
                run(phase_wkv, io, g, carry, 0, CTX // WC, None, io["wkv_out"], "wc")
                run(phase_wkv, io, g, carry, CTX // WC, LAT // WC, io["wkv_in"], None, "wl")
                y_r = sb(rwkv, "y_r", [P, KD, T])
                run(phase_wkv_out, io, g, low, bonus, y_r)
                run(phase_mix_out, g, "r_out", io["w_r"], y_r, KD, add=True)
            g.x = sb(mixers, "x_again", [P, KD, T])
            run(phase_load_x, io, g)
            run(phase_residual, g, "w_o", io["w_o"], g.mix, KD, 2 * KD)
            run(phase_norm, g, "norm2", g.v("norm2"), 3 * KD, g.h)
            with ExitStack() as ffn:
                hidden = sb(ffn, "hidden", [P, KF, T])
                run(phase_up, io, g, hidden)
                run(phase_residual, g, "w_down", io["w_down"], hidden, KF, 5 * KD)
            run(phase_norm, g, "final", g.v("final"), None, g.h)
            run(phase_store, io, g)


def _tiles(w):
    k, m = w.shape
    return np.ascontiguousarray(w.reshape(k // P, P, m // P, P).transpose(2, 1, 0, 3).reshape(m // P, P, k))


def _cols(v):
    return np.ascontiguousarray(v.reshape(-1, P).T)


def _constants():
    f32 = np.float32
    i, f = np.arange(P)[:, None], np.arange(P)[None, :]
    r, w = np.arange(P)[:, None] % WC, np.arange(WC)[None, :]
    masks = []
    for d in (0, 1):
        a, b = (r, w) if d == 0 else (w, r)
        masks += [b > a, b >= a]
        for n in range(LEVELS):
            size = 1 << n
            masks.append((a // size % 2 == 1) & (b // size == a // size - 1))
    t = np.arange(T)
    ch = (np.arange(27)[None, :, None] * P + np.arange(P)[:, None, None]) // QUARTER
    parts = dict(
        ident=np.eye(P), ones=np.ones((P, P)), head_ones=(i // HD == f // HD),
        tri=np.concatenate([f >= i, f <= i], 1), wmask=np.concatenate(masks, 1),
        reset=np.repeat(np.concatenate([t % WC != 0, t % WC != WC - 1])[None], P, 0),
        qmask=(ch == np.arange(4)[None, None, :]).reshape(P, -1), ident_w=(r == w))
    return np.ascontiguousarray(np.concatenate([parts[n].astype(f32) for n in CST], 1))


def _lay_out(i):
    a = {n: np.asarray(v) for n, v in i.items()}
    l = {n: a[n][0] for n in a if n not in ("c_ctx", "final_norm_w")}
    w_in = l["w_in"]
    o1, o2 = M_INNER, M_INNER + M_INNER + 2 * M_GROUPS * M_STATE
    o3 = o2 + 2 * M_HEADS
    o4 = o3 + R_COLS
    z, xbc, dt, rw, gates = w_in[:, :o1], w_in[:, o1:o2], w_in[:, o2:o3], w_in[:, o3:o4], w_in[:, o4:]
    rt, gt = _tiles(rw), _tiles(gates)
    low_w = rt[[8, 25, 26]]
    up = np.stack([l["w2"].reshape(P, D), l["a2"].reshape(P, D)])
    up = up.reshape(2, P, KD, P).transpose(2, 1, 0, 3).reshape(KD, P, 2 * P)
    rkv_w = np.concatenate([rt[0:8], rt[9:17], rt[17:25], up], 2)
    vec = dict(norm1=l["norm1_w"], norm2=l["norm2_w"], final=a["final_norm_w"],
               conv_b=l["conv_b"], m_norm=l["m_norm_w"], mu=l["mu_shift"], w0=l["w0"], a0=l["a0"],
               k_k=l["k_k"], k_a=l["k_a"], r_k=l["r_k"], lnx_w=l["lnx_w"], lnx_b=l["lnx_b"])
    vec = {n: _cols(v) for n, v in vec.items()}
    vec["b_ada"] = np.repeat(_cols(l["b_ada"]), 2, 1)
    vec["conv_w"] = l["conv_w"].reshape(M_CONV, 24, P).transpose(2, 1, 0).reshape(P, -1)
    row = dict(dt_bias=l["dt_bias"], a_log=l["a_log"], d_skip=l["d_skip"])
    row = np.concatenate([np.repeat(row[n].reshape(1, -1), P, 0) for n in ROW], 1)
    gu = _tiles(l["w_gu"])
    ssm = np.stack([l["state_ssm_fwd"], l["state_ssm_bwd"]])
    ssm = ssm.reshape(2, M_GROUPS, GI, M_STATE).transpose(0, 1, 3, 2)
    wkv = np.stack([l["state_wkv_fwd"], l["state_wkv_bwd"]])
    wkv = wkv.reshape(2, PAIRS, 2, HD, HD).transpose(0, 2, 4, 1, 3).reshape(2, P, PAIRS * HD)
    x = np.concatenate([a["x_prompt"][0], a["x_sample"][0]], 0)
    out = dict(
        x_t=x.T.reshape(KD, P, T), cond=np.stack([_cols(a["c_ctx"]), _cols(a["c"])], 2), cst=_constants(),
        vec=np.concatenate([vec[n] for n in VEC], 1), row=row,
        w_ada=_tiles(l["w_ada"]).reshape(16, 3, P, D).transpose(0, 2, 1, 3).reshape(16, P, 3 * D),
        w_xbc=_tiles(xbc), w_dt=dt.reshape(KD, P, 64).transpose(1, 0, 2).reshape(P, -1),
        w_z=z.reshape(KD, P, M_GROUPS, GI).transpose(2, 1, 0, 3).reshape(M_GROUPS, P, -1),
        w_m=np.concatenate([_tiles(l["w_m_out"]), gt[:KD]], 2), w_low=low_w, w_rkv=rkv_w,
        w_r=np.concatenate([_tiles(l["w_r_out"]), gt[KD:]], 2), w_o=_tiles(l["w_o"]),
        w_gu=np.concatenate([gu[:KF], gu[KF:]], 2), w_down=_tiles(l["w_down"]), g2=l["g2"], ssm_in=ssm, wkv_in=wkv)
    return {n: np.ascontiguousarray(v) for n, v in out.items()}


OUTS = dict(y=[KD, P, T], ssm_out=[2, M_GROUPS, M_STATE, GI], wkv_out=[2, P, PAIRS * HD])
SCRATCH = dict(chan=[2, NWC, P, 4 * PAIRS * WC], tok=[2, T, 2 * D], val=[T, D], wkv_y=[2, NWC, P, PAIRS * HD])


def declare(nc, arrays):
    io = {}
    for name, a in arrays.items():
        io[name] = nc.dram_tensor("in_" + name, a.shape, F32, kind="ExternalInput").ap()
    for name, shape in OUTS.items():
        io[name] = nc.dram_tensor("out_" + name, shape, F32, kind="ExternalOutput").ap()
    for name, shape in SCRATCH.items():
        io[name] = nc.dram_tensor("scratch_" + name, shape, F32, kind="Internal").ap()
    return io


def kernel(**inputs):
    import concourse.bacc as bacc
    from concourse.bass_utils import run_bass_kernel_spmd

    nc = bacc.Bacc("TRN2", target_bir_lowering=False, num_devices=1)
    arrays = _lay_out(inputs)
    build(nc, declare(nc, arrays))
    sent = {"in_" + name: a for name, a in arrays.items()}
    got = run_bass_kernel_spmd(nc, [sent], core_ids=[0]).results[0]
    y = np.asarray(got["out_y"]).reshape(D, T).T
    ssm = np.asarray(got["out_ssm_out"]).transpose(0, 1, 3, 2).reshape(2, 1, 1, M_HEADS, HD, M_STATE)
    wkv = np.asarray(got["out_wkv_out"]).reshape(2, 2, HD, PAIRS, HD).transpose(0, 3, 1, 4, 2)
    wkv = wkv.reshape(2, 1, 1, R_HEADS, HD, HD)
    return y[None, :CTX], y[None, CTX:], ssm[0], ssm[1], wkv[0], wkv[1]
```

```python
from contextlib import ExitStack

import numpy as np
import concourse.bass as bass
import concourse.mybir as mybir

P = 128
D = 1024
KD = D // P
CTX, LAT = 128, 512
T = CTX + LAT
SEG = ((0, 0, CTX), (1, CTX, T))
BANKS = ((0, 512), (512, T))
GRID_W = 64
M_INNER, M_HEADS, M_GROUPS, M_STATE, M_CONV = 2048, 32, 4, 128, 5
HPG = M_HEADS // M_GROUPS
HD = 64
GI = M_INNER // M_GROUPS
KI = M_INNER // P
NCH = T // P
R_HEADS = 16
PAIRS = R_HEADS // 2
WC = 64
NWC = T // WC
D_FF = 2816
KF = D_FF // P
R_COLS = 3 * D + 2 * 64 + 2 * 64 + 128
QUARTER = R_COLS // 4
LOG_DECAY = float(np.exp(-0.5))

F32 = mybir.dt.float32
F32R = mybir.dt.float32r
ACT = mybir.ActivationFunctionType
ALU = mybir.AluOpType
AX = mybir.AxisListType

VEC = dict(norm1=KD, norm2=KD, final=KD, b_ada=96, conv_w=24 * M_CONV, conv_b=24, m_norm=KI, mu=27,
           w0=16, a0=16, k_k=KD, k_a=KD, r_k=KD, lnx_w=KD, lnx_b=KD)
ROW = dict(dt_bias=64, a_log=64, d_skip=32)
QB = WC // 2
BLOCK_GROUPS = 2 * NWC * 4 * PAIRS // P
STRICT, UPTO, BETWEEN = 0, 1, 2
CST = dict(ident=P, ones=P, head_ones=P, tri=2 * P, wmask=2 * 3 * WC, reset=2 * T,
           qmask=27 * 4, ident_w=WC, sel=2)


HALF = T // 2
PIECES = ((0, 0, 0, CTX), (1, 0, CTX, HALF), (1, 1, HALF, T))


class Resident:
    pass


def offsets(widths):
    at, out = 0, {}
    for name, n in widths.items():
        out[name] = (at, at + n)
        at += n
    return out, at


VEC_AT, VEC_N = offsets(VEC)
ROW_AT, ROW_N = offsets(ROW)
CST_AT, CST_N = offsets(CST)


def project(pe, psum, w, rhs, k_tiles):
    for lo, hi in BANKS:
        for k in range(k_tiles):
            last = pe.matmul(psum[:, lo:hi], w[:, k, :], rhs[:, k, lo:hi],
                             start=(k == 0), stop=(k == k_tiles - 1))
    return last


def halves(psum):
    return psum.rearrange("p (b n) -> p b n", b=2)[:, :, 0:HALF]


def by_half(a):
    return a.rearrange("p (b n) -> p b n", b=2)


def project_halves(pe, psum, w, rhs, k_tiles):
    for b in (0, 1):
        for k in range(k_tiles):
            last = pe.matmul(halves(psum)[:, b, :], w[:, k, :], by_half(rhs[:, k, :])[:, b, :],
                             start=(k == 0), stop=(k == k_tiles - 1))
    return last


def project_split(pe, psum, w, rhs, k_tiles):
    (wh, wl), (xh, xl) = w, rhs
    terms = ((wh, xh), (wh, xl), (wl, xh))
    for b in (0, 1):
        for k in range(k_tiles):
            for n, (a, x) in enumerate(terms):
                last = pe.matmul(halves(psum)[:, b, :], a[:, k, :], by_half(x[:, k, :])[:, b, :],
                                 start=(k == 0 and n == 0), stop=(k == k_tiles - 1 and n == len(terms) - 1))
    return last


class SplitWeights:

    def __init__(self, nc, sem, ctx, tag, n, width, source, raw, used):
        self.n, self.source, self.used, self.raw = n, source, used, raw
        self.w_in = [sem(tag + "_w_in0"), sem(tag + "_w_in1")]
        self.high, self.low = sem(tag + "_w_high"), sem(tag + "_w_low")
        self.hi = ctx.enter_context(nc.sbuf_tensor(tag + "_w_hi", [P, 2, width], F32R))
        self.lo = ctx.enter_context(nc.sbuf_tensor(tag + "_w_lo", [P, 2, width], F32R))

    def load_all(self, sp):
        stream(sp, self.n, lambda it, s: sp.dma_start(self.raw[:, s, :], self.source(2 * it + s))
               .then_inc(self.w_in[s], 16), used=self.low)

    def round_tile(self, act, it, s):
        act.wait_ge(self.w_in[s], 16 * it + 16)
        act.activation(self.hi[:, s, :], self.raw[:, s, :], ACT.Copy).then_inc(self.high, 1)

    def low_all(self, pool):
        with pool.Fori(0, self.n // 2) as it:
            for s in (0, 1):
                pool.wait_ge(self.high, 2 * it + s + 1)
                pool.tensor_tensor(self.lo[:, s, :], self.raw[:, s, :], self.hi[:, s, :].bitcast(F32),
                                   ALU.subtract).then_inc(self.low, 1)

    def rounding(self, act, use):
        for s in (0, 1):
            self.round_tile(act, 0, s)
        if self.n > 2:
            with act.Fori(0, self.n // 2 - 1) as it:
                for s in (0, 1):
                    use(it, s)
                    self.round_tile(act, it + 1, s)
        for s in (0, 1):
            use(self.n // 2 - 1, s)

    def tile(self, pe, it, s):
        pe.wait_ge(self.low, 2 * it + s + 1)
        return tiles_of(self.hi[:, s, :]), tiles_of(self.lo[:, s, :])

    def parts(self, pe, it, s):
        pe.wait_ge(self.low, 2 * it + s + 1)
        return self.hi[:, s, :], self.lo[:, s, :]


def stream(sp, n, load, used):
    load(0, 0)
    load(0, 1)
    if n > 2:
        with sp.Fori(1, n // 2) as it:
            for s in (0, 1):
                sp.wait_ge(used, 2 * it + s - 1)
                load(it, s)


def tiles_of(w):
    return w.rearrange("p (k m) -> p k m", m=P)


def phase_load(nc, sem, io, g):
    cst_in, vec_in, row_in = sem("cst_in"), sem("vec_in"), sem("row_in")
    derived = sem("derived")
    with nc.Block() as block:
        @block.sync
        def _(sp):
            sp.dma_start(g.cst[:, :], io["cst"]).then_inc(cst_in, 16)
            sp.dma_start(g.vec[:, :], io["vec"]).then_inc(vec_in, 16)
            sp.dma_start(g.row[:, :], io["row"]).then_inc(row_in, 16)

        @block.vector
        def _(dve):
            dve.wait_ge(vec_in, 16)
            dve.wait_ge(cst_in, 16)
            dve.tensor_tensor(g.mu_q[:, :, :], g.qmask, g.v("mu").unsqueeze(2).to_broadcast([P, 27, 4]),
                              ALU.mult).then_inc(derived, 1)
            dve.tensor_scalar(g.mu_own[:, :], g.v("mu"), -1.0, 1.0, ALU.mult, ALU.add).then_inc(derived, 1)
            dve.tensor_scalar(g.k_a_c[:, :], g.v("k_a"), -1.0, 1.0, ALU.mult, ALU.add).then_inc(derived, 1)

        @block.scalar
        def _(act):
            act.wait_ge(row_in, 16)
            act.activation(g.neg_a[:, :], g.r("a_log"), ACT.Exp).then_inc(derived, 1)
            act.wait_ge(derived, 4)
            act.mul(g.neg_a[:, :], g.neg_a[:, :], -1.0).then_inc(derived, 1)


def phase_modulation(nc, sem, io, g):
    COLS = 512
    GROUPS = 6 * D // COLS
    cond_in, cond_ready, cond_high, cond_split = (sem("cond_in"), sem("cond_ready"), sem("cond_high"),
                                                  sem("cond_split"))
    full, copied, turned = sem("ada_full"), sem("ada_copied"), sem("ada_turned")
    with ExitStack() as ctx:
        cond = ctx.enter_context(nc.sbuf_tensor("cond", [P, KD, 2], F32))
        parts = ctx.enter_context(nc.sbuf_tensor("cond_parts", [P, KD, 4], F32R))
        raw = ctx.enter_context(nc.sbuf_tensor("ada_raw", [P, 2, KD * COLS], F32))
        rows = ctx.enter_context(nc.sbuf_tensor("ada_rows", [4, GROUPS, COLS], F32))
        weights = SplitWeights(nc, sem, ctx, "ada", GROUPS, KD * COLS, lambda n: io["w_ada"][n], raw, full)
        ps = ctx.enter_context(nc.psum_tensor("ada_ps", [4, 2, 512], F32))
        pt = ctx.enter_context(nc.psum_tensor("ada_pt", [P, 512], F32))
        block = ctx.enter_context(nc.Block())

        @block.sync
        def _(sp):
            sp.dma_start(cond[:, :, :], io["cond"]).then_inc(cond_in, 16)
            weights.load_all(sp)

        @block.scalar
        def _(act):
            act.wait_ge(cond_in, 16)
            act.activation(cond[:, :, :], cond[:, :, :], ACT.Silu).then_inc(cond_ready, 1)
            act.wait_ge(cond_ready, 1)
            act.activation(parts[:, :, 0:2], cond[:, :, :], ACT.Copy).then_inc(cond_high, 1)

            def take(it, s):
                act.wait_ge(full, 2 * it + s + 1)
                act.activation(rows[:, bass.ds(2 * it + s, 1), :].squeeze(1), ps[:, s, :], ACT.Copy)\
                   .then_inc(copied, 1)

            weights.rounding(act, take)

        @block.tensor
        def _(pe):
            pe.wait_ge(cond_split, 1)

            def group(it, s):
                for n, w in enumerate(weights.parts(pe, it, s)):
                    for k in range(KD):
                        last = pe.matmul(ps[:, s, :], parts[:, k, :], w[:, COLS * k:COLS * k + COLS],
                                         start=(n == 0 and k == 0), stop=(n == 1 and k == KD - 1))
                last.then_inc(full, 1)

            group(0, 0)
            group(0, 1)
            with pe.Fori(1, GROUPS // 2) as it:
                for s in (0, 1):
                    pe.wait_ge(copied, 2 * it + s - 1)
                    group(it, s)
            pe.wait_ge(copied, GROUPS)
            flat = rows[:, :, :].rearrange("r g c -> r (g c)")
            for m in range(6 * KD):
                last = pe.matmul(pt[:, 2 * m:2 * m + 2], flat[:, P * m:P * m + P], g.sel[0:4, :],
                                 start=True, stop=True)
            last.then_inc(turned, 1)

        @block.vector
        def _(dve):
            dve.wait_ge(cond_high, 1)
            dve.tensor_tensor(parts[:, :, 2:4], cond[:, :, :], parts[:, :, 0:2].bitcast(F32), ALU.subtract)\
               .then_inc(cond_split, 1)
            weights.low_all(dve)
            dve.wait_ge(turned, 1)
            dve.tensor_tensor(g.mod[:, :, :].rearrange("p m c -> p (m c)"), pt[:, 0:12 * KD], g.v("b_ada"), ALU.add)


def phase_norm(nc, sem, g, tag, weight, shift_at, out, split=None):
    normed, rounded = sem(tag + "_normed"), sem(tag + "_rounded")
    squared, square_free = sem(tag + "_squared"), sem(tag + "_square_free")
    inv_done, rstd_done, chain = sem(tag + "_inv_done"), sem(tag + "_rstd_done"), sem(tag + "_norm_chain")
    with ExitStack() as ctx:
        sq = ctx.enter_context(nc.sbuf_tensor(tag + "_sq", [P, 2, T], F32))
        rstd = ctx.enter_context(nc.sbuf_tensor(tag + "_rstd", [P, T], F32))
        gain = ctx.enter_context(nc.sbuf_tensor(tag + "_gain", [P, KD, 2], F32))
        ps = ctx.enter_context(nc.psum_tensor(tag + "_ps", [P, 1024], F32))
        block = ctx.enter_context(nc.Block())

        @block.scalar
        def _(act):
            for k in range(KD):
                if k >= 2:
                    act.wait_ge(square_free, k - 1)
                act.activation(sq[:, k % 2, :], g.x[:, k, :], ACT.Square).then_inc(squared, 1)
            act.wait_ge(inv_done, 2)
            act.activation(rstd[:, :], rstd[:, :], ACT.Sqrt).then_inc(rstd_done, 1)
            if split is not None:
                for k in range(KD):
                    act.wait_ge(normed, k + 1)
                    act.activation(split[0][:, k, :], out[:, k, :], ACT.Copy).then_inc(rounded, 1)

        @block.tensor
        def _(pe):
            for k in range(KD):
                pe.wait_ge(squared, k + 1)
                for lo, hi in BANKS:
                    last = pe.matmul(ps[:, lo:hi], g.ones, sq[:, k % 2, lo:hi],
                                     start=(k == 0), stop=(k == KD - 1))
                last.then_inc(square_free, 1)
        @block.vector
        def _(dve):
            if shift_at is not None:
                scale = g.mod[:, shift_at + KD:shift_at + 2 * KD, :]
                dve.scalar_tensor_tensor(out=gain[:, :, :], in0=scale, scalar=1.0,
                                         in1=weight.unsqueeze(2).to_broadcast([P, KD, 2]),
                                         op0=ALU.add, op1=ALU.mult).then_inc(chain, 1)
            else:
                dve.tensor_copy(gain[:, :, :], weight.unsqueeze(2).to_broadcast([P, KD, 2])).then_inc(chain, 1)
            dve.wait_ge(square_free, KD)
            dve.tensor_scalar(rstd[:, :], ps[:, 0:T], 1.0 / D, 1e-6, ALU.mult, ALU.add).then_inc(inv_done, 1)
            dve.wait_ge(inv_done, 1)
            dve.reciprocal(rstd[:, :], rstd[:, :]).then_inc(inv_done, 1)
            dve.wait_ge(rstd_done, 1)
            dve.wait_ge(chain, 1)
            for k in range(KD):
                dve.tensor_tensor(out[:, k, :], g.x[:, k, :], rstd[:, :], ALU.mult).then_inc(chain, 1)
            def low_part(k):
                dve.wait_ge(rounded, k + 1)
                dve.tensor_tensor(split[1][:, k, :], out[:, k, :], split[0][:, k, :].bitcast(F32), ALU.subtract)

            for k in range(KD):
                dve.wait_ge(chain, k + 2)
                for c, lo, hi in SEG:
                    if shift_at is not None:
                        last = dve.tensor_scalar(out[:, k, lo:hi], out[:, k, lo:hi], gain[:, k, c:c + 1],
                                          g.mod[:, shift_at + k, c:c + 1], ALU.mult, ALU.add)
                    else:
                        last = dve.tensor_scalar(out[:, k, lo:hi], out[:, k, lo:hi], gain[:, k, c:c + 1], None,
                                                 ALU.mult)
                last.then_inc(normed, 1)
                if split is not None and k > 0:
                    low_part(k - 1)
            if split is not None:
                low_part(KD - 1)


def phase_conv(nc, sem, io, g, tag, first, n, keep, tok):
    w_in = [sem(tag + "_w_in0"), sem(tag + "_w_in1")]
    psum_full, psum_free = sem(tag + "_psum_full"), sem(tag + "_psum_free")
    padded, pad_free, conv = sem(tag + "_padded"), sem(tag + "_pad_free"), sem(tag + "_conv_chain")
    conv_free, act_done, act_free = sem(tag + "_conv_free"), sem(tag + "_act_done"), sem(tag + "_act_free")
    tr_full, tr_free, kept = sem(tag + "_tr_full"), sem(tag + "_tr_free"), sem(tag + "_kept")
    PAD = M_CONV // 2
    W_PAD = T + 3 * PAD
    W_OUT = T + PAD
    PARTS = ((0, 0, CTX), (CTX + PAD, CTX, T))
    with ExitStack() as ctx:
        w = ctx.enter_context(nc.sbuf_tensor(tag + "_w", [P, 2, KD * P], F32))
        pad = ctx.enter_context(nc.sbuf_tensor(tag + "_pad", [P, 2, W_PAD], F32))
        acc = ctx.enter_context(nc.sbuf_tensor(tag + "_acc", [P, 2, W_OUT], F32))
        res = ctx.enter_context(nc.sbuf_tensor(tag + "_res", [P, 2, T], F32))
        ps = ctx.enter_context(nc.psum_tensor(tag + "_ps", [P, 2, 1024], F32))
        pt = ctx.enter_context(nc.psum_tensor(tag + "_pt", [P, 2, 1024], F32))
        zeroed = sem(tag + "_pad_zeroed")
        block = ctx.enter_context(nc.Block())
        cw = g.v("conv_w").rearrange("p (j i) -> p j i", i=M_CONV)

        @block.sync
        def _(sp):
            stream(sp, n, lambda it, s: sp.dma_start(w[:, s, :], io["w_xbc"][2 * it + s + first])
                   .then_inc(w_in[s], 16), used=psum_full)

        @block.gpsimd
        def _(pool):
            pool.memset(pad[:, :, :], 0.0).then_inc(zeroed, 1)

        @block.tensor
        def _(pe):
            def tile(it, s):
                pe.wait_ge(w_in[s], 16 * it + 16)
                pe.wait_ge(psum_free, 2 * it + s + 1)
                project(pe, ps[:, s, :], tiles_of(w[:, s, :]), g.h, KD).then_inc(psum_full, 1)

            def turn(it, s):
                if tok is None:
                    return
                pe.wait_ge(act_done, 2 * it + s + 1)
                pe.wait_ge(tr_free, 2 * it + s + 1)
                for c in range(NCH):
                    last = pe.transpose(pt[:, s, P * c:P * c + P], res[:, s, P * c:P * c + P], g.ident)
                last.then_inc(tr_full, 1)

            tile(0, 0)
            if n > 2:
                with pe.Fori(0, n // 2 - 1) as it:
                    tile(it, 1)
                    turn(it, 0)
                    tile(it + 1, 0)
                    turn(it, 1)
            tile(n // 2 - 1, 1)
            turn(n // 2 - 1, 0)
            turn(n // 2 - 1, 1)

        @block.scalar
        def _(act):
            act.sem_inc(psum_free, 2)
            act.sem_inc(conv_free, 2)
            act.wait_ge(zeroed, 1)
            with act.Fori(0, n // 2) as it:
                for s in (0, 1):
                    act.wait_ge(psum_full, 2 * it + s + 1)
                    act.wait_ge(pad_free, 2 * it + s + 1)
                    act.activation(pad[:, s, PAD:PAD + CTX], ps[:, s, 0:CTX], ACT.Copy)
                    act.activation(pad[:, s, 2 * PAD + CTX:2 * PAD + T], ps[:, s, CTX:T],
                                   ACT.Copy).then_inc(padded, 1)
                    act.wait_ge(padded, 2 * it + s + 1)
                    act.sem_inc(psum_free, 1)
                for s in (0, 1):
                    act.wait_ge(conv, 2 * M_CONV * it + M_CONV * s + M_CONV)
                    act.wait_ge(act_free, 2 * it + s + 1)
                    for at, lo, hi in PARTS:
                        last = act.activation(res[:, s, lo:hi], acc[:, s, at:at + hi - lo], ACT.Silu,
                                              bias=g.v("conv_b")[:, bass.ds(2 * it + s + first, 1)])
                    last.then_inc(act_done, 1)
                    act.wait_ge(act_done, 2 * it + s + 1)
                    act.sem_inc(conv_free, 1)

        @block.vector
        def _(dve):
            dve.sem_inc(pad_free, 2)
            dve.sem_inc(tr_free, 2)
            dve.sem_inc(act_free, 2)
            with dve.Fori(0, n // 2) as it:
                for s in (0, 1):
                    dve.wait_ge(padded, 2 * it + s + 1)
                    dve.wait_ge(conv_free, 2 * it + s + 1)
                    for i in range(M_CONV):
                        src, wi = pad[:, s, i:i + W_OUT], cw[:, bass.ds(2 * it + s + first, 1), i]
                        if i == 0:
                            dve.tensor_scalar(acc[:, s, :], src, wi, None, ALU.mult).then_inc(conv, 1)
                        else:
                            dve.wait_ge(conv, 2 * M_CONV * it + M_CONV * s + i)
                            dve.scalar_tensor_tensor(out=acc[:, s, :], in0=src, scalar=wi, in1=acc[:, s, :],
                                                     op0=ALU.mult, op1=ALU.add).then_inc(conv, 1)
                    dve.wait_ge(conv, 2 * M_CONV * it + M_CONV * s + M_CONV)
                    dve.sem_inc(pad_free, 1)
                for s in (0, 1):
                    if keep is not None:
                        dve.wait_ge(act_done, 2 * it + s + 1)
                        dve.tensor_copy(keep[:, bass.ds(2 * it + s, 1), :].squeeze(1),
                                        res[:, s, :]).then_inc(kept, 1)
                        dve.wait_ge(kept, 2 * it + s + 1)
                    if tok is not None:
                        dve.wait_ge(tr_full, 2 * it + s + 1)
                        dve.tensor_copy(tok[:, :, bass.ds((2 * it + s) * P, P)],
                                        pt[:, s, 0:T].rearrange("p (c m) -> p c m", m=P)).then_inc(tr_free, 1)
                    dve.sem_inc(act_free, 1)


DT_PARTS = ("dt", "da", "cs", "ecs", "edec", "etot")


def phase_dt(nc, sem, io, g, dts):
    rows_full, rows_ready, rows_out = sem("dt_rows_full"), sem("dt_rows_ready"), sem("dt_rows_out")
    w_in, raw_full, cum_full = sem("dt_w_in"), sem("dt_raw_full"), sem("dt_cum_full")
    vec, act_done = sem("dt_vec"), sem("dt_act")
    N = NCH * 64
    SERIES = [1.0 / n for n in (13, 11, 9, 7, 5, 3)]
    with ExitStack() as ctx:
        w = ctx.enter_context(nc.sbuf_tensor("dt_w", [P, KD, 64], F32))
        raw = ctx.enter_context(nc.sbuf_tensor("dt_raw", [P, NCH, 64], F32))
        e = ctx.enter_context(nc.sbuf_tensor("dt_e", [P, NCH, 64], F32))
        s2 = ctx.enter_context(nc.sbuf_tensor("dt_s2", [P, NCH, 64], F32))
        q = ctx.enter_context(nc.sbuf_tensor("dt_q", [P, NCH, 64], F32))
        pr = ctx.enter_context(nc.psum_tensor("dt_pr", [P, 512], F32))
        pc = ctx.enter_context(nc.psum_tensor("dt_pc", [P, 512], F32))
        pt = ctx.enter_context(nc.psum_tensor("dt_pt", [P, 512], F32))
        prow = ctx.enter_context(nc.psum_tensor("dt_prow", [P, NCH, P], F32))
        rows = ctx.enter_context(nc.sbuf_tensor("dt_rows", [64, NCH, P], F32))
        block = ctx.enter_context(nc.Block())
        view = lambda p: p[:, 0:N].rearrange("p (c n) -> p c n", n=64)
        over_chunks = lambda r: r.unsqueeze(1).to_broadcast([P, NCH, 64])

        @block.sync
        def _(sp):
            sp.dma_start(w[:, :, :], io["w_dt"].rearrange("p (k n) -> p k n", n=64)).then_inc(w_in, 16)
            sp.wait_ge(rows_ready, 1)
            sp.dma_start(io["cs_rows"].rearrange("c n t -> n c t"), rows[:, :, :]).then_inc(rows_out, 16)
            sp.wait_ge(rows_out, 16)

        @block.tensor
        def _(pe):
            pe.wait_ge(w_in, 16)
            for c in range(NCH):
                for k in range(KD):
                    last = pe.matmul(pr[:, 64 * c:64 * c + 64], g.h[:, k, P * c:P * c + P], w[:, k, :],
                                     start=(k == 0), stop=(k == KD - 1))
            last.then_inc(raw_full, 1)
            pe.wait_ge(vec, DA_DONE)
            for d in (0, 1):
                half = slice(32 * d, 32 * d + 32)
                pe.matmul(view(pc)[:, :, half], g.tri[:, d, :], dts["da"][:, :, half], start=True, stop=True)
            pe.matmul(view(pt), g.ones, dts["da"][:, :, :], start=True, stop=True).then_inc(cum_full, 1)
            pe.wait_ge(vec, DA_DONE + 1)
            for c in range(NCH):
                last = pe.transpose(prow[0:64, c, :], dts["cs"][:, c, :], g.ident)
            last.then_inc(rows_full, 1)

        steps = [0]

        @block.vector
        def _(dve):
            def then(ins):
                steps[0] += 1
                ins.then_inc(vec, 1)
                dve.wait_ge(vec, steps[0])

            dve.wait_ge(raw_full, 1)
            then(dve.tensor_tensor(raw[:, :, :], view(pr), over_chunks(g.r("dt_bias")), ALU.add))
            dve.wait_ge(act_done, 2)
            then(dve.tensor_scalar(q[:, :, :], e[:, :, :], 2.0, None, ALU.add))
            then(dve.reciprocal(q[:, :, :], q[:, :, :]))
            then(dve.tensor_tensor(e[:, :, :], e[:, :, :], q[:, :, :], ALU.mult))
            then(dve.tensor_tensor(s2[:, :, :], e[:, :, :], e[:, :, :], ALU.mult))
            then(dve.tensor_scalar(q[:, :, :], s2[:, :, :], SERIES[0], None, ALU.mult))
            for c in SERIES[1:]:
                then(dve.scalar_tensor_tensor(out=q[:, :, :], in0=q[:, :, :], scalar=c, in1=s2[:, :, :],
                                              op0=ALU.add, op1=ALU.mult))
            then(dve.scalar_tensor_tensor(out=q[:, :, :], in0=q[:, :, :], scalar=1.0, in1=e[:, :, :],
                                          op0=ALU.add, op1=ALU.mult))
            then(dve.tensor_scalar(q[:, :, :], q[:, :, :], 2.0, None, ALU.mult))
            then(dve.scalar_tensor_tensor(out=dts["dt"][:, :, :], in0=raw[:, :, :], scalar=0.0, in1=q[:, :, :],
                                          op0=ALU.max, op1=ALU.add))
            then(dve.tensor_tensor(dts["da"][:, :, :], dts["dt"][:, :, :], over_chunks(g.neg_a[:, :]), ALU.mult))
            assert steps[0] == DA_DONE
            dve.wait_ge(cum_full, 1)
            then(dve.tensor_copy(dts["cs"][:, :, :], view(pc)))
            then(dve.tensor_copy(dts["etot"][:, :, :], view(pt)))
            then(dve.tensor_tensor(dts["edec"][:, :, :], dts["etot"][:, :, :], dts["cs"][:, :, :], ALU.subtract))
            dve.wait_ge(rows_full, 1)
            dve.tensor_copy(rows[:, :, :], prow[0:64, :, :]).then_inc(rows_ready, 1)
            dve.wait_ge(act_done, 3)
            then(dve.tensor_tensor(dts["edec"][:, :, :], dts["edec"][:, :, :], dts["dt"][:, :, :], ALU.mult))

        @block.scalar
        def _(act):
            act.wait_ge(vec, 1)
            act.activation(e[:, :, :], raw[:, :, :], ACT.Abs).then_inc(act_done, 1)
            act.wait_ge(act_done, 1)
            act.activation(e[:, :, :], e[:, :, :], ACT.Exp, scale=-1.0).then_inc(act_done, 1)
            act.wait_ge(vec, DA_DONE + 3)
            act.activation(dts["ecs"][:, :, :], dts["cs"][:, :, :], ACT.Exp)
            act.activation(dts["etot"][:, :, :], dts["etot"][:, :, :], ACT.Exp)
            act.activation(dts["edec"][:, :, :], dts["edec"][:, :, :], ACT.Exp).then_inc(act_done, 1)


DA_DONE = 15


def phase_ssd(nc, sem, io, g, dts, x_tok, b_chan, c_chan, b_tok, y_tok):
    UNITS = 2 * NCH
    chunk = lambda u: 0 if u < 2 else (u // 2 if u % 2 == 0 else NCH - u // 2)
    with_state = lambda u: u >= 2
    makes_state = lambda u: u < UNITS - 2
    s_in, s_out = [sem("s_in0"), sem("s_in1")], [sem("s_out0"), sem("s_out1")]
    parts_ready, mats_ready, y_init = sem("ssd_parts_ready"), sem("ssd_mats_ready"), sem("ssd_y_init")
    row_in = [sem("ssd_row_in0"), sem("ssd_row_in1")]
    dist_done, decay_done = sem("ssd_dist_done"), sem("ssd_decay_done")
    cb_full, cb_done, m_done = sem("ssd_cb_full"), sem("ssd_cb_done"), sem("ssd_m_done")
    xdt_done, xdec_done, sdec_done = sem("ssd_xdt_done"), sem("ssd_xdec_done"), sem("ssd_sdec_done")
    st_full, s_done = sem("ssd_st_full"), sem("ssd_s_done")
    off_full, off_done, diag_full, y_new = (sem("ssd_off_full"), sem("ssd_off_done"), sem("ssd_diag_full"),
                                            sem("ssd_y_new"))
    y_added, pool_go = sem("ssd_y_added"), sem("ssd_pool_go")
    with ExitStack() as ctx:
        sb = lambda n, shape: ctx.enter_context(nc.sbuf_tensor("ssd_" + n, shape, F32))
        pb = lambda n, shape: ctx.enter_context(nc.psum_tensor("ssd_" + n, shape, F32))
        part = {n: sb(n, [P, NCH, 2, HPG]) for n in DT_PARTS}
        ct, bt, bk = sb("ct", [P, T]), sb("bt", [P, T]), sb("bk", [P, NCH, M_STATE])
        row = sb("row", [P, 2, HPG * P])
        m = sb("m", [P, 2, HPG, P])
        cb = sb("cb", [P, 2, P])
        xdt, xdec, yn = sb("xdt", [P, 2, GI]), sb("xdec", [P, 2, GI]), sb("yn", [P, 2, GI])
        off, sdec = sb("off", [P, 2, GI]), sb("sdec", [P, GI])
        s_ctx, s_lat = sb("s_ctx", [P, 2, GI]), sb("s_lat", [P, 2, GI])
        p_cb, p_diag, p_off, p_st = (pb(n, [P, 2, 512]) for n in ("p_cb", "p_diag", "p_off", "p_st"))
        block = ctx.enter_context(nc.Block())
        heads = lambda a: a.rearrange("p (e f) -> p e f", f=HD)
        per_head = lambda n, u: part[n][:, chunk(u), u % 2, :].unsqueeze(2).to_broadcast([P, HPG, HD])
        ONE, TWO = 1, 2

        @block.sync
        def _(sp):
            for d in (0, 1):
                sp.dma_start(s_lat[:, d, :], io["ssm_in"][d, 0]).then_inc(s_in[d], 16)

            def rows(gi, us):
                for u in us:
                    sp.wait_ge(dist_done, UNITS * gi + u + 1)
                    src = io["cs_rows"][chunk(u), bass.ds(HPG * gi + M_HEADS * (u % 2), HPG), :]
                    sp.dma_start(row[:, u % 2, :], src.rearrange("e t -> (e t)").unsqueeze(0)
                                 .to_broadcast([P, HPG * P])).then_inc(row_in[u % 2], 16)

            def context_out(gi):
                for d in (0, 1):
                    sp.wait_ge(s_done, 8 * gi + d + 1 + TWO)
                    sp.dma_start(io["ssm_out"][d, bass.ds(gi, 1)].squeeze(0), s_ctx[:, d, :]).then_inc(s_out[d], 16)

            with sp.Fori(0, M_GROUPS - 1) as gi:
                rows(gi, range(0, 5))
                context_out(gi)
                rows(gi, range(5, UNITS))
                sp.wait_ge(off_full, 8 * gi + 8)
                for d in (0, 1):
                    sp.dma_start(s_lat[:, d, :], io["ssm_in"][d, bass.ds(gi + 1, 1)].squeeze(0)).then_inc(s_in[d], 16)
            rows(M_GROUPS - 1, range(0, 5))
            context_out(M_GROUPS - 1)
            rows(M_GROUPS - 1, range(5, UNITS))
            for d in (0, 1):
                sp.wait_ge(s_out[d], 16 * M_GROUPS + 16)

        @block.gpsimd
        def _(pool):
            pool.sem_inc(y_added, TWO)
            with pool.Fori(0, M_GROUPS) as gi:
                pool.wait_ge(diag_full, UNITS * gi + TWO)
                pool.wait_ge(y_new, UNITS * gi + TWO)
                for n in DT_PARTS:
                    src = dts[n][:, :, :].rearrange("p c (d q e) -> p c d q e", d=2, e=HPG)
                    for d in (0, 1):
                        last = pool.tensor_copy(part[n][:, :, d, :], src[:, :, d, bass.ds(gi, 1), :].squeeze(2))
                last.then_inc(parts_ready, 1)
                for c in range(NCH):
                    last = pool.tensor_tensor(
                        heads(y_tok[:, c, bass.ds(gi * GI, GI)]), heads(x_tok[:, c, bass.ds(gi * GI, GI)]),
                        g.r("d_skip")[:, bass.ds(gi * HPG, HPG)].unsqueeze(2).to_broadcast([P, HPG, HD]), ALU.mult)
                last.then_inc(y_init, 1)
                pool.wait_ge(parts_ready, gi + 1)

                def add_y(u):
                    n = UNITS * gi + u
                    pool.wait_ge(y_init, gi + 1)
                    pool.wait_ge(y_new, n + 1 + TWO)
                    pool.wait_ge(y_added, n + TWO)
                    pool.sem_inc(pool_go, 1)
                    y = y_tok[:, chunk(u), bass.ds(gi * GI, GI)]
                    pool.tensor_tensor(y, y, yn[:, u % 2, :], ALU.add).then_inc(y_added, 1)

                for u in range(UNITS):
                    n, d, i = UNITS * gi + u, u % 2, 8 * gi + u
                    pool.wait_ge(diag_full, n + 1)
                    pool.sem_inc(pool_go, 1)
                    x = heads(x_tok[:, chunk(u), bass.ds(gi * GI, GI)])
                    pool.tensor_tensor(heads(xdt[:, d, :]), x, per_head("dt", u), ALU.mult).then_inc(xdt_done, 1)
                    if makes_state(u):
                        pool.tensor_tensor(heads(xdec[:, d, :]), x, per_head("edec", u), ALU.mult).then_inc(xdec_done, 1)
                    if u >= 2:
                        add_y(u - 2)
                add_y(UNITS - 2)
                add_y(UNITS - 1)

        @block.scalar
        def _(act):
            act.sem_inc(dist_done, TWO)
            with act.Fori(0, M_GROUPS) as gi:
                act.wait_ge(diag_full, UNITS * gi + TWO)
                act.activation(ct[:, :], c_chan[:, bass.ds(gi, 1), :].squeeze(1), ACT.Copy)
                act.activation(bt[:, :], b_chan[:, bass.ds(gi, 1), :].squeeze(1), ACT.Copy)
                act.activation(bk[:, :, :], b_tok[:, :, bass.ds(gi * M_STATE, M_STATE)], ACT.Copy)\
                   .then_inc(mats_ready, 1)
                act.wait_ge(parts_ready, gi + 1)
                for u in range(UNITS):
                    n = UNITS * gi + u
                    act.wait_ge(row_in[u % 2], 16 * (UNITS // 2) * gi + 16 * (u // 2 + 1))
                    act.wait_ge(diag_full, n + 1)
                    for e in range(HPG):
                        last = act.activation(m[:, u % 2, e, :], row[:, u % 2, P * e:P * e + P], ACT.Relu, scale=-1.0,
                                              bias=part["cs"][:, chunk(u), u % 2, e:e + 1])
                    last.then_inc(dist_done, 1)
                    act.wait_ge(dist_done, n + 1 + TWO)
                    act.activation(m[:, u % 2, :, :], m[:, u % 2, :, :], ACT.Exp, scale=-1.0)\
                       .then_inc(decay_done, 1)

        @block.tensor
        def _(pe):
            pe.sem_inc(diag_full, TWO)
            with pe.Fori(0, M_GROUPS) as gi:
                pe.wait_ge(parts_ready, gi + 1)
                pe.wait_ge(mats_ready, gi + 1)

                def products(u):
                    span = slice(P * chunk(u), P * chunk(u) + P)
                    pe.wait_ge(cb_done, UNITS * gi + u + 1)
                    pe.matmul(p_cb[:, u % 2, 0:P], bt[:, span], ct[:, span], start=True, stop=True).then_inc(cb_full, 1)

                products(0)
                for u in range(UNITS):
                    n, d, i = UNITS * gi + u, u % 2, 8 * gi + u
                    span = slice(P * chunk(u), P * chunk(u) + P)
                    if u + 1 < UNITS:
                        products(u + 1)
                    if with_state(u):
                        if u < 4:
                            pe.wait_ge(s_in[d], 16 * gi + 16)
                        else:
                            pe.wait_ge(s_done, i - 1 + TWO)
                        pe.wait_ge(off_done, 8 * gi + u - 2 + 1)
                        pe.matmul(p_off[:, d, :], ct[:, span], s_lat[:, d, :], start=True, stop=True)\
                          .then_inc(off_full, 1)
                    if makes_state(u):
                        pe.wait_ge(xdec_done, i + 1)
                        pe.wait_ge(s_done, i + 1)
                        pe.matmul(p_st[:, d, :], bk[:, chunk(u), :], xdec[:, d, :], start=True, stop=True)\
                          .then_inc(st_full, 1)
                    pe.wait_ge(xdt_done, n + 1)
                    pe.wait_ge(m_done, n + 1)
                    pe.wait_ge(y_new, n + 1)
                    for e in range(HPG):
                        last = pe.matmul(p_diag[:, d, HD * e:HD * e + HD], m[:, d, e, :],
                                         xdt[:, d, HD * e:HD * e + HD], start=True, stop=True)
                    last.then_inc(diag_full, 1)

        @block.vector
        def _(dve):
            dve.sem_inc(cb_done, TWO)
            dve.sem_inc(off_done, TWO)
            dve.sem_inc(s_done, TWO)
            dve.sem_inc(y_new, TWO)
            for d in (0, 1):
                dve.sem_inc(s_out[d], 16)
            with dve.Fori(0, M_GROUPS) as gi:
                dve.wait_ge(parts_ready, gi + 1)

                def sum_up(u):
                    n, d = UNITS * gi + u, u % 2
                    dve.wait_ge(diag_full, n + 1 + TWO)
                    dve.wait_ge(y_added, n + 1)
                    if with_state(u):
                        dve.wait_ge(off_done, 8 * gi + u - 1 + TWO)
                        dve.tensor_tensor(yn[:, d, :], off[:, d, :], p_diag[:, d, :], ALU.add).then_inc(y_new, 1)
                    else:
                        dve.tensor_copy(yn[:, d, :], p_diag[:, d, :]).then_inc(y_new, 1)

                for u in range(UNITS):
                    n, d, i = UNITS * gi + u, u % 2, 8 * gi + u
                    dve.wait_ge(cb_full, n + 1)
                    dve.wait_ge(y_new, n + 1)
                    dve.tensor_tensor(cb[:, d, :], p_cb[:, d, 0:P], g.tri[:, d, :], ALU.mult).then_inc(cb_done, 1)
                    if makes_state(u) and with_state(u):
                        if u < 4:
                            dve.wait_ge(s_in[d], 16 * gi + 16)
                        dve.wait_ge(s_done, i + TWO)
                        dve.tensor_tensor(heads(sdec[:, :]), heads(s_lat[:, d, :]), per_head("etot", u),
                                          ALU.mult).then_inc(sdec_done, 1)
                    dve.wait_ge(cb_done, n + 1 + TWO)
                    dve.wait_ge(decay_done, n + 1)
                    dve.tensor_tensor(m[:, d, :, :], m[:, d, :, :],
                                      cb[:, d, :].unsqueeze(1).to_broadcast([P, HPG, P]), ALU.mult).then_inc(m_done, 1)
                    if with_state(u):
                        dve.wait_ge(off_full, 8 * gi + u - 1)
                        dve.wait_ge(y_new, n - 2 + TWO + 1)
                        dve.tensor_tensor(heads(off[:, d, :]), heads(p_off[:, d, :]), per_head("ecs", u),
                                          ALU.mult).then_inc(off_done, 1)
                    if makes_state(u):
                        dve.wait_ge(st_full, i + 1)
                        if with_state(u):
                            dve.wait_ge(sdec_done, 6 * gi + u - 1)
                            dve.tensor_tensor(s_lat[:, d, :], sdec[:, :], p_st[:, d, :], ALU.add).then_inc(s_done, 1)
                        else:
                            dve.wait_ge(s_out[d], 16 * gi + 16)
                            dve.tensor_copy(s_ctx[:, d, :], p_st[:, d, :]).then_inc(s_done, 1)
                    if u:
                        sum_up(u - 1)
                sum_up(UNITS - 1)


def phase_m_gate(nc, sem, io, g, y_tok, y_chan):
    w_in = [sem("z_w_in0"), sem("z_w_in1")]
    z_full, z_done, gated = sem("z_full"), sem("z_done"), sem("z_gated")
    sum_done, mean_done, root_done, inv_done = sem("z_sum_done"), sem("z_mean_done"), sem("z_root_done"), sem("z_inv")
    normed, tr_full, tr_done = sem("z_normed"), sem("z_tr_full"), sem("z_tr_done")
    SUB = GI // P
    with ExitStack() as ctx:
        sb = lambda n, shape: ctx.enter_context(nc.sbuf_tensor("z_" + n, shape, F32))
        w = sb("w", [P, 2, KD * GI])
        z, sq = sb("z", [P, 2, GI]), sb("sq", [P, GI])
        ms = sb("ms", [P, 2, 1])
        pz = ctx.enter_context(nc.psum_tensor("z_pz", [P, 2, 512], F32))
        pt = ctx.enter_context(nc.psum_tensor("z_pt", [P, 2, 512], F32))
        block = ctx.enter_context(nc.Block())
        units = [(q, c) for q in range(M_GROUPS) for c in range(NCH)]

        @block.sync
        def _(sp):
            for q in range(M_GROUPS):
                if q >= 2:
                    sp.wait_ge(z_full, NCH * (q - 1))
                sp.dma_start(w[:, q % 2, :], io["w_z"][q]).then_inc(w_in[q % 2], 16)

        @block.tensor
        def _(pe):
            def turn(n):
                q, c = units[n]
                pe.wait_ge(normed, n + 1)
                if n >= 2:
                    pe.wait_ge(tr_done, n - 1)
                for j in range(SUB):
                    at = GI * q + P * j
                    last = pe.transpose(pt[:, n % 2, P * j:P * j + P], y_tok[:, c, at:at + P], g.ident)
                last.then_inc(tr_full, 1)

            for n, (q, c) in enumerate(units):
                pe.wait_ge(w_in[q % 2], 16 * (q // 2 + 1))
                if n >= 2:
                    pe.wait_ge(z_done, n - 1)
                for k in range(KD):
                    last = pe.matmul(pz[:, n % 2, :], g.h[:, k, P * c:P * c + P],
                                     w[:, q % 2, GI * k:GI * k + GI], start=(k == 0), stop=(k == KD - 1))
                last.then_inc(z_full, 1)
                if n >= 1:
                    turn(n - 1)
            turn(len(units) - 1)

        @block.scalar
        def _(act):
            for n in range(len(units)):
                act.wait_ge(z_full, n + 1)
                if n >= 2:
                    act.wait_ge(gated, n - 1)
                act.activation(z[:, n % 2, :], pz[:, n % 2, :], ACT.Silu).then_inc(z_done, 1)
                act.wait_ge(inv_done, n + 1)
                act.activation(ms[:, n % 2, :], ms[:, n % 2, :], ACT.Sqrt).then_inc(root_done, 1)

        @block.vector
        def _(dve):
            for n, (q, c) in enumerate(units):
                y = y_tok[:, c, GI * q:GI * q + GI]
                dve.wait_ge(z_done, n + 1)
                dve.tensor_tensor(y, y, z[:, n % 2, :], ALU.mult).then_inc(gated, 1)
                dve.wait_ge(gated, n + 1)
                dve.tensor_tensor_reduce(out=sq[:, :], in0=y, in1=y, scale=1.0, scalar=0.0, op0=ALU.mult,
                                         op1=ALU.add, accum_out=ms[:, n % 2, :]).then_inc(sum_done, 1)
                dve.wait_ge(sum_done, n + 1)
                dve.tensor_scalar(ms[:, n % 2, :], ms[:, n % 2, :], 1.0 / GI, 1e-5, ALU.mult, ALU.add)\
                   .then_inc(mean_done, 1)
                dve.wait_ge(mean_done, n + 1)
                dve.reciprocal(ms[:, n % 2, :], ms[:, n % 2, :]).then_inc(inv_done, 1)
                dve.wait_ge(root_done, n + 1)
                dve.tensor_scalar(y, y, ms[:, n % 2, :], None, ALU.mult).then_inc(normed, 1)
                dve.wait_ge(tr_full, n + 1)
                dve.tensor_tensor(y_chan[:, SUB * q:SUB * q + SUB, P * c:P * c + P],
                                  pt[:, n % 2, :].rearrange("p (j t) -> p j t", t=P),
                                  g.v("m_norm")[:, SUB * q:SUB * q + SUB].unsqueeze(2).to_broadcast([P, SUB, P]),
                                  ALU.mult).then_inc(tr_done, 1)


def phase_m_out(nc, sem, io, g, y):
    w_in = [sem("m_w_in0"), sem("m_w_in1")]
    out_full, gate_full, gate_done, done = sem("m_out_full"), sem("m_gate_full"), sem("m_gate_done"), sem("m_done")
    KW = KI + KD
    with ExitStack() as ctx:
        w = ctx.enter_context(nc.sbuf_tensor("m_w", [P, 2, KW * P], F32))
        gate = ctx.enter_context(nc.sbuf_tensor("m_gate", [P, 2, T], F32))
        po = ctx.enter_context(nc.psum_tensor("m_po", [P, 2, 1024], F32))
        pg = ctx.enter_context(nc.psum_tensor("m_pg", [P, 2, 1024], F32))
        block = ctx.enter_context(nc.Block())

        @block.sync
        def _(sp):
            stream(sp, KD, lambda it, s: sp.dma_start(w[:, s, :], io["w_m"][2 * it + s]).then_inc(w_in[s], 16),
                   used=out_full)

        @block.tensor
        def _(pe):
            with pe.Fori(0, KD // 2) as it:
                for s in (0, 1):
                    n = 2 * it + s
                    wt = tiles_of(w[:, s, :])
                    pe.wait_ge(w_in[s], 16 * it + 16)
                    pe.wait_ge(gate_done, n + 1)
                    project_halves(pe, pg[:, s, :], wt[:, KI:, :], g.h, KD).then_inc(gate_full, 1)
                    pe.wait_ge(done, n + 1)
                    project_halves(pe, po[:, s, :], wt[:, :KI, :], y, KI).then_inc(out_full, 1)

        @block.scalar
        def _(act):
            act.sem_inc(gate_done, 2)
            with act.Fori(0, KD // 2) as it:
                for s in (0, 1):
                    n = 2 * it + s
                    act.wait_ge(gate_full, n + 1)
                    act.wait_ge(done, n + 1)
                    act.activation(by_half(gate[:, s, :]), halves(pg[:, s, :]), ACT.Sigmoid).then_inc(gate_done, 1)

        @block.vector
        def _(dve):
            dve.sem_inc(done, 2)
            with dve.Fori(0, KD // 2) as it:
                for s in (0, 1):
                    n = 2 * it + s
                    dve.wait_ge(gate_done, n + 3)
                    dve.wait_ge(out_full, n + 1)
                    mix = g.mix[:, bass.ds(n, 1), :].squeeze(1)
                    dve.tensor_tensor(by_half(mix), by_half(gate[:, s, :]), halves(po[:, s, :]), ALU.mult)\
                       .then_inc(done, 1)


def phase_r_out(nc, sem, io, g, y, mix):
    gate_in = [sem("r_gate_in0"), sem("r_gate_in1")]
    full, done, scaled, rounded = sem("r_full"), sem("r_done"), sem("r_scaled"), sem("r_rounded")
    x_in = sem("r_x_in")
    with ExitStack() as ctx:
        raw = ctx.enter_context(nc.sbuf_tensor("r_raw", [P, 2, KD * P], F32))
        weights = SplitWeights(nc, sem, ctx, "r", KD, KD * P, lambda n: io["w_r"][n], raw, full)
        gate = g.h
        ps = ctx.enter_context(nc.psum_tensor("r_ps", [P, 2, 1024], F32))
        block = ctx.enter_context(nc.Block())

        @block.sync
        def _(sp):
            for k in (0, 1):
                half = slice(KD // 2 * k, KD // 2 * (k + 1))
                sp.dma_start(gate[:, half, :], io["gate_r"][half].rearrange("k p t -> p k t")).then_inc(gate_in[k], 16)
            weights.load_all(sp)
            sp.dma_start(g.x[:, :, :], io["x_t"].rearrange("k p t -> p k t")).then_inc(x_in, 16)
            sp.wait_ge(x_in, 16)

        @block.gpsimd
        def _(pool):
            weights.low_all(pool)

        @block.scalar
        def _(act):
            for s in (0, 1):
                weights.round_tile(act, 0, s)
            for n in range(KD):
                act.wait_ge(full, n + 1)
                if n + 2 < KD:
                    weights.round_tile(act, n // 2 + 1, n % 2)
                act.wait_ge(done, n + 1)
                act.activation(mix[0][:, n, :], g.mix[:, n, :], ACT.Copy).then_inc(rounded, 1)

        @block.tensor
        def _(pe):
            for n in range(KD):
                parts = weights.tile(pe, n // 2, n % 2)
                if n >= 2:
                    pe.wait_ge(scaled, n - 1)
                project_split(pe, ps[:, n % 2, :], parts, y, KD).then_inc(full, 1)

        @block.vector
        def _(dve):
            for k in (0, 1):
                dve.wait_ge(gate_in[k], 16)
            for n in range(KD):
                dve.wait_ge(full, n + 1)
                dve.tensor_tensor(by_half(gate[:, n, :]), by_half(gate[:, n, :]), halves(ps[:, n % 2, :]),
                                  ALU.mult).then_inc(scaled, 1)
                dve.wait_ge(scaled, n + 1)
                dve.tensor_tensor(g.mix[:, n, :], g.mix[:, n, :], gate[:, n, :], ALU.add).then_inc(done, 1)
                dve.wait_ge(rounded, n + 1)
                dve.tensor_tensor(mix[1][:, n, :], g.mix[:, n, :], mix[0][:, n, :].bitcast(F32), ALU.subtract)


def phase_residual(nc, sem, g, tag, source, raw, rhs, k_tiles, gate_at):
    full, done = sem(tag + "_full"), sem(tag + "_done")
    with ExitStack() as ctx:
        weights = SplitWeights(nc, sem, ctx, tag, KD, k_tiles * P, source, raw, full)
        ps = ctx.enter_context(nc.psum_tensor(tag + "_ps", [P, 2, 1024], F32))
        block = ctx.enter_context(nc.Block())

        @block.sync
        def _(sp):
            weights.load_all(sp)

        @block.gpsimd
        def _(pool):
            weights.low_all(pool)

        @block.scalar
        def _(act):
            weights.rounding(act, lambda it, s: act.wait_ge(full, 2 * it + s + 1))

        @block.tensor
        def _(pe):
            with pe.Fori(0, KD // 2) as it:
                for s in (0, 1):
                    parts = weights.tile(pe, it, s)
                    pe.wait_ge(done, 2 * it + s + 1)
                    project_split(pe, ps[:, s, :], parts, rhs, k_tiles).then_inc(full, 1)

        @block.vector
        def _(dve):
            dve.sem_inc(done, 2)
            with dve.Fori(0, KD // 2) as it:
                for s in (0, 1):
                    dve.wait_ge(full, 2 * it + s + 1)
                    for c, b, lo, hi in PIECES:
                        x = g.x[:, bass.ds(2 * it + s, 1), lo:hi].squeeze(1)
                        last = dve.scalar_tensor_tensor(
                            out=x, in0=halves(ps[:, s, :])[:, b, lo - HALF * b:hi - HALF * b], in1=x,
                            op0=ALU.mult, op1=ALU.add, scalar=g.mod[:, bass.ds(2 * it + s + gate_at, 1), c])
                    last.then_inc(done, 1)


def phase_up(nc, sem, io, g, tag, first, tiles, h, spare, raw, hidden):
    full, silu_done, done = [sem(tag + "_g_full"), sem(tag + "_u_full")], sem(tag + "_silu_done"), sem(tag + "_done")
    rounded = sem(tag + "_rounded")
    silu, plain = spare
    with ExitStack() as ctx:
        weights = SplitWeights(nc, sem, ctx, tag, 2 * tiles, KD * P, lambda n: io["w_gu"][n + 2 * first], raw, None)
        ps = ctx.enter_context(nc.psum_tensor(tag + "_ps", [P, 2, 2, 1024], F32))
        block = ctx.enter_context(nc.Block())

        @block.sync
        def _(sp):
            weights.load_all(sp)

        @block.gpsimd
        def _(pool):
            weights.low_all(pool)

        @block.tensor
        def _(pe):
            for n in range(tiles):
                for s, free in ((0, silu_done), (1, done)):
                    parts = weights.tile(pe, n, s)
                    if n >= 2:
                        pe.wait_ge(free, n - 1)
                    project_split(pe, ps[:, s, n % 2, :], parts, h, KD).then_inc(full[s], 1)

        @block.scalar
        def _(act):
            for s in (0, 1):
                weights.round_tile(act, 0, s)
            for n in range(tiles):
                act.wait_ge(full[0], n + 1)
                if n + 1 < tiles:
                    weights.round_tile(act, n + 1, 0)
                if n >= 2:
                    act.wait_ge(done, n - 1)
                act.activation(by_half(silu[:, n % 2, :]), halves(ps[:, 0, n % 2, :]), ACT.Silu)\
                   .then_inc(silu_done, 1)
                act.wait_ge(full[1], n + 1)
                if n + 1 < tiles:
                    weights.round_tile(act, n + 1, 1)
                act.wait_ge(done, n + 1)
                act.activation(hidden[0][:, n, :], plain[:, n % 2, :], ACT.Copy).then_inc(rounded, 1)

        @block.vector
        def _(dve):
            for n in range(tiles):
                dve.wait_ge(silu_done, n + 1)
                dve.wait_ge(full[1], n + 1)
                dve.tensor_tensor(by_half(plain[:, n % 2, :]), by_half(silu[:, n % 2, :]),
                                  halves(ps[:, 1, n % 2, :]), ALU.mult).then_inc(done, 1)
                dve.wait_ge(rounded, n + 1)
                dve.tensor_tensor(hidden[1][:, n, :], plain[:, n % 2, :], hidden[0][:, n, :].bitcast(F32),
                                  ALU.subtract)


def phase_store(nc, sem, io, g):
    stored = sem("stored")
    with nc.Block() as block:
        @block.sync
        def _(sp):
            sp.dma_start(io["y"].rearrange("k p t -> p k t"), g.h[:, :, :]).then_inc(stored, 16)
            sp.wait_ge(stored, 16)


def phase_load_x(nc, sem, io, g):
    x_in = sem("x_again")
    with nc.Block() as block:
        @block.sync
        def _(sp):
            sp.dma_start(g.x[:, :, :], io["x_t"].rearrange("k p t -> p k t")).then_inc(x_in, 16)
            sp.wait_ge(x_in, 16)


R_TILES, W_TILE, K_TILES, V_TILES, A_TILE, G_TILE = range(0, 8), 8, range(9, 17), range(17, 25), 25, 26


def quarters_of(tiles):
    return sorted({ch // QUARTER for m in tiles for ch in (P * m, P * m + P - 1)})


def shifted_views(q, dst, src):
    before = q % 2 == 0
    far, near = slice(1, CTX), slice(0, CTX - 1)
    context = (dst[:, far], src[:, near]) if before else (dst[:, near], src[:, far])
    if q < 2:
        grid = lambda a: a[:, CTX:T].rearrange("p (r w) -> p r w", w=GRID_W)
        far, near = slice(1, GRID_W), slice(0, GRID_W - 1)
        latent = (grid(dst)[:, :, far], grid(src)[:, :, near]) if before else \
                 (grid(dst)[:, :, near], grid(src)[:, :, far])
    else:
        far, near = slice(CTX + GRID_W, T), slice(CTX, T - GRID_W)
        latent = (dst[:, far], src[:, near]) if before else (dst[:, near], src[:, far])
    return context, latent


def phase_low(nc, sem, io, g, low):
    w_in = [sem(f"low_w_in{m}") for m in range(3)]
    full, own, mixed, ready = sem("low_full"), sem("low_own"), sem("low_mixed"), sem("low_ready")
    tiles = (W_TILE, A_TILE, G_TILE)
    with ExitStack() as ctx:
        w = ctx.enter_context(nc.sbuf_tensor("low_w", [P, 3, KD * P], F32))
        ps = ctx.enter_context(nc.psum_tensor("low_ps", [P, 3, 1024], F32))
        block = ctx.enter_context(nc.Block())

        @block.sync
        def _(sp):
            for m in range(3):
                sp.dma_start(w[:, m, :], io["w_low"][m]).then_inc(w_in[m], 16)

        @block.tensor
        def _(pe):
            for m in range(3):
                pe.wait_ge(w_in[m], 16)
                project(pe, ps[:, m, :], tiles_of(w[:, m, :]), g.h, KD).then_inc(full, 1)

        @block.scalar
        def _(act):
            for m, tile in enumerate(tiles):
                act.wait_ge(full, m + 1)
                act.activation(low[:, m, :], ps[:, m, 0:T], ACT.Copy,
                               scale=g.mu_own[:, tile:tile + 1]).then_inc(own, 1)
            act.wait_ge(mixed, 1)
            act.activation(low[:, 0, :], low[:, 0, :], ACT.Tanh)
            act.wait_ge(mixed, 3)
            act.activation(low[:, 2, :], low[:, 2, :], ACT.Sigmoid)

        @block.vector
        def _(dve):
            for m, tile in enumerate(tiles):
                dve.wait_ge(own, m + 1)
                (q,) = quarters_of([tile])
                for dst, src in shifted_views(q, low[:, m, :], ps[:, m, 0:T]):
                    last = dve.scalar_tensor_tensor(out=dst, in0=src, scalar=g.mu_q[:, tile, q:q + 1],
                                                    in1=dst, op0=ALU.mult, op1=ALU.add)
                last.then_inc(mixed, 1)


A_HAT, R_HAT, B_HAT, K_HAT = range(4)


def phase_rwkv_in(nc, sem, io, g, low, bonus, carry):
    w_in = [sem("rw_w_in0"), sem("rw_w_in1")]
    a_full, a_done = [sem("rw_a_full0"), sem("rw_a_full1")], [sem("rw_a_done0"), sem("rw_a_done1")]
    b_full, b_done = [sem("rw_b_full0"), sem("rw_b_full1")], [sem("rw_b_done0"), sem("rw_b_done1")]
    own, half_mixed = sem("rw_own"), sem("rw_half_mixed")
    sq_done, inv_chain, root_done, kk_done = (sem("rw_sq_done"), sem("rw_inv_chain"), sem("rw_root_done"),
                                              sem("rw_kk_done"))
    cum_done, before_done, g_done, ginv_done, gbef_done = (sem("rw_cum_done"), sem("rw_before_done"),
                                                           sem("rw_g_done"), sem("rw_ginv_done"),
                                                           sem("rw_gbef_done"))
    rate_done, kd_done, kd_sum, kk_a, rk_done = (sem("rw_rate_done"), sem("rw_kd_done"), sem("rw_kd_sum"),
                                                 sem("rw_kk_a"), sem("rw_rk_done"))
    ahat, rhat, bhat, khat = sem("rw_ahat"), sem("rw_rhat"), sem("rw_bhat"), sem("rw_khat")
    turned = sem("rw_turned")
    chan_out, tok_out = sem("rw_chan_out"), sem("rw_tok_out")
    vec_tile, pool_tile = sem("rw_vec_tile"), sem("rw_pool_tile")
    roles = (R_TILES, K_TILES, V_TILES)
    TURNS = ((0, B_HAT), (0, K_HAT), (1, B_HAT), (1, K_HAT), None)
    A_USES, B_USES = 3, 6 + len(TURNS)
    TWO = 2

    def a_use(it, s, x):
        return (A_USES * s + x) % 2, A_USES * it + (A_USES * s + x) // 2

    def b_use(it, s, x):
        return (B_USES * s + x) % 2, B_USES * it + (B_USES * s + x) // 2

    with ExitStack() as ctx:
        sb = lambda n, shape: ctx.enter_context(nc.sbuf_tensor("rw_" + n, shape, F32))
        KW = 3 * KD + 2
        w = sb("w", [P, 2, KW * P])
        rkv = sb("rkv", [P, 2, 3, T])
        dec, rate = sb("dec", [P, 2, T]), sb("rate", [P, 2, T])
        cum, gg = sb("cum", [P, 2, T]), sb("gg", [P, 2, T])
        kd = sb("kd", [P, 2, T])
        kk, inv, kds = sb("kk", [P, T]), sb("inv", [P, T]), sb("kds", [P, T])
        hat = sb("hat", [P, 2, 4, T])
        tb = sb("tb", [P, len(TURNS), T])
        pa = ctx.enter_context(nc.psum_tensor("rw_pa", [P, 2, 1024], F32))
        pb = ctx.enter_context(nc.psum_tensor("rw_pb", [P, 2, 1024], F32))
        block = ctx.enter_context(nc.Block())
        one = lambda base, n: bass.ds(n + base, 1)

        @block.sync
        def _(sp):
            def load(it, s):
                sp.dma_start(w[:, s, :], io["w_rkv"][2 * it + s]).then_inc(w_in[s], 16)

            def store(it, s):
                n = 2 * it + s
                chan = io["chan"].rearrange("d c p (q j t) -> d q j p c t", q=4, j=PAIRS)
                for d in (0, 1):
                    for q, made in ((A_HAT, ahat), (R_HAT, rhat), (B_HAT, bhat), (K_HAT, khat)):
                        sp.wait_ge(made, 2 * n + d + 1)
                        sp.dma_start(chan[d, q, bass.ds(n, 1)].squeeze(0),
                                     hat[:, d, q, :].rearrange("p (c t) -> p c t", t=WC)).then_inc(chan_out, 16)
                tok = io["tok"].rearrange("d (c p) (q j m) -> d q j p c m", p=P, q=2, m=P)
                val = io["val"].rearrange("(c p) (j m) -> j p c m", p=P, m=P)
                for x, turn in enumerate(TURNS):
                    sp.wait_ge(turned, len(TURNS) * n + x + 1)
                    dst = val[bass.ds(n, 1)] if turn is None else tok[turn[0], turn[1] - B_HAT, bass.ds(n, 1)]
                    sp.dma_start(dst.squeeze(0), tb[:, x, :].rearrange("p (c m) -> p c m", m=P)).then_inc(tok_out, 16)

            load(0, 0)
            load(0, 1)
            with sp.Fori(0, PAIRS // 2 - 1) as it:
                for s in (0, 1):
                    store(it, s)
                    load(it + 1, s)
            for s in (0, 1):
                store(PAIRS // 2 - 1, s)
            sp.wait_ge(chan_out, 16 * 8 * (PAIRS + 1))
            sp.wait_ge(tok_out, 16 * len(TURNS) * (PAIRS + 1))

        @block.tensor
        def _(pe):
            def proj(it, s, x):
                slot, before = a_use(it, s, x)
                if x == 0:
                    pe.wait_ge(w_in[s], 16 * it + 16)
                pe.wait_ge(a_done[slot], before + 1)
                wt = tiles_of(w[:, s, :])
                project(pe, pa[:, slot, :], wt[:, KD * x:KD * x + KD, :], g.h, KD).then_inc(a_full[slot], 1)

            def small(it, s, x, lhs, rhs, ready=None):
                slot, before = b_use(it, s, x)
                if ready is not None:
                    pe.wait_ge(*ready)
                pe.wait_ge(b_done[slot], before + 1)
                for lo, hi in BANKS:
                    last = pe.matmul(pb[:, slot, lo:hi], lhs, rhs[:, lo:hi], start=True, stop=True)
                last.then_inc(b_full[slot], 1)

            def finish(it, s, ahead):
                n = 2 * it + s
                wt = tiles_of(w[:, s, :])
                proj(it, s, 2)
                for x, tile in ((0, 0), (2, 1)):
                    for d in (0, 1):
                        rows = slice(64 * d, 64 * d + 64)
                        small(it, s, x + d, wt[rows, 3 * KD + tile, :], low[rows, tile, :])
                if ahead is not None:
                    proj(*ahead, 0)
                small(it, s, 4, g.head_ones, inv, (sq_done, n + 1))
                if ahead is not None:
                    proj(*ahead, 1)
                small(it, s, 5, g.head_ones, kds, (rk_done, n + 1))
                for x, turn in enumerate(TURNS):
                    slot, before = b_use(it, s, 6 + x)
                    if turn is None:
                        src = rkv[:, s, 2, :]
                    else:
                        src = hat[:, turn[0], turn[1], :]
                        pe.wait_ge(bhat if turn[1] == B_HAT else khat, 2 * n + turn[0] + 1)
                    pe.wait_ge(b_done[slot], before + 1)
                    for c in range(NCH):
                        last = pe.transpose(pb[:, slot, P * c:P * c + P], src[:, P * c:P * c + P], g.ident)
                    last.then_inc(b_full[slot], 1)

            proj(0, 0, 0)
            proj(0, 0, 1)
            with pe.Fori(0, PAIRS // 2 - 1) as it:
                finish(it, 0, (it, 1))
                finish(it, 1, (it + 1, 0))
            finish(PAIRS // 2 - 1, 0, (PAIRS // 2 - 1, 1))
            finish(PAIRS // 2 - 1, 1, None)

        def mixed(eng, it, s, x):
            slot, before = a_use(it, s, x)
            eng.wait_ge(a_done[slot], before + 2)

        @block.scalar
        def _(act):
            def take(it, s, xs):
                n = 2 * it + s
                if 0 in xs:
                    act.wait_ge(vec_tile, n + 1)
                    act.wait_ge(pool_tile, n + 1)
                for x in xs:
                    slot, before = a_use(it, s, x)
                    act.wait_ge(a_full[slot], before + 1)
                    act.activation(rkv[:, s, x, :], pa[:, slot, 0:T], ACT.Copy,
                                   scale=g.mu_own[:, one(roles[x][0], n)]).then_inc(own, 1)

            def tile(it, s, ahead):
                n = 2 * it + s
                take(it, s, (2,))
                act.wait_ge(vec_tile, n + 2)
                act.wait_ge(pool_tile, n + 2)
                act.wait_ge(chan_out, 16 * 8 * n + 16 * 8)
                for x, bias, dst in ((0, "w0", dec), (2, "a0", rate)):
                    for d in (0, 1):
                        slot, before = b_use(it, s, x + d)
                        act.wait_ge(b_full[slot], before + 1)
                        act.activation(dst[:, d, :], pb[:, slot, 0:T], ACT.Sigmoid,
                                       bias=g.v(bias)[:, one(KD * d, n)]).then_inc(b_done[slot], 1)
                mixed(act, it, s, 1)
                act.activation(inv[:, :], rkv[:, s, 1, :], ACT.Square,
                               scale=g.v("k_k")[:, one(0, n)]).then_inc(sq_done, 1)
                for d in (0, 1):
                    act.wait_ge(before_done, 2 * n + d + 1)
                    act.activation(gg[:, d, :], cum[:, d, :], ACT.Exp, scale=-LOG_DECAY).then_inc(g_done, 1)
                    act.activation(dec[:, d, :], dec[:, d, :], ACT.Exp, scale=-LOG_DECAY).then_inc(gbef_done, 1)
                    act.activation(cum[:, d, :], cum[:, d, :], ACT.Exp, scale=LOG_DECAY).then_inc(ginv_done, 1)
                act.wait_ge(inv_chain, 2 * n + 2)
                act.activation(inv[:, :], inv[:, :], ACT.Sqrt).then_inc(root_done, 1)
                for d in (0, 1):
                    end = WC - 1 if d == 0 else 0
                    act.wait_ge(g_done, 2 * n + d + 1)
                    act.activation(carry[:, d, :, one(0, n)].squeeze(2), gg[:, d, end:T:WC], ACT.Copy)
                if ahead is not None:
                    take(*ahead, (0, 1))
                act.wait_ge(tok_out, 16 * len(TURNS) * n + 16 * len(TURNS))
                for x in range(len(TURNS)):
                    slot, before = b_use(it, s, 6 + x)
                    act.wait_ge(b_full[slot], before + 1)
                    act.activation(tb[:, x, :], pb[:, slot, 0:T], ACT.Copy).then_inc(turned, 1)
                    act.wait_ge(turned, len(TURNS) * n + x + 1)
                    act.sem_inc(b_done[slot], 1)

            take(0, 0, (0, 1))
            with act.Fori(0, PAIRS // 2 - 1) as it:
                tile(it, 0, (it, 1))
                tile(it, 1, (it + 1, 0))
            tile(PAIRS // 2 - 1, 0, (PAIRS // 2 - 1, 1))
            tile(PAIRS // 2 - 1, 1, None)

        @block.gpsimd
        def _(pool):
            pool.sem_inc(pool_tile, TWO)
            with pool.Fori(0, PAIRS // 2) as it:
                for s in (0, 1):
                    n = 2 * it + s
                    r, k = rkv[:, s, 0, :], rkv[:, s, 1, :]
                    for d in (0, 1):
                        pool.wait_ge(cum_done, 2 * n + d + 1)
                        pool.tensor_tensor(dec[:, d, :], cum[:, d, :], dec[:, d, :], ALU.subtract)\
                            .then_inc(before_done, 1)
                    for d in (0, 1):
                        pool.wait_ge(rate_done, 2 * n + d + 1)
                        if d == 0:
                            mixed(pool, it, s, 1)
                        pool.tensor_tensor(kd[:, d, :], kd[:, d, :], k, ALU.mult).then_inc(kd_done, 1)
                    pool.wait_ge(kd_done, 2 * n + 2)
                    pool.wait_ge(vec_tile, n + 2)
                    pool.tensor_tensor(kds[:, :], kd[:, 0, :], kd[:, 1, :], ALU.add).then_inc(kd_sum, 1)
                    for d in (0, 1):
                        pool.wait_ge(kk_done, n + 1)
                        pool.tensor_tensor(rate[:, d, :], rate[:, d, :], kk[:, :], ALU.mult).then_inc(kk_a, 1)
                    mixed(pool, it, s, 0)
                    for d in (0, 1):
                        pool.wait_ge(g_done, 2 * n + d + 1)
                        pool.tensor_tensor(hat[:, d, R_HAT, :], gg[:, d, :], r, ALU.mult).then_inc(rhat, 1)
                    pool.wait_ge(rhat, 2 * n + 2)
                    pool.sem_inc(pool_tile, 1)

        @block.vector
        def _(dve):
            dve.sem_inc(vec_tile, TWO)
            dve.sem_inc(a_done[0], 1)
            dve.sem_inc(a_done[1], 1)
            dve.sem_inc(b_done[0], 1)
            dve.sem_inc(b_done[1], 1)
            dve.sem_inc(chan_out, 16 * 8)
            dve.sem_inc(tok_out, 16 * len(TURNS))
            with dve.Fori(0, PAIRS // 2) as it:
                for s in (0, 1):
                    n = 2 * it + s
                    r, k, v = (rkv[:, s, x, :] for x in range(3))
                    for x, role in enumerate(roles):
                        slot, before = a_use(it, s, x)
                        dve.wait_ge(own, 3 * n + x + 1)
                        qa, qb = quarters_of(role)
                        for q in (qa, qb):
                            for dst, src in shifted_views(q, rkv[:, s, x, :], pa[:, slot, 0:T]):
                                last = dve.scalar_tensor_tensor(
                                    out=dst, in0=src, scalar=g.mu_q[:, one(role[0], n), q], in1=dst,
                                    op0=ALU.mult, op1=ALU.add)
                            if q == qa:
                                last.then_inc(half_mixed, 1)
                                dve.wait_ge(half_mixed, 3 * n + x + 1)
                        last.then_inc(a_done[slot], 1)
                    for d in (0, 1):
                        slot, before = b_use(it, s, d)
                        dve.wait_ge(b_done[slot], before + 2)
                        flow = (lambda a: a) if d == 0 else (lambda a: a[:, ::-1])
                        dve.tensor_tensor_scan(flow(cum[:, d, :]), flow(g.reset[:, d, :]), flow(dec[:, d, :]),
                                               0.0, ALU.mult, ALU.add).then_inc(cum_done, 1)
                    for d in (0, 1):
                        slot, before = b_use(it, s, 2 + d)
                        dve.wait_ge(b_done[slot], before + 2)
                        dve.tensor_scalar(kd[:, d, :], rate[:, d, :], g.v("k_a")[:, one(0, n)],
                                          g.k_a_c[:, one(0, n)], ALU.mult, ALU.add).then_inc(rate_done, 1)
                    slot, before = b_use(it, s, 4)
                    dve.wait_ge(b_full[slot], before + 1)
                    dve.tensor_scalar(inv[:, :], pb[:, slot, 0:T], 1e-12, None, ALU.add).then_inc(inv_chain, 1)
                    dve.wait_ge(inv_chain, 2 * n + 1)
                    dve.sem_inc(b_done[slot], 1)
                    dve.reciprocal(inv[:, :], inv[:, :]).then_inc(inv_chain, 1)
                    mixed(dve, it, s, 0)
                    dve.wait_ge(kd_sum, n + 1)
                    dve.scalar_tensor_tensor(out=kds[:, :], in0=r, scalar=g.v("r_k")[:, one(0, n)], in1=kds[:, :],
                                             op0=ALU.mult, op1=ALU.mult).then_inc(rk_done, 1)
                    dve.wait_ge(root_done, n + 1)
                    dve.scalar_tensor_tensor(out=kk[:, :], in0=k, scalar=g.v("k_k")[:, one(0, n)], in1=inv[:, :],
                                             op0=ALU.mult, op1=ALU.mult).then_inc(kk_done, 1)
                    for d in (0, 1):
                        dve.wait_ge(ginv_done, 2 * n + d + 1)
                        dve.tensor_tensor(hat[:, d, K_HAT, :], kd[:, d, :], cum[:, d, :], ALU.mult).then_inc(khat, 1)
                    dve.wait_ge(kk_done, n + 1)
                    for d in (0, 1):
                        dve.wait_ge(gbef_done, 2 * n + d + 1)
                        dve.scalar_tensor_tensor(out=hat[:, d, A_HAT, :], in0=kk[:, :], scalar=-1.0,
                                                 in1=dec[:, d, :], op0=ALU.mult, op1=ALU.mult).then_inc(ahat, 1)
                    for d in (0, 1):
                        dve.wait_ge(kk_a, 2 * n + d + 1)
                        dve.tensor_tensor(hat[:, d, B_HAT, :], rate[:, d, :], cum[:, d, :], ALU.mult).then_inc(bhat, 1)
                    slot, before = b_use(it, s, 5)
                    dve.wait_ge(b_full[slot], before + 1)
                    mixed(dve, it, s, 2)
                    dve.scalar_tensor_tensor(out=bonus[:, one(0, n), :].squeeze(1), in0=pb[:, slot, 0:T],
                                             scalar=0.5, in1=v, op0=ALU.mult, op1=ALU.mult)\
                       .then_inc(b_done[slot], 1)
                    dve.wait_ge(b_done[slot], before + 2)
                    dve.sem_inc(vec_tile, 1)


def phase_blocks(nc, sem, io):
    loaded = [sem("bl_in0"), sem("bl_in1")]
    full, copied = [sem("bl_full0"), sem("bl_full1")], [sem("bl_copied0"), sem("bl_copied1")]
    out = [sem("bl_out0"), sem("bl_out1")]
    go, sp_go = sem("bl_pe_go"), sem("bl_sp_go")
    with ExitStack() as ctx:
        ab = ctx.enter_context(nc.sbuf_tensor("bl_ab", [P, 2, 2, 2, PAIRS, WC], F32))
        m = ctx.enter_context(nc.sbuf_tensor("bl_m", [P, 2, 2, PAIRS, WC], F32))
        ps = ctx.enter_context(nc.psum_tensor("bl_ps", [P, 2, 2, 512], F32))
        block = ctx.enter_context(nc.Block())

        @block.sync
        def _(sp):
            def load(it, s):
                for d in (0, 1):
                    src = io["chan"][d, bass.ds(2 * it + s, 1)].squeeze(0).rearrange("p (q f) -> p q f", q=4)
                    sp.dma_start(ab[:, s, d, :, :, :].rearrange("p q j t -> p q (j t)"),
                                 src[:, A_HAT:B_HAT + 1:B_HAT, :]).then_inc(loaded[s], 16)

            def store(it, s):
                for d in (0, 1):
                    sp.wait_ge(copied[d], 2 * it + s + 2 + 1)
                sp.sem_inc(sp_go, 1)
                dst = io["blk_m"][bass.ds(2 * it + s, 1)].squeeze(0)
                for hb in range(4):
                    rows, cols = slice(QB * hb, QB * hb + QB), slice(QB * (hb % 2), QB * (hb % 2) + QB)
                    sp.dma_start(dst[hb].rearrange("d j (r c) -> r (d j) c", c=QB),
                                 m[rows, s, :, :, cols].rearrange("r d j c -> r (d j) c")).then_inc(out[s], 16)

            load(0, 0)
            load(0, 1)
            with sp.Fori(0, NWC // 2 - 1) as it:
                for s in (0, 1):
                    store(it, s)
                    load(it + 1, s)
            for s in (0, 1):
                store(NWC // 2 - 1, s)
            for s in (0, 1):
                sp.wait_ge(out[s], 16 * 4 * (NWC // 2 + 1))

        @block.tensor
        def _(pe):
            with pe.Fori(0, NWC // 2) as it:
                for s in (0, 1):
                    pe.wait_ge(loaded[s], 32 * it + 32)
                    for d in (0, 1):
                        pe.wait_ge(copied[d], 2 * it + s + 1)
                        pe.sem_inc(go, 1)
                        for j in range(PAIRS):
                            for rows in (slice(0, 64), slice(64, 128)):
                                last = pe.matmul(ps[rows, s, d, WC * j:WC * j + WC], ab[rows, s, d, 1 - d, j, :],
                                                 ab[rows, s, d, d, j, :], start=True, stop=True)
                        last.then_inc(full[d], 1)

        def copy(eng, d, instruction):
            for s in (0, 1):
                eng.sem_inc(out[s], 16 * 2)
            eng.sem_inc(copied[d], 2)
            with eng.Fori(0, NWC // 2) as it:
                for s in (0, 1):
                    eng.wait_ge(full[d], 2 * it + s + 1)
                    eng.wait_ge(out[s], 16 * 4 * it + 16 * 4)
                    instruction(m[:, s, d, :, :], ps[:, s, d, :].rearrange("p (j w) -> p j w", w=WC))\
                        .then_inc(copied[d], 1)

        @block.scalar
        def _(act):
            copy(act, 0, lambda o, i: nc.scalar.activation(o, i, ACT.Copy))

        @block.vector
        def _(dve):
            copy(dve, 1, lambda o, i: nc.vector.tensor_copy(o, i))


def phase_solve(nc, sem, io, g):
    w_in, w_used = [sem("so_w_in0"), sem("so_w_in1")], sem("so_w_used")
    gate_done, gate_out = sem("so_gate_done"), [sem("so_gate_out0"), sem("so_gate_out1")]
    u_in, w_out = sem("so_u_in"), sem("so_w_out")
    prepared, zeroed = sem("so_prepared"), sem("so_zeroed")
    SHARES = (("so_v", 0, 4), ("so_p", 4, BLOCK_GROUPS))
    product = [sem(n + "_product") for n, _, _ in SHARES]
    summed = [sem(n + "_summed") for n, _, _ in SHARES]
    turned = [sem(n + "_turned") for n, _, _ in SHARES]
    with ExitStack() as ctx:
        sb = lambda n, shape: ctx.enter_context(nc.sbuf_tensor("so_" + n, shape, F32))
        u, w, wt = (sb(n, [P, BLOCK_GROUPS, QB, QB]) for n in ("u", "w", "wt"))
        part = sb("part", [P, BLOCK_GROUPS, (QB // 2) ** 2])
        gw, gate = sb("gw", [P, 2, KD * P]), sb("gate", [P, 2, T])
        ps = ctx.enter_context(nc.psum_tensor("so_ps", [P, 2, 1024], F32))
        block = ctx.enter_context(nc.Block())

        def flat(t):
            return t.rearrange("p g i k -> p g (i k)")

        @block.sync
        def _(sp):
            src = io["blk_m"].rearrange("c h d j e -> (c h d j) e").rearrange("(g p) e -> p g e", p=P)
            sp.dma_start(flat(u[:, :, :, :]), src).then_inc(u_in, 16)

            def load(j):
                sp.dma_start(gw[:, j % 2, :], io["w_r_gate"][j]).then_inc(w_in[j % 2], 16)

            load(0)
            load(1)
            for j in range(KD):
                sp.wait_ge(gate_done, j + 1)
                sp.dma_start(io["gate_r"][j], gate[:, j % 2, :]).then_inc(gate_out[j % 2], 16)
                if j + 2 < KD:
                    load(j + 2)
            for s in (0, 1):
                sp.wait_ge(gate_out[s], 16 * KD // 2)
            dst = io["blk_w"].rearrange("c h d k j e -> k (c h d) j e").rearrange("k (g q) j e -> k g q j e", g=BLOCK_GROUPS)
            n = 0
            for share, (_, lo, hi) in enumerate(SHARES):
                for kind, src, ready in ((0, w, (summed[share], QB - 1)), (1, wt, (turned[share], 1))):
                    sp.wait_ge(*ready)
                    for gr in range(lo, hi):
                        sp.dma_start(dst[kind, gr], flat(src[:, :, :, :])[:, gr, :]).then_inc(w_out, 16)
                        n += 1
            sp.wait_ge(w_out, 16 * n)

        def solve(eng, share):
            _, lo, hi = SHARES[share]
            n = hi - lo
            eng.wait_ge(u_in, 16)
            eng.wait_ge(prepared, 1)
            for step, k in enumerate(range(QB - 1, 0, -1)):
                shape = [P, n, k, QB - k]
                p = part[:, lo:hi, 0:k * (QB - k)].rearrange("p g (i c) -> p g i c", c=QB - k)
                col, row, acc = u[:, lo:hi, 0:k, k:k + 1], w[:, lo:hi, k:k + 1, k:QB], w[:, lo:hi, 0:k, k:QB]
                if step > 0:
                    eng.wait_ge(summed[share], step)
                eng.tensor_tensor(p, col.to_broadcast(shape), row.to_broadcast(shape), ALU.mult)\
                   .then_inc(product[share], 1)
                eng.wait_ge(product[share], step + 1)
                eng.tensor_tensor(acc, acc, p, ALU.add).then_inc(summed[share], 1)
            eng.wait_ge(summed[share], QB - 1)
            eng.tensor_copy(wt[:, lo:hi, :, :], w[:, lo:hi, :, :].rearrange("p g i k -> p g k i"))\
               .then_inc(turned[share], 1)

        @block.tensor
        def _(pe):
            for j in range(KD):
                pe.wait_ge(w_in[j % 2], 16 * (j // 2 + 1))
                if j >= 2:
                    pe.wait_ge(gate_done, j - 1)
                project_halves(pe, ps[:, j % 2, :], tiles_of(gw[:, j % 2, :]), g.h, KD).then_inc(w_used, 1)

        @block.scalar
        def _(act):
            for j in range(KD):
                act.wait_ge(w_used, j + 1)
                if j >= 2:
                    act.wait_ge(gate_out[j % 2], 16 * (j // 2))
                act.activation(by_half(gate[:, j % 2, :]), halves(ps[:, j % 2, :]), ACT.Sigmoid)\
                   .then_inc(gate_done, 1)

        @block.vector
        def _(dve):
            solve(dve, 0)

        @block.gpsimd
        def _(pool):
            pool.memset(w[:, :, :, :], 0.0).then_inc(zeroed, 1)
            pool.wait_ge(zeroed, 1)
            pool.memset(flat(w[:, :, :, :])[:, :, 0:QB * QB:QB + 1], 1.0).then_inc(prepared, 1)
            solve(pool, 1)


PE_STEPS = ["MB", "MK", "Z", "T", "X", "U", "Y", "S"]
DVE_STEPS = ["MB", "MK", "Z", "T", "S"]
ACT_STEPS = ["X", "U", "Y"]


def phase_wkv(nc, sem, io, g, carry, first, n_chunks, state_in, state_out, tag):
    count = lambda steps, i, name: len(steps) * i + steps.index(name) + 1
    loaded = [[sem(f"{tag}_in{d}{s}") for s in (0, 1)] for d in (0, 1)]
    bk_in = [sem(f"{tag}_bk_in{d}") for d in (0, 1)]
    y_out = [[sem(f"{tag}_y_out{d}{s}") for s in (0, 1)] for d in (0, 1)]
    pe_done, dve_done, act_done = ([sem(f"{tag}_{e}_done{d}") for d in (0, 1)] for e in ("pe", "dve", "act"))
    summed = [sem(f"{tag}_summed{d}") for d in (0, 1)]
    pe_ready, dve_ready, sp_ready = sem(tag + "_pe_go"), sem(tag + "_dve_go"), sem(tag + "_sp_go")
    state_ready, state_stored, zeroed = sem(tag + "_state_ready"), sem(tag + "_state_stored"), sem(tag + "_zeroed")
    STEP_LOADS = 9
    with ExitStack() as ctx:
        sb = lambda n, shape: ctx.enter_context(nc.sbuf_tensor(f"{tag}_{n}", shape, F32))
        ar = sb("ar", [P, 2, 2, 2, PAIRS, WC])
        bk = sb("bk", [P, 2, 2, PAIRS, P])
        tk = sb("tk", [P, 2, 2, 2, PAIRS, HD])
        vv = sb("vv", [P, 2, 2, PAIRS, HD])
        mb, mk = sb("mb", [P, 2, PAIRS, 2, WC]), sb("mk", [P, 2, PAIRS, 2, WC])
        ww = sb("ww", [P, 2, 2, 2, PAIRS, WC])
        z, tt = sb("z", [P, 2, PAIRS, WC]), sb("tt", [P, 2, PAIRS, WC])
        x_, u_, st = sb("x", [P, 2, PAIRS, HD]), sb("u", [P, 2, PAIRS, HD]), sb("st", [P, 2, PAIRS, HD])
        y_ = sb("y", [P, 2, 2, PAIRS, HD])
        p0 = ctx.enter_context(nc.psum_tensor(tag + "_p0", [P, 2, 2, 512], F32))
        p1 = ctx.enter_context(nc.psum_tensor(tag + "_p1", [P, 2, 2, 512], F32))
        block = ctx.enter_context(nc.Block())
        narrow = lambda p: p.rearrange("p (j w) -> p j w", w=WC)
        wide = lambda p: p.rearrange("p b (j f) -> p (b j) f", f=2 * WC)
        over_heads = lambda m: m.unsqueeze(1).to_broadcast([P, PAIRS, WC])
        chunk = lambda d, i: i + first if d == 0 else first + n_chunks - 1 - i
        plain = lambda s, d: ww[:, s, d, 1 - d]
        turned = lambda s, d: ww[:, s, d, d]
        ITERS = n_chunks // 2

        @block.sync
        def _(sp):
            if state_in is not None:
                sp.dma_start(st[:, :, :, :], state_in.rearrange("d p (j w) -> p d j w", w=HD)).then_inc(state_ready, 16)

            def load_bk(it, s):
                for d in (0, 1):
                    src = io["chan"][d, bass.ds(chunk(d, 2 * it + s), 1)].squeeze(0)\
                        .rearrange("p (q t) -> p q t", t=WC)
                    for h in (0, 1):
                        rows = slice(64 * h, 64 * h + 64)
                        sp.dma_start(bk[rows, d, :, :, rows].rearrange("p q j t -> p (q j) t"),
                                     src[rows, B_HAT * PAIRS:, :]).then_inc(bk_in[d], 16)

            def load(it, s):
                for d in (0, 1):
                    c = chunk(d, 2 * it + s)
                    sp.dma_start(ar[:, s, d, :, :, :].rearrange("p q j t -> p (q j t)"),
                                 io["chan"][d, bass.ds(c, 1)].squeeze(0)[:, 0:B_HAT * PAIRS * WC])\
                      .then_inc(loaded[d][s], 16)
                    for h in (0, 1):
                        rows = slice(64 * h, 64 * h + 64)
                        tok = io["tok"][d, bass.ds(c * WC, WC), :].rearrange("t (n h m) -> h t n m", h=2, m=HD)
                        val = io["val"][bass.ds(c * WC, WC), :].rearrange("t (n h m) -> h t n m", h=2, m=HD)
                        sp.dma_start(tk[rows, s, d, :, :, :].rearrange("p q j m -> p (q j) m"), tok[h])\
                          .then_inc(loaded[d][s], 16)
                        sp.dma_start(vv[rows, s, d, :, :], val[h]).then_inc(loaded[d][s], 16)
                    for hb in range(4):
                        rows, cols = slice(QB * hb, QB * hb + QB), slice(QB * (hb % 2), QB * (hb % 2) + QB)
                        src = io["blk_w"][bass.ds(c, 1)].squeeze(0)[hb, d]
                        sp.dma_start(ww[rows, s, d, :, :, cols].rearrange("p k j e -> p (k j) e"),
                                     src.rearrange("k j (r e) -> r (k j) e", e=QB)).then_inc(loaded[d][s], 16)

            def store(it, s):
                for d in (0, 1):
                    i = 2 * it + s
                    sp.wait_ge(act_done[d], count(ACT_STEPS, i, "Y") + 1)
                    sp.sem_inc(sp_ready, 1)
                    dst = io["wkv_y"][d, bass.ds(chunk(d, i), 1)].squeeze(0).rearrange("p (j w) -> p j w", w=HD)
                    sp.dma_start(dst, y_[:, s, d, :, :]).then_inc(y_out[d][s], 16)

            def next_bk(it, s):
                for d in (0, 1):
                    sp.wait_ge(pe_done[d], count(PE_STEPS, 2 * it + s, "MK"))
                sp.sem_inc(sp_ready, 1)
                load_bk(it + s, 1 - s)

            sp.wait_ge(zeroed, 2)
            load_bk(0, 0)
            load(0, 0)
            load(0, 1)
            if ITERS > 1:
                with sp.Fori(0, ITERS - 1) as it:
                    for s in (0, 1):
                        next_bk(it, s)
                        store(it, s)
                        for d in (0, 1):
                            sp.wait_ge(pe_done[d], len(PE_STEPS) * (2 * it + s + 1))
                        sp.sem_inc(sp_ready, 1)
                        load(it + 1, s)
            next_bk(ITERS - 1, 0)
            for s in (0, 1):
                store(ITERS - 1, s)
            for d in (0, 1):
                for s in (0, 1):
                    sp.wait_ge(y_out[d][s], 16 * ITERS + 16)
            if state_out is not None:
                for d in (0, 1):
                    sp.wait_ge(dve_done[d], len(DVE_STEPS) * n_chunks + 1)
                sp.dma_start(state_out.rearrange("d p (j w) -> p d j w", w=HD), st[:, :, :, :]).then_inc(state_stored, 16)
                sp.wait_ge(state_stored, 16)

        @block.gpsimd
        def _(pool):
            pool.memset(bk[:, :, :, :, :], 0.0).then_inc(zeroed, 1)
            pool.memset(ww[:, :, :, :, :, :], 0.0).then_inc(zeroed, 1)
            if state_in is None:
                pool.memset(st[:, :, :, :], 0.0).then_inc(state_ready, 16)
            for d in (0, 1):
                for s in (0, 1):
                    pool.sem_inc(y_out[d][s], 16)

        @block.tensor
        def _(pe):
            pe.wait_ge(state_ready, 16)
            halves = (slice(0, 64), slice(64, 128))

            def stage(d, products, waits, rows_of=halves):
                for s, v in waits:
                    pe.wait_ge(s, v)
                pe.sem_inc(pe_ready, 1)
                for j in range(PAIRS):
                    for rows in rows_of:
                        for out, lhs, rhs, starts, stops in products(j):
                            last = pe.matmul(out[rows], lhs[rows], rhs[rows], start=starts, stop=stops)
                last.then_inc(pe_done[d], 1)

            def alone(out, lhs, rhs):
                return [(out, lhs, rhs, True, True)]

            def total(out, *pairs):
                return [(out, l, r, n == 0, n == len(pairs) - 1) for n, (l, r) in enumerate(pairs)]

            def step(it, s):
                i = 2 * it + s
                dve = lambda d, name, at=i: (dve_done[d], count(DVE_STEPS, at, name) + 1)
                act = lambda d, name, at=i: (act_done[d], count(ACT_STEPS, at, name) + 1)
                both_heads = (slice(0, P),)
                for d in (0, 1):
                    stage(d, lambda j: alone(wide(p0[:, d])[:, j], bk[:, d, 0, j, :], ar[:, s, d, :, j, :]),
                          [(bk_in[d], 32 * i + 32), (loaded[d][s], 16 * STEP_LOADS * (it + 1)),
                           (act_done[d], len(ACT_STEPS) * i + 1)], both_heads)
                for d in (0, 1):
                    stage(d, lambda j: alone(wide(p1[:, d])[:, j], bk[:, d, 1, j, :], ar[:, s, d, :, j, :]),
                          [(dve_done[d], len(DVE_STEPS) * i + 1)], both_heads)
                for d in (0, 1):
                    stage(d, lambda j: alone(narrow(p0[:, d, 0])[:, j], mb[:, d, j, 0, :], plain(s, d)[:, j]),
                          [dve(d, "MB")])
                for d in (0, 1):
                    stage(d, lambda j: alone(narrow(p1[:, d, 1])[:, j], z[:, d, j, :], turned(s, d)[:, j]),
                          [dve(d, "Z")])
                for d in (0, 1):
                    stage(d, lambda j: total(narrow(p0[:, d, 0])[:, j], (ar[:, s, d, 0, j, :], st[:, d, j, :]),
                                             (mk[:, d, j, 0, :], vv[:, s, d, j, :])), [])
                for d in (0, 1):
                    stage(d, lambda j: alone(narrow(p0[:, d, 1])[:, j], tt[:, d, j, :], x_[:, d, j, :]),
                          [act(d, "X"), dve(d, "T")])
                for d in (0, 1):
                    stage(d, lambda j: total(narrow(p1[:, d, 0])[:, j], (ar[:, s, d, 1, j, :], st[:, d, j, :]),
                                             (mb[:, d, j, 1, :], u_[:, d, j, :]),
                                             (mk[:, d, j, 1, :], vv[:, s, d, j, :])), [act(d, "U")])
                    stage(d, lambda j: total(narrow(p1[:, d, 1])[:, j], (tk[:, s, d, 0, j, :], u_[:, d, j, :]),
                                             (tk[:, s, d, 1, j, :], vv[:, s, d, j, :])), [])

            with pe.Fori(0, ITERS) as it:
                step(it, 0)
                step(it, 1)

        @block.scalar
        def _(act):
            for d in (0, 1):
                act.sem_inc(act_done[d], 1)
            with act.Fori(0, ITERS) as it:
                for s in (0, 1):
                    i = 2 * it + s
                    for name, src, dst in (("X", lambda d: p0[:, d, 0, :], lambda d: x_[:, d]),
                                           ("U", lambda d: p0[:, d, 1, :], lambda d: u_[:, d]),
                                           ("Y", lambda d: p1[:, d, 0, :], lambda d: y_[:, s, d])):
                        for d in (0, 1):
                            act.wait_ge(pe_done[d], count(PE_STEPS, i, name))
                            if name == "Y":
                                act.wait_ge(y_out[d][s], 16 * it + 16)
                            act.activation(dst(d), narrow(src(d)), ACT.Copy).then_inc(act_done[d], 1)

        @block.vector
        def _(dve):
            for d in (0, 1):
                dve.sem_inc(dve_done[d], 1)
            with dve.Fori(0, ITERS) as it:
                for s in (0, 1):
                    i = 2 * it + s
                    pairs = lambda d: g.wmask[:, d, STRICT:UPTO + 1, :].rearrange("p l w -> p (l w)")\
                        .unsqueeze(1).to_broadcast([P, PAIRS, 2 * WC])
                    flat = lambda m: m.rearrange("p j q w -> p j (q w)")
                    for d in (0, 1):
                        dve.wait_ge(pe_done[d], count(PE_STEPS, i, "MB"))
                        dve.tensor_tensor(flat(mb[:, d]), wide(p0[:, d]), pairs(d), ALU.mult).then_inc(dve_done[d], 1)
                    for d in (0, 1):
                        dve.wait_ge(pe_done[d], count(PE_STEPS, i, "MK"))
                        dve.tensor_tensor(flat(mk[:, d]), wide(p1[:, d]), pairs(d), ALU.mult).then_inc(dve_done[d], 1)
                    for d in (0, 1):
                        dve.wait_ge(pe_done[d], count(PE_STEPS, i, "Z"))
                        dve.tensor_tensor(z[:, d], narrow(p0[:, d, 0]), over_heads(g.wmask[:, d, BETWEEN, :]),
                                          ALU.mult).then_inc(dve_done[d], 1)
                    for d in (0, 1):
                        dve.wait_ge(pe_done[d], count(PE_STEPS, i, "T"))
                        dve.tensor_tensor(tt[:, d], turned(s, d), narrow(p1[:, d, 1]), ALU.add)\
                           .then_inc(dve_done[d], 1)
                    for d in (0, 1):
                        dve.wait_ge(pe_done[d], count(PE_STEPS, i, "S"))
                        dve.tensor_tensor(st[:, d], st[:, d], narrow(p1[:, d, 1]), ALU.add).then_inc(summed[d], 1)
                        dve.wait_ge(summed[d], i + 1)
                        dve.sem_inc(dve_ready, 1)
                        end = carry[:, d, bass.ds(chunk(d, i), 1), :].squeeze(1)
                        dve.tensor_tensor(st[:, d], st[:, d], end.unsqueeze(2).to_broadcast([P, PAIRS, HD]),
                                          ALU.mult).then_inc(dve_done[d], 1)


def phase_wkv_out(nc, sem, io, g, low, bonus, y_r, split):
    rounded = sem("wo_rounded")
    y_in = [sem("wo_y_in0"), sem("wo_y_in1")]
    norm_chain, sq_done, root_done = sem("wo_norm_chain"), sem("wo_sq_done"), sem("wo_root_done")
    normed, go, tr_full, tr_chain, tr_done = (sem("wo_normed"), sem("wo_go"), sem("wo_tr_full"),
                                              sem("wo_tr_chain"), sem("wo_tr_done"))
    g_in, g_full, g_done = sem("wo_g_in"), sem("wo_g_full"), sem("wo_g_done")
    CHAIN = 6
    with ExitStack() as ctx:
        sb = lambda n, shape: ctx.enter_context(nc.sbuf_tensor("wo_" + n, shape, F32))
        y = sb("y", [P, 2, 2, PAIRS, HD])
        sq = sb("sq", [P, PAIRS, HD])
        mean, var = sb("mean", [P, PAIRS]), sb("var", [P, PAIRS])
        g2 = sb("g2", [P, D])
        ps = ctx.enter_context(nc.psum_tensor("wo_ps", [P, 2, 512], F32))
        pg = ctx.enter_context(nc.psum_tensor("wo_pg", [P, 2, 1024], F32))
        block = ctx.enter_context(nc.Block())
        per_head = lambda a: a.unsqueeze(2).to_broadcast([P, PAIRS, HD])

        @block.sync
        def _(sp):
            sp.dma_start(g2[:, :], io["g2"]).then_inc(g_in, 16)

            def load(it, s):
                for d in (0, 1):
                    src = io["wkv_y"][d, bass.ds(2 * it + s, 1)].squeeze(0).rearrange("p (j w) -> p j w", w=HD)
                    sp.dma_start(y[:, s, d, :, :], src).then_inc(y_in[s], 16)

            stream(sp, NWC, load, used=tr_full)

        @block.tensor
        def _(pe):
            with pe.Fori(0, NWC // 2) as it:
                for s in (0, 1):
                    n = 2 * it + s
                    pe.wait_ge(normed, n + 1)
                    pe.wait_ge(tr_done, n + 1)
                    pe.sem_inc(go, 1)
                    for j in range(PAIRS):
                        for rows in (slice(0, 64), slice(64, 128)):
                            last = pe.matmul(ps[rows, s, WC * j:WC * j + WC], y[rows, s, 0, j, :],
                                             g.ident_w[rows], start=True, stop=True)
                    last.then_inc(tr_full, 1)
            pe.wait_ge(g_in, 16)
            for j in range(PAIRS):
                if j >= 2:
                    pe.wait_ge(g_done, j - 1)
                for lo, hi in BANKS:
                    last = pe.matmul(pg[:, j % 2, lo:hi], g2[:, P * j:P * j + P], low[:, 2, lo:hi],
                                     start=True, stop=True)
                last.then_inc(g_full, 1)

        @block.scalar
        def _(act):
            with act.Fori(0, NWC // 2) as it:
                for s in (0, 1):
                    n = 2 * it + s
                    act.wait_ge(norm_chain, CHAIN * n + 3)
                    act.activation(sq[:, :, :], y[:, s, 0, :, :], ACT.Square).then_inc(sq_done, 1)
                    act.wait_ge(norm_chain, CHAIN * n + 6)
                    act.activation(var[:, :], var[:, :], ACT.Sqrt).then_inc(root_done, 1)
            for j in range(PAIRS):
                act.wait_ge(g_done, j + 1)
                act.activation(split[0][:, j, :], y_r[:, j, :], ACT.Copy).then_inc(rounded, 1)

        @block.vector
        def _(dve):
            dve.sem_inc(tr_done, 2)
            with dve.Fori(0, NWC // 2) as it:
                for s in (0, 1):
                    n = 2 * it + s
                    yy = y[:, s, 0, :, :]

                    def then(ins, at):
                        ins.then_inc(norm_chain, 1)
                        dve.wait_ge(norm_chain, CHAIN * n + at)

                    dve.wait_ge(y_in[s], 32 * it + 32)
                    then(dve.tensor_tensor(yy, yy, y[:, s, 1, :, :], ALU.add), 1)
                    then(dve.tensor_reduce(mean[:, :], yy, AX.X, ALU.add), 2)
                    dve.tensor_scalar(mean[:, :], mean[:, :], 1.0 / HD, None, ALU.mult).then_inc(tr_chain, 1)
                    dve.wait_ge(tr_chain, 3 * n + 1)
                    then(dve.tensor_tensor(yy, yy, per_head(mean[:, :]), ALU.subtract), 3)
                    dve.wait_ge(sq_done, n + 1)
                    then(dve.tensor_reduce(var[:, :], sq[:, :, :], AX.X, ALU.add), 4)
                    then(dve.tensor_scalar(var[:, :], var[:, :], 1.0 / HD, 64e-5, ALU.mult, ALU.add), 5)
                    then(dve.reciprocal(var[:, :], var[:, :]), 6)
                    dve.wait_ge(root_done, n + 1)
                    dve.tensor_tensor(yy, yy, per_head(var[:, :]), ALU.mult).then_inc(normed, 1)
                    dve.wait_ge(tr_full, n + 1)
                    out = y_r[:, :, bass.ds(WC * n, WC)]
                    dve.tensor_tensor(out, ps[:, s, :].rearrange("p (j t) -> p j t", t=WC),
                                      per_head(g.v("lnx_w")), ALU.mult).then_inc(tr_chain, 1)
                    dve.wait_ge(tr_chain, 3 * n + 2)
                    dve.tensor_tensor(out, out, per_head(g.v("lnx_b")), ALU.add).then_inc(tr_chain, 1)
                    dve.wait_ge(tr_chain, 3 * n + 3)
                    dve.tensor_tensor(out, out, bonus[:, :, bass.ds(WC * n, WC)], ALU.add).then_inc(tr_done, 1)
            dve.wait_ge(tr_done, NWC + 2)

            def low_part(j):
                dve.wait_ge(rounded, j + 1)
                dve.tensor_tensor(split[1][:, j, :], y_r[:, j, :], split[0][:, j, :].bitcast(F32), ALU.subtract)

            for j in range(PAIRS):
                dve.wait_ge(g_full, j + 1)
                dve.tensor_tensor(y_r[:, j, :], y_r[:, j, :], pg[:, j % 2, 0:T], ALU.mult).then_inc(g_done, 1)
                if j > 0:
                    low_part(j - 1)
            low_part(PAIRS - 1)


def build(nc, io):
    with ExitStack() as ctx:
        serial = [0]

        def run(phase, *args, **kw):
            used = []
            serial[0] += 1

            def sem(name):
                used.append(nc.alloc_semaphore(f"p{serial[0]}_{name}"))
                return used[-1]

            phase(nc, sem, *args, **kw)
            nc.all_engine_barrier()
            nc.clear_and_free_semaphores(used)
            nc.all_engine_barrier()

        def sb(scope, name, shape):
            return scope.enter_context(nc.sbuf_tensor(name, shape, F32))

        g = Resident()
        g.h = sb(ctx, "h", [P, KD, T])
        g.mod = sb(ctx, "mod", [P, 6 * KD, 2])
        g.cst, g.vec, g.row = sb(ctx, "cst", [P, CST_N]), sb(ctx, "vec", [P, VEC_N]), sb(ctx, "row", [P, ROW_N])
        g.mu_q, g.mu_own = sb(ctx, "mu_q", [P, 27, 4]), sb(ctx, "mu_own", [P, 27])
        g.k_a_c, g.neg_a = sb(ctx, "k_a_c", [P, KD]), sb(ctx, "neg_a", [P, 64])
        g.v = lambda name: g.vec[:, VEC_AT[name][0]:VEC_AT[name][1]]
        g.r = lambda name: g.row[:, ROW_AT[name][0]:ROW_AT[name][1]]
        c = lambda name: g.cst[:, CST_AT[name][0]:CST_AT[name][1]]
        g.ident, g.ones, g.head_ones, g.ident_w = c("ident"), c("ones"), c("head_ones"), c("ident_w")
        g.sel = c("sel")
        g.tri = c("tri").rearrange("p (d f) -> p d f", d=2)
        g.wmask = c("wmask").rearrange("p (d l f) -> p d l f", d=2, f=WC)
        g.reset = c("reset").rearrange("p (d t) -> p d t", d=2)
        g.qmask = c("qmask").rearrange("p (m q) -> p m q", q=4)

        pair = lambda scope, name, tiles: tuple(
            scope.enter_context(nc.sbuf_tensor(f"{name}_{part}", [P, tiles, T], F32R)) for part in ("hi", "lo"))
        run(phase_load, io, g)
        run(phase_modulation, io, g)
        with ExitStack() as scope:
            g.x = sb(scope, "x", [P, KD, T])
            run(phase_load_x, io, g)
            run(phase_norm, g, "norm1", g.v("norm1"), 0, g.h)
        with ExitStack() as mixers:
            g.mix = sb(mixers, "mix", [P, KD, T])
            with ExitStack() as mamba:
                y_tok = sb(mamba, "y_tok", [P, NCH, M_INNER])
                with ExitStack() as scan:
                    x_tok = sb(scan, "x_tok", [P, NCH, M_INNER])
                    b_chan, c_chan = g.mix[:, 0:M_GROUPS, :], g.mix[:, M_GROUPS:2 * M_GROUPS, :]
                    b_tok = sb(scan, "b_tok", [P, NCH, M_GROUPS * M_STATE])
                    dts = {n: sb(scan, n, [P, NCH, 64]) for n in DT_PARTS}
                    run(phase_conv, io, g, "xin", 0, KI, None, x_tok)
                    run(phase_conv, io, g, "bin", KI, M_GROUPS, b_chan, b_tok)
                    run(phase_conv, io, g, "cin", KI + M_GROUPS, M_GROUPS, c_chan, None)
                    run(phase_dt, io, g, dts)
                    run(phase_ssd, io, g, dts, x_tok, b_chan, c_chan, b_tok, y_tok)
                y_chan = sb(mamba, "y_chan", [P, KI, T])
                run(phase_m_gate, io, g, y_tok, y_chan)
                run(phase_m_out, io, g, y_chan)
            g.x = sb(mixers, "x_again", [P, KD, T])
            with ExitStack() as rwkv:
                low = sb(rwkv, "low", [P, 3, T])
                bonus = g.x
                carry = sb(rwkv, "carry", [P, 2, NWC, PAIRS])
                run(phase_low, io, g, low)
                run(phase_rwkv_in, io, g, low, bonus, carry)
                run(phase_blocks, io)
                run(phase_solve, io, g)
                run(phase_wkv, io, g, carry, 0, CTX // WC, None, io["wkv_out"], "wc")
                run(phase_wkv, io, g, carry, CTX // WC, LAT // WC, io["wkv_in"], None, "wl")
                mix = pair(rwkv, "mix", KD)
                with ExitStack() as out:
                    y = pair(out, "y_parts", KD)
                    run(phase_wkv_out, io, g, low, bonus, g.h, y)
                    run(phase_r_out, io, g, y, mix)
                raw = sb(rwkv, "w_o_raw", [P, 2, KD * P])
                run(phase_residual, g, "w_o", lambda n: io["w_o"][n], raw, mix, KD, 2 * KD)
            with ExitStack() as ffn:
                h = pair(ffn, "h", KD)
                run(phase_norm, g, "norm2", g.v("norm2"), 3 * KD, g.h, h)
                part = KF // 2
                hidden = pair(ffn, "hidden", part)
                spare = g.mix[:, 0:2, :], g.mix[:, 2:4, :]
                room = g.mix[:, :, :].rearrange("p k t -> p (k t)")
                raw_up = room[:, 4 * T:4 * T + 2 * D].rearrange("p (s w) -> p s w", s=2)
                raw_down = room[:, 0:2 * part * P].rearrange("p (s w) -> p s w", s=2)
                for n in range(KF // part):
                    down = io["w_down"][n]
                    run(phase_up, io, g, f"up{n}", n * part, part, h, spare, raw_up, hidden)
                    run(phase_residual, g, f"down{n}", lambda t: down[t], raw_down, hidden, part, 5 * KD)
            run(phase_norm, g, "final", g.v("final"), None, g.h)
            run(phase_store, io, g)


def _tiles(w):
    k, m = w.shape
    return np.ascontiguousarray(w.reshape(k // P, P, m // P, P).transpose(2, 1, 0, 3).reshape(m // P, P, k))


def _cols(v):
    return np.ascontiguousarray(v.reshape(-1, P).T)


def _constants():
    f32 = np.float32
    i, f = np.arange(P)[:, None], np.arange(P)[None, :]
    r, w = np.arange(P)[:, None] % WC, np.arange(WC)[None, :]
    masks = []
    for d in (0, 1):
        a, b = (r, w) if d == 0 else (w, r)
        masks += [b > a, b >= a]
        masks.append((a >= QB) & (b < QB))
    t = np.arange(T)
    ch = (np.arange(27)[None, :, None] * P + np.arange(P)[:, None, None]) // QUARTER
    parts = dict(
        ident=np.eye(P), ones=np.ones((P, P)), head_ones=(i // HD == f // HD),
        tri=np.concatenate([f >= i, f <= i], 1), wmask=np.concatenate(masks, 1),
        reset=np.repeat(np.concatenate([t % WC != 0, t % WC != WC - 1])[None], P, 0),
        qmask=(ch == np.arange(4)[None, None, :]).reshape(P, -1), ident_w=(r == w),
        sel=(np.arange(P)[:, None] % 2 == np.arange(2)[None, :]))
    return np.ascontiguousarray(np.concatenate([parts[n].astype(f32) for n in CST], 1))


def _lay_out(i):
    a = {n: np.asarray(v) for n, v in i.items()}
    l = {n: a[n][0] for n in a if n not in ("c_ctx", "final_norm_w")}
    w_in = l["w_in"]
    o1, o2 = M_INNER, M_INNER + M_INNER + 2 * M_GROUPS * M_STATE
    o3 = o2 + 2 * M_HEADS
    o4 = o3 + R_COLS
    z, xbc, dt, rw, gates = w_in[:, :o1], w_in[:, o1:o2], w_in[:, o2:o3], w_in[:, o3:o4], w_in[:, o4:]
    rt, gt = _tiles(rw), _tiles(gates)
    low_w = rt[[8, 25, 26]]
    up = np.stack([l["w2"].reshape(P, D), l["a2"].reshape(P, D)])
    up = up.reshape(2, P, KD, P).transpose(2, 1, 0, 3).reshape(KD, P, 2 * P)
    rkv_w = np.concatenate([rt[0:8], rt[9:17], rt[17:25], up], 2)
    vec = dict(norm1=l["norm1_w"], norm2=l["norm2_w"], final=a["final_norm_w"],
               conv_b=l["conv_b"], m_norm=l["m_norm_w"], mu=l["mu_shift"], w0=l["w0"], a0=l["a0"],
               k_k=l["k_k"], k_a=l["k_a"], r_k=l["r_k"], lnx_w=l["lnx_w"], lnx_b=l["lnx_b"])
    vec = {n: _cols(v) for n, v in vec.items()}
    vec["b_ada"] = np.repeat(_cols(l["b_ada"]), 2, 1)
    vec["conv_w"] = l["conv_w"].reshape(M_CONV, 24, P).transpose(2, 1, 0).reshape(P, -1)
    row = dict(dt_bias=l["dt_bias"], a_log=l["a_log"], d_skip=l["d_skip"])
    row = np.concatenate([np.repeat(row[n].reshape(1, -1), P, 0) for n in ROW], 1)
    gu = _tiles(l["w_gu"])
    ssm = np.stack([l["state_ssm_fwd"], l["state_ssm_bwd"]])
    ssm = ssm.reshape(2, M_GROUPS, GI, M_STATE).transpose(0, 1, 3, 2)
    wkv = np.stack([l["state_wkv_fwd"], l["state_wkv_bwd"]])
    wkv = wkv.reshape(2, PAIRS, 2, HD, HD).transpose(0, 2, 4, 1, 3).reshape(2, P, PAIRS * HD)
    x = np.concatenate([a["x_prompt"][0], a["x_sample"][0]], 0)
    out = dict(
        x_t=x.T.reshape(KD, P, T), cond=np.stack([_cols(a["c_ctx"]), _cols(a["c"])], 2), cst=_constants(),
        vec=np.concatenate([vec[n] for n in VEC], 1), row=row,
        w_ada=l["w_ada"].reshape(KD, P, 12, 512).transpose(2, 1, 0, 3).reshape(12, P, KD * 512),
        w_xbc=_tiles(xbc), w_dt=dt.reshape(KD, P, 64).transpose(1, 0, 2).reshape(P, -1),
        w_z=z.reshape(KD, P, M_GROUPS, GI).transpose(2, 1, 0, 3).reshape(M_GROUPS, P, -1),
        w_m=np.concatenate([_tiles(l["w_m_out"]), gt[:KD]], 2), w_low=low_w, w_rkv=rkv_w,
        w_r=_tiles(l["w_r_out"]), w_r_gate=gt[KD:], w_o=_tiles(l["w_o"]),
        w_gu=np.stack([gu[:KF], gu[KF:]], 1).reshape(2 * KF, P, D),
        w_down=np.stack(np.split(_tiles(l["w_down"]), 2, 2)), g2=l["g2"], ssm_in=ssm, wkv_in=wkv)
    return {n: np.ascontiguousarray(v) for n, v in out.items()}


OUTS = dict(y=[KD, P, T], ssm_out=[2, M_GROUPS, M_STATE, GI], wkv_out=[2, P, PAIRS * HD])
SCRATCH = dict(chan=[2, NWC, P, 4 * PAIRS * WC], tok=[2, T, 2 * D], val=[T, D], wkv_y=[2, NWC, P, PAIRS * HD],
               cs_rows=[NCH, 64, P],
               blk_m=[NWC, 4, 2, PAIRS, QB * QB], blk_w=[NWC, 4, 2, 2, PAIRS, QB * QB],
               gate_r=[KD, P, T])


def declare(nc, arrays):
    io = {}
    for name, a in arrays.items():
        io[name] = nc.dram_tensor("in_" + name, a.shape, F32, kind="ExternalInput").ap()
    for name, shape in OUTS.items():
        io[name] = nc.dram_tensor("out_" + name, shape, F32, kind="ExternalOutput").ap()
    for name, shape in SCRATCH.items():
        io[name] = nc.dram_tensor("scratch_" + name, shape, F32, kind="Internal").ap()
    return io


def kernel(**inputs):
    import concourse.bacc as bacc
    from concourse.bass_utils import run_bass_kernel_spmd

    nc = bacc.Bacc("TRN2", target_bir_lowering=False, num_devices=1)
    arrays = _lay_out(inputs)
    build(nc, declare(nc, arrays))
    sent = {"in_" + name: a for name, a in arrays.items()}
    got = run_bass_kernel_spmd(nc, [sent], core_ids=[0]).results[0]
    y = np.asarray(got["out_y"]).reshape(D, T).T
    ssm = np.asarray(got["out_ssm_out"]).transpose(0, 1, 3, 2).reshape(2, 1, 1, M_HEADS, HD, M_STATE)
    wkv = np.asarray(got["out_wkv_out"]).reshape(2, 2, HD, PAIRS, HD).transpose(0, 3, 1, 4, 2)
    wkv = wkv.reshape(2, 1, 1, R_HEADS, HD, HD)
    return y[None, :CTX], y[None, CTX:], ssm[0], ssm[1], wkv[0], wkv[1]
```

```python
from contextlib import ExitStack

import numpy as np
import concourse.bass as bass
import concourse.mybir as mybir

P = 128
D = 1024
KD = D // P
CTX, LAT = 128, 512
T = CTX + LAT
SEG = ((0, 0, CTX), (1, CTX, T))
BANKS = ((0, 512), (512, T))
GRID_W = 64
M_INNER, M_HEADS, M_GROUPS, M_STATE, M_CONV = 2048, 32, 4, 128, 5
HPG = M_HEADS // M_GROUPS
HD = 64
GI = M_INNER // M_GROUPS
KI = M_INNER // P
NCH = T // P
R_HEADS = 16
PAIRS = R_HEADS // 2
WC = 64
NWC = T // WC
D_FF = 2816
KF = D_FF // P
R_COLS = 3 * D + 2 * 64 + 2 * 64 + 128
QUARTER = R_COLS // 4
LOG_DECAY = float(np.exp(-0.5))

F32 = mybir.dt.float32
F32R = mybir.dt.float32r
ACT = mybir.ActivationFunctionType
ALU = mybir.AluOpType
AX = mybir.AxisListType

VEC = dict(norm1=KD, norm2=KD, final=KD, b_ada=96, conv_w=24 * M_CONV, conv_b=24, m_norm=KI, mu=27,
           w0=16, a0=16, k_k=KD, k_a=KD, r_k=KD, lnx_w=KD, lnx_b=KD)
ROW = dict(dt_bias=64, a_log=64, d_skip=32)
QB = WC // 2
BLOCK_GROUPS = 2 * NWC * 4 * PAIRS // P
STRICT, UPTO, BETWEEN = 0, 1, 2
CST = dict(ident=P, ones=P, head_ones=P, tri=2 * P, wmask=2 * 3 * WC, reset=2 * T,
           qmask=27 * 4, ident_w=WC, sel=2)


HALF = T // 2
PIECES = ((0, 0, 0, CTX), (1, 0, CTX, HALF), (1, 1, HALF, T))


class Resident:
    pass


def offsets(widths):
    at, out = 0, {}
    for name, n in widths.items():
        out[name] = (at, at + n)
        at += n
    return out, at


VEC_AT, VEC_N = offsets(VEC)
ROW_AT, ROW_N = offsets(ROW)
CST_AT, CST_N = offsets(CST)


def project(pe, psum, w, rhs, k_tiles):
    for lo, hi in BANKS:
        for k in range(k_tiles):
            last = pe.matmul(psum[:, lo:hi], w[:, k, :], rhs[:, k, lo:hi],
                             start=(k == 0), stop=(k == k_tiles - 1))
    return last


def halves(psum):
    return psum.rearrange("p (b n) -> p b n", b=2)[:, :, 0:HALF]


def by_half(a):
    return a.rearrange("p (b n) -> p b n", b=2)


def project_halves(pe, psum, w, rhs, k_tiles):
    for b in (0, 1):
        for k in range(k_tiles):
            last = pe.matmul(halves(psum)[:, b, :], w[:, k, :], by_half(rhs[:, k, :])[:, b, :],
                             start=(k == 0), stop=(k == k_tiles - 1))
    return last


def project_split(pe, psum, w, rhs, k_tiles):
    (wh, wl), (xh, xl) = w, rhs
    terms = ((wh, xh), (wh, xl), (wl, xh))
    for b in (0, 1):
        for k in range(k_tiles):
            for n, (a, x) in enumerate(terms):
                last = pe.matmul(halves(psum)[:, b, :], a[:, k, :], by_half(x[:, k, :])[:, b, :],
                                 start=(k == 0 and n == 0), stop=(k == k_tiles - 1 and n == len(terms) - 1))
    return last


class SplitWeights:

    def __init__(self, nc, sem, ctx, tag, n, width, source, raw, early=None, pieces=1):
        self.n, self.source, self.raw, self.early, self.pieces = n, source, raw, early, pieces
        self.w_in = [[w] for w in early.w_in] if early else [
            [sem(f"{tag}_w_in{s}_{c}") for c in range(pieces)] for s in (0, 1)]
        self.cuts = [slice(width // pieces * c, width // pieces * (c + 1)) for c in range(pieces)]
        self.high, self.low = sem(tag + "_w_high"), sem(tag + "_w_low")
        self.hi = ctx.enter_context(nc.sbuf_tensor(tag + "_w_hi", [P, 2, width], F32R))
        self.lo = ctx.enter_context(nc.sbuf_tensor(tag + "_w_lo", [P, 2, width], F32R))

    def load_all(self, sp):
        def load(it, s):
            for c, cut in enumerate(self.cuts):
                if not (isinstance(it, int) and it == 0):
                    sp.wait_ge(self.low, self.pieces * (2 * it + s - 2) + c + 1)
                sp.dma_start(self.raw[:, s, cut], self.source(2 * it + s)[:, cut]).then_inc(self.w_in[s][c], 16)

        if self.early is None:
            for s in (0, 1):
                load(0, s)
        if self.n > 2:
            with sp.Fori(1, self.n // 2) as it:
                for s in (0, 1):
                    load(it, s)

    def round_tile(self, act, it, s):
        for c, cut in enumerate(self.cuts):
            act.wait_ge(self.w_in[s][c], 16 * it + 16)
            act.activation(self.hi[:, s, cut], self.raw[:, s, cut], ACT.Copy).then_inc(self.high, 1)

    def low_all(self, eng):
        with eng.Fori(0, self.n // 2) as it:
            for s in (0, 1):
                for c, cut in enumerate(self.cuts):
                    eng.wait_ge(self.high, self.pieces * (2 * it + s) + c + 1)
                    eng.tensor_tensor(self.lo[:, s, cut], self.raw[:, s, cut], self.hi[:, s, cut].bitcast(F32),
                                      ALU.subtract).then_inc(self.low, 1)

    def rounding(self, act, use):
        for s in (0, 1):
            self.round_tile(act, 0, s)
        if self.n > 2:
            with act.Fori(0, self.n // 2 - 1) as it:
                for s in (0, 1):
                    use(it, s)
                    self.round_tile(act, it + 1, s)
        for s in (0, 1):
            use(self.n // 2 - 1, s)

    def tile(self, pe, it, s):
        pe.wait_ge(self.low, self.pieces * (2 * it + s + 1))
        return tiles_of(self.hi[:, s, :]), tiles_of(self.lo[:, s, :])

    def parts(self, pe, it, s):
        pe.wait_ge(self.low, self.pieces * (2 * it + s + 1))
        return self.hi[:, s, :], self.lo[:, s, :]


class EarlyLoads:

    def __init__(self, nc, tag, source, raw):
        self.w_in = [nc.alloc_semaphore(f"{tag}_w_in{s}") for s in (0, 1)]
        self.source, self.raw = source, raw

    def start(self, sp):
        for s in (0, 1):
            sp.dma_start(self.raw[:, s, :], self.source(s)).then_inc(self.w_in[s], 16)


class SquareSum:

    def __init__(self, nc, sem, ctx, tag, g):
        self.sq, self.total = ctx.enter_context(nc.sbuf_tensor(tag + "_sq", [P, 2, T], F32)), g.squares
        self.squared, self.added = sem(tag + "_squared"), sem(tag + "_squares_added")

    def clear(self, eng):
        eng.memset(self.total[:, :], 0.0).then_inc(self.added, 1)

    def wait_slot(self, eng, n):
        if n >= 2:
            eng.wait_ge(self.added, n)

    def add(self, eng, n, s):
        eng.wait_ge(self.squared, n + 1)
        eng.wait_ge(self.added, n + 1)
        eng.tensor_tensor(self.total[:, :], self.total[:, :], self.sq[:, s, :], ALU.add).then_inc(self.added, 1)


def stream(sp, n, load, used):
    with sp.Fori(1, n // 2) as it:
        for s in (0, 1):
            sp.wait_ge(used, 2 * it + s - 1)
            load(it, s)


def tiles_of(w):
    return w.rearrange("p (k m) -> p k m", m=P)


def phase_load(nc, sem, io, g):
    cst_in, vec_in, row_in = sem("cst_in"), sem("vec_in"), sem("row_in")
    derived = sem("derived")
    with nc.Block() as block:
        @block.sync
        def _(sp):
            sp.dma_start(g.cst[:, :], io["cst"]).then_inc(cst_in, 16)
            sp.dma_start(g.vec[:, :], io["vec"]).then_inc(vec_in, 16)
            sp.dma_start(g.row[:, :], io["row"]).then_inc(row_in, 16)

        @block.vector
        def _(dve):
            dve.wait_ge(vec_in, 16)
            dve.wait_ge(cst_in, 16)
            dve.tensor_tensor(g.mu_q[:, :, :], g.qmask, g.v("mu").unsqueeze(2).to_broadcast([P, 27, 4]),
                              ALU.mult).then_inc(derived, 1)
            dve.tensor_scalar(g.mu_own[:, :], g.v("mu"), -1.0, 1.0, ALU.mult, ALU.add).then_inc(derived, 1)
            dve.tensor_scalar(g.k_a_c[:, :], g.v("k_a"), -1.0, 1.0, ALU.mult, ALU.add).then_inc(derived, 1)

        @block.scalar
        def _(act):
            act.wait_ge(row_in, 16)
            act.activation(g.neg_a[:, :], g.r("a_log"), ACT.Exp).then_inc(derived, 1)
            act.wait_ge(derived, 4)
            act.mul(g.neg_a[:, :], g.neg_a[:, :], -1.0).then_inc(derived, 1)


def phase_modulation(nc, sem, io, g):
    COLS = 512
    GROUPS = 6 * D // COLS
    cond_in, cond_ready, cond_high, cond_split = (sem("cond_in"), sem("cond_ready"), sem("cond_high"),
                                                  sem("cond_split"))
    full, copied, turned = sem("ada_full"), sem("ada_copied"), sem("ada_turned")
    x_in = sem("ada_x_in")
    with ExitStack() as ctx:
        cond = ctx.enter_context(nc.sbuf_tensor("cond", [P, KD, 2], F32))
        parts = ctx.enter_context(nc.sbuf_tensor("cond_parts", [P, KD, 4], F32R))
        raw = ctx.enter_context(nc.sbuf_tensor("ada_raw", [P, 2, KD * COLS], F32))
        total = SquareSum(nc, sem, ctx, "ada", g)
        rows = ctx.enter_context(nc.sbuf_tensor("ada_rows", [4, GROUPS, COLS], F32))
        weights = SplitWeights(nc, sem, ctx, "ada", GROUPS, KD * COLS, lambda n: io["w_ada"][n], raw, pieces=4)
        ps = ctx.enter_context(nc.psum_tensor("ada_ps", [4, 2, 512], F32))
        pt = ctx.enter_context(nc.psum_tensor("ada_pt", [P, 512], F32))
        block = ctx.enter_context(nc.Block())

        @block.sync
        def _(sp):
            sp.dma_start(cond[:, :, :], io["cond"]).then_inc(cond_in, 16)
            weights.load_all(sp)

        @block.scalar
        def _(act):
            act.dma_start(g.h[:, :, :], io["x_t"].rearrange("k p t -> p k t")).then_inc(x_in, 16)
            act.wait_ge(cond_in, 16)
            act.activation(cond[:, :, :], cond[:, :, :], ACT.Silu).then_inc(cond_ready, 1)
            act.wait_ge(cond_ready, 1)
            act.activation(parts[:, :, 0:2], cond[:, :, :], ACT.Copy).then_inc(cond_high, 1)

            def take(it, s):
                act.wait_ge(full, 2 * it + s + 1)
                act.activation(rows[:, bass.ds(2 * it + s, 1), :].squeeze(1), ps[:, s, :], ACT.Copy)\
                   .then_inc(copied, 1)

            weights.rounding(act, take)

        @block.gpsimd
        def _(pool):
            total.clear(pool)
            pool.wait_ge(x_in, 16)
            for k in range(KD):
                total.wait_slot(pool, k)
                pool.tensor_tensor(total.sq[:, k % 2, :], g.h[:, k, :], g.h[:, k, :], ALU.mult)\
                    .then_inc(total.squared, 1)
                if k > 0:
                    total.add(pool, k - 1, (k - 1) % 2)
            total.add(pool, KD - 1, (KD - 1) % 2)

        @block.tensor
        def _(pe):
            pe.wait_ge(cond_split, 1)

            def group(it, s):
                for n, w in enumerate(weights.parts(pe, it, s)):
                    for k in range(KD):
                        last = pe.matmul(ps[:, s, :], parts[:, k, :], w[:, COLS * k:COLS * k + COLS],
                                         start=(n == 0 and k == 0), stop=(n == 1 and k == KD - 1))
                last.then_inc(full, 1)

            group(0, 0)
            group(0, 1)
            with pe.Fori(1, GROUPS // 2) as it:
                for s in (0, 1):
                    pe.wait_ge(copied, 2 * it + s - 1)
                    group(it, s)
            pe.wait_ge(copied, GROUPS)
            flat = rows[:, :, :].rearrange("r g c -> r (g c)")
            for m in range(6 * KD):
                last = pe.matmul(pt[:, 2 * m:2 * m + 2], flat[:, P * m:P * m + P], g.sel[0:4, :],
                                 start=True, stop=True)
            last.then_inc(turned, 1)

        @block.vector
        def _(dve):
            dve.wait_ge(cond_high, 1)
            dve.tensor_tensor(parts[:, :, 2:4], cond[:, :, :], parts[:, :, 0:2].bitcast(F32), ALU.subtract)\
               .then_inc(cond_split, 1)
            weights.low_all(dve)
            dve.wait_ge(turned, 1)
            dve.tensor_tensor(g.mod[:, :, :].rearrange("p m c -> p (m c)"), pt[:, 0:12 * KD], g.v("b_ada"), ALU.add)


def phase_norm(nc, sem, g, tag, weight, shift_at, out, split=None, keep=False,
               store=None, then=None):
    low_done, stored = sem(tag + "_low_done"), sem(tag + "_stored")
    summed = sem(tag + "_summed")
    mean_done, inv_done, rstd_done, gained = (sem(tag + "_mean_done"), sem(tag + "_inv_done"),
                                              sem(tag + "_rstd_done"), sem(tag + "_gained"))
    scaled, rounded = sem(tag + "_scaled"), sem(tag + "_rounded")
    with ExitStack() as ctx:
        rstd = ctx.enter_context(nc.sbuf_tensor(tag + "_rstd", [P, T], F32))
        gain = ctx.enter_context(nc.sbuf_tensor(tag + "_gain", [P, KD, 2], F32))
        ps = ctx.enter_context(nc.psum_tensor(tag + "_ps", [P, 1024], F32))
        block = ctx.enter_context(nc.Block())

        @block.tensor
        def _(pe):
            for lo, hi in BANKS:
                last = pe.matmul(ps[:, lo:hi], g.ones, g.squares[:, lo:hi], start=True, stop=True)
            last.then_inc(summed, 1)

        @block.sync
        def _(sp):
            if then is not None:
                then.start(sp)
            if store is not None:
                for k in range(KD):
                    sp.wait_ge(scaled, k + 1)
                    sp.dma_start(store[k], out[:, k, :]).then_inc(stored, 16)
                sp.wait_ge(stored, 16 * KD)

        @block.scalar
        def _(act):
            act.wait_ge(inv_done, 1)
            act.activation(rstd[:, :], rstd[:, :], ACT.Sqrt).then_inc(rstd_done, 1)

            def shift(k):
                act.wait_ge(low_done, k + 1)
                for c, lo, hi in SEG:
                    act.activation(out[:, k, lo:hi], out[:, k, lo:hi], ACT.Identity,
                                   bias=g.mod[:, shift_at + k, c:c + 1])

            if shift_at is not None:
                for k in range(KD):
                    act.wait_ge(scaled, k + 1)
                    dst = out if split is None else split[0]
                    for c, lo, hi in SEG:
                        last = act.activation(dst[:, k, lo:hi], out[:, k, lo:hi], ACT.Identity,
                                              bias=g.mod[:, shift_at + k, c:c + 1])
                    last.then_inc(rounded, 1)
                    if keep and k > 0:
                        shift(k - 1)
                if keep:
                    shift(KD - 1)

        @block.vector
        def _(dve):
            if shift_at is not None:
                scale = g.mod[:, shift_at + KD:shift_at + 2 * KD, :]
                dve.scalar_tensor_tensor(out=gain[:, :, :], in0=scale, scalar=1.0,
                                         in1=weight.unsqueeze(2).to_broadcast([P, KD, 2]),
                                         op0=ALU.add, op1=ALU.mult).then_inc(gained, 1)
            else:
                dve.tensor_copy(gain[:, :, :], weight.unsqueeze(2).to_broadcast([P, KD, 2])).then_inc(gained, 1)
            dve.wait_ge(summed, 1)
            dve.tensor_scalar(rstd[:, :], ps[:, 0:T], 1.0 / D, 1e-6, ALU.mult, ALU.add).then_inc(mean_done, 1)
            dve.wait_ge(mean_done, 1)
            dve.reciprocal(rstd[:, :], rstd[:, :]).then_inc(inv_done, 1)
            dve.wait_ge(rstd_done, 1)
            dve.wait_ge(gained, 1)

            def low_part(k):
                dve.wait_ge(rounded, k + 1)
                for c, lo, hi in SEG:
                    last = dve.scalar_tensor_tensor(
                        out=split[1][:, k, lo:hi], in0=out[:, k, lo:hi], scalar=g.mod[:, shift_at + k, c:c + 1],
                        in1=split[0][:, k, lo:hi].bitcast(F32), op0=ALU.add, op1=ALU.subtract)
                last.then_inc(low_done, 1)

            for k in range(KD):
                for c, lo, hi in SEG:
                    last = dve.scalar_tensor_tensor(out=out[:, k, lo:hi], in0=g.x[:, k, lo:hi],
                                                    scalar=gain[:, k, c:c + 1], in1=rstd[:, lo:hi],
                                                    op0=ALU.mult, op1=ALU.mult)
                last.then_inc(scaled, 1)
                if split is not None and k > 0:
                    low_part(k - 1)
            if split is not None:
                low_part(KD - 1)


CONV_PAD = M_CONV // 2


def conv_rooms(spare):
    rooms, _ = offsets(dict(raw=2 * KD * P, pad=2 * (T + 3 * CONV_PAD), acc=2 * (T + CONV_PAD), res=2 * T))
    return [spare[:, lo:hi].rearrange("p (s n) -> p s n", s=2) for lo, hi in rooms.values()]


def phase_conv(nc, sem, io, g, h, spare, early, keep, tok):
    tag, n = "conv", KI + 2 * M_GROUPS
    SECTIONS = ((0, KI // 2, False, True), (KI // 2, (KI + M_GROUPS) // 2, True, True),
                ((KI + M_GROUPS) // 2, n // 2, True, False))
    TURNED = (KI + M_GROUPS) // 2
    psum_full, psum_free = sem(tag + "_psum_full"), sem(tag + "_psum_free")
    padded, pad_free, conv = sem(tag + "_padded"), sem(tag + "_pad_free"), sem(tag + "_conv_chain")
    conv_free, act_done, act_free = sem(tag + "_conv_free"), sem(tag + "_act_done"), sem(tag + "_act_free")
    tr_full, tr_free, kept = sem(tag + "_tr_full"), sem(tag + "_tr_free"), sem(tag + "_kept")
    PAD = CONV_PAD
    W_OUT = T + PAD
    PARTS = ((0, 0, CTX), (CTX + PAD, CTX, T))
    with ExitStack() as ctx:
        raw, pad, acc, res = conv_rooms(spare)
        weights = SplitWeights(nc, sem, ctx, tag, n, KD * P, early.source, raw, early)
        ps = ctx.enter_context(nc.psum_tensor(tag + "_ps", [P, 2, 1024], F32))
        pt = ctx.enter_context(nc.psum_tensor(tag + "_pt", [P, 2, 1024], F32))
        zeroed = sem(tag + "_pad_zeroed")
        block = ctx.enter_context(nc.Block())
        cw = g.v("conv_w").rearrange("p (j i) -> p j i", i=M_CONV)

        @block.sync
        def _(sp):
            weights.load_all(sp)

        @block.gpsimd
        def _(pool):
            pool.memset(pad[:, :, :], 0.0).then_inc(zeroed, 1)
            weights.low_all(pool)

        @block.tensor
        def _(pe):
            def tile(it, s):
                parts = weights.tile(pe, it, s)
                pe.wait_ge(psum_free, 2 * it + s + 1)
                project_split(pe, ps[:, s, :], parts, h, KD).then_inc(psum_full, 1)

            def turn(it, s):
                pe.wait_ge(act_done, 2 * it + s + 1)
                pe.wait_ge(tr_free, 2 * it + s + 1)
                for c in range(NCH):
                    last = pe.transpose(pt[:, s, P * c:P * c + P], res[:, s, P * c:P * c + P], g.ident)
                last.then_inc(tr_full, 1)

            tile(0, 0)
            tile(0, 1)
            with pe.Fori(0, TURNED) as it:
                for s in (0, 1):
                    tile(it + 1, s)
                    turn(it, s)
            with pe.Fori(TURNED + 1, n // 2) as it:
                for s in (0, 1):
                    tile(it, s)

        @block.scalar
        def _(act):
            act.sem_inc(psum_free, 2)
            act.sem_inc(conv_free, 2)
            act.wait_ge(zeroed, 1)
            for s in (0, 1):
                weights.round_tile(act, 0, s)

            def pair(it, more):
                for s in (0, 1):
                    act.wait_ge(psum_full, 2 * it + s + 1)
                    act.wait_ge(pad_free, 2 * it + s + 1)
                    for _, b, lo, hi in PIECES:
                        at = lo + (PAD if lo < CTX else 2 * PAD)
                        last = act.activation(pad[:, s, at:at + hi - lo],
                                              halves(ps[:, s, :])[:, b, lo - HALF * b:hi - HALF * b], ACT.Copy)
                    last.then_inc(padded, 1)
                    act.wait_ge(padded, 2 * it + s + 1)
                    act.sem_inc(psum_free, 1)
                    if more:
                        weights.round_tile(act, it + 1, s)
                for s in (0, 1):
                    act.wait_ge(conv, 2 * M_CONV * it + M_CONV * s + M_CONV)
                    act.wait_ge(act_free, 2 * it + s + 1)
                    for at, lo, hi in PARTS:
                        last = act.activation(res[:, s, lo:hi], acc[:, s, at:at + hi - lo], ACT.Silu,
                                              bias=g.v("conv_b")[:, bass.ds(2 * it + s, 1)])
                    last.then_inc(act_done, 1)
                    act.wait_ge(act_done, 2 * it + s + 1)
                    act.sem_inc(conv_free, 1)

            with act.Fori(0, n // 2 - 1) as it:
                pair(it, True)
            pair(n // 2 - 1, False)

        @block.vector
        def _(dve):
            dve.sem_inc(pad_free, 2)
            dve.sem_inc(tr_free, 2)
            dve.sem_inc(act_free, 2)

            def pair(it, keeps, turns):
                for s in (0, 1):
                    dve.wait_ge(padded, 2 * it + s + 1)
                    dve.wait_ge(conv_free, 2 * it + s + 1)
                    for i in range(M_CONV):
                        src, wi = pad[:, s, i:i + W_OUT], cw[:, bass.ds(2 * it + s, 1), i]
                        if i == 0:
                            dve.tensor_scalar(acc[:, s, :], src, wi, None, ALU.mult).then_inc(conv, 1)
                        else:
                            dve.wait_ge(conv, 2 * M_CONV * it + M_CONV * s + i)
                            dve.scalar_tensor_tensor(out=acc[:, s, :], in0=src, scalar=wi, in1=acc[:, s, :],
                                                     op0=ALU.mult, op1=ALU.add).then_inc(conv, 1)
                    dve.wait_ge(conv, 2 * M_CONV * it + M_CONV * s + M_CONV)
                    dve.sem_inc(pad_free, 1)
                for s in (0, 1):
                    if keeps:
                        dve.wait_ge(act_done, 2 * it + s + 1)
                        dve.tensor_copy(keep[:, bass.ds(2 * it + s - KI, 1), :].squeeze(1),
                                        res[:, s, :]).then_inc(kept, 1)
                        dve.wait_ge(kept, 2 * it + s + 1 - KI)
                    if turns:
                        dve.wait_ge(tr_full, 2 * it + s + 1)
                        dve.tensor_copy(tok[:, :, bass.ds((2 * it + s) * P, P)],
                                        pt[:, s, 0:T].rearrange("p (c m) -> p c m", m=P)).then_inc(tr_free, 1)
                    dve.sem_inc(act_free, 1)

            for lo, hi, keeps, turns in SECTIONS:
                with dve.Fori(lo, hi) as it:
                    pair(it, keeps, turns)


DT_PARTS = ("dt", "da", "cs", "ecs", "edec", "etot")


def phase_dt(nc, sem, io, g, dts):
    rows_full, rows_ready, rows_out = sem("dt_rows_full"), sem("dt_rows_ready"), sem("dt_rows_out")
    w_in, raw_full, cum_full = sem("dt_w_in"), sem("dt_raw_full"), sem("dt_cum_full")
    vec, act_done = sem("dt_vec"), sem("dt_act")
    N = NCH * 64
    SERIES = [1.0 / n for n in (13, 11, 9, 7, 5, 3)]
    with ExitStack() as ctx:
        w = ctx.enter_context(nc.sbuf_tensor("dt_w", [P, KD, 64], F32))
        raw = ctx.enter_context(nc.sbuf_tensor("dt_raw", [P, NCH, 64], F32))
        e = ctx.enter_context(nc.sbuf_tensor("dt_e", [P, NCH, 64], F32))
        s2 = ctx.enter_context(nc.sbuf_tensor("dt_s2", [P, NCH, 64], F32))
        q = ctx.enter_context(nc.sbuf_tensor("dt_q", [P, NCH, 64], F32))
        pr = ctx.enter_context(nc.psum_tensor("dt_pr", [P, 512], F32))
        pc = ctx.enter_context(nc.psum_tensor("dt_pc", [P, 512], F32))
        pt = ctx.enter_context(nc.psum_tensor("dt_pt", [P, 512], F32))
        prow = ctx.enter_context(nc.psum_tensor("dt_prow", [P, NCH, P], F32))
        rows = ctx.enter_context(nc.sbuf_tensor("dt_rows", [64, NCH, P], F32))
        block = ctx.enter_context(nc.Block())
        view = lambda p: p[:, 0:N].rearrange("p (c n) -> p c n", n=64)
        over_chunks = lambda r: r.unsqueeze(1).to_broadcast([P, NCH, 64])

        @block.sync
        def _(sp):
            sp.dma_start(w[:, :, :], io["w_dt"].rearrange("p (k n) -> p k n", n=64)).then_inc(w_in, 16)
            sp.wait_ge(rows_ready, 1)
            sp.dma_start(io["cs_rows"].rearrange("c n t -> n c t"), rows[:, :, :]).then_inc(rows_out, 16)
            sp.wait_ge(rows_out, 16)

        @block.tensor
        def _(pe):
            pe.wait_ge(w_in, 16)
            for c in range(NCH):
                for k in range(KD):
                    last = pe.matmul(pr[:, 64 * c:64 * c + 64], g.h[:, k, P * c:P * c + P], w[:, k, :],
                                     start=(k == 0), stop=(k == KD - 1))
            last.then_inc(raw_full, 1)
            pe.wait_ge(vec, DA_DONE)
            for d in (0, 1):
                half = slice(32 * d, 32 * d + 32)
                pe.matmul(view(pc)[:, :, half], g.tri[:, d, :], dts["da"][:, :, half], start=True, stop=True)
            pe.matmul(view(pt), g.ones, dts["da"][:, :, :], start=True, stop=True).then_inc(cum_full, 1)
            pe.wait_ge(vec, DA_DONE + 1)
            for c in range(NCH):
                last = pe.transpose(prow[0:64, c, :], dts["cs"][:, c, :], g.ident)
            last.then_inc(rows_full, 1)

        steps = [0]

        @block.vector
        def _(dve):
            def then(ins):
                steps[0] += 1
                ins.then_inc(vec, 1)
                dve.wait_ge(vec, steps[0])

            dve.wait_ge(raw_full, 1)
            then(dve.tensor_tensor(raw[:, :, :], view(pr), over_chunks(g.r("dt_bias")), ALU.add))
            dve.wait_ge(act_done, 2)
            then(dve.tensor_scalar(q[:, :, :], e[:, :, :], 2.0, None, ALU.add))
            then(dve.reciprocal(q[:, :, :], q[:, :, :]))
            then(dve.tensor_tensor(e[:, :, :], e[:, :, :], q[:, :, :], ALU.mult))
            then(dve.tensor_tensor(s2[:, :, :], e[:, :, :], e[:, :, :], ALU.mult))
            then(dve.tensor_scalar(q[:, :, :], s2[:, :, :], SERIES[0], None, ALU.mult))
            for c in SERIES[1:]:
                then(dve.scalar_tensor_tensor(out=q[:, :, :], in0=q[:, :, :], scalar=c, in1=s2[:, :, :],
                                              op0=ALU.add, op1=ALU.mult))
            then(dve.scalar_tensor_tensor(out=q[:, :, :], in0=q[:, :, :], scalar=1.0, in1=e[:, :, :],
                                          op0=ALU.add, op1=ALU.mult))
            then(dve.tensor_scalar(q[:, :, :], q[:, :, :], 2.0, None, ALU.mult))
            then(dve.scalar_tensor_tensor(out=dts["dt"][:, :, :], in0=raw[:, :, :], scalar=0.0, in1=q[:, :, :],
                                          op0=ALU.max, op1=ALU.add))
            then(dve.tensor_tensor(dts["da"][:, :, :], dts["dt"][:, :, :], over_chunks(g.neg_a[:, :]), ALU.mult))
            assert steps[0] == DA_DONE
            dve.wait_ge(cum_full, 1)
            then(dve.tensor_copy(dts["cs"][:, :, :], view(pc)))
            then(dve.tensor_copy(dts["etot"][:, :, :], view(pt)))
            then(dve.tensor_tensor(dts["edec"][:, :, :], dts["etot"][:, :, :], dts["cs"][:, :, :], ALU.subtract))
            dve.wait_ge(rows_full, 1)
            dve.tensor_copy(rows[:, :, :], prow[0:64, :, :]).then_inc(rows_ready, 1)
            dve.wait_ge(act_done, 3)
            then(dve.tensor_tensor(dts["edec"][:, :, :], dts["edec"][:, :, :], dts["dt"][:, :, :], ALU.mult))

        @block.scalar
        def _(act):
            act.wait_ge(vec, 1)
            act.activation(e[:, :, :], raw[:, :, :], ACT.Abs).then_inc(act_done, 1)
            act.wait_ge(act_done, 1)
            act.activation(e[:, :, :], e[:, :, :], ACT.Exp, scale=-1.0).then_inc(act_done, 1)
            act.wait_ge(vec, DA_DONE + 3)
            act.activation(dts["ecs"][:, :, :], dts["cs"][:, :, :], ACT.Exp)
            act.activation(dts["etot"][:, :, :], dts["etot"][:, :, :], ACT.Exp)
            act.activation(dts["edec"][:, :, :], dts["edec"][:, :, :], ACT.Exp).then_inc(act_done, 1)


DA_DONE = 15


def phase_ssd(nc, sem, io, g, dts, x_tok, b_chan, c_chan, b_tok, y_tok):
    UNITS = 2 * NCH
    chunk = lambda u: 0 if u < 2 else (u // 2 if u % 2 == 0 else NCH - u // 2)
    with_state = lambda u: u >= 2
    makes_state = lambda u: u < UNITS - 2
    s_in, s_out = [sem("s_in0"), sem("s_in1")], [sem("s_out0"), sem("s_out1")]
    mats_ready, y_init = sem("ssd_mats_ready"), sem("ssd_y_init")
    row_in = [sem("ssd_row_in0"), sem("ssd_row_in1")]
    dist_done, decay_done = sem("ssd_dist_done"), sem("ssd_decay_done")
    cb_full, cb_done, m_done = sem("ssd_cb_full"), sem("ssd_cb_done"), sem("ssd_m_done")
    xdt_done, xdec_done, sdec_done = sem("ssd_xdt_done"), sem("ssd_xdec_done"), sem("ssd_sdec_done")
    st_full, s_done = sem("ssd_st_full"), sem("ssd_s_done")
    off_full, off_done, diag_full, y_new = (sem("ssd_off_full"), sem("ssd_off_done"), sem("ssd_diag_full"),
                                            sem("ssd_y_new"))
    y_added, pool_go = sem("ssd_y_added"), sem("ssd_pool_go")
    with ExitStack() as ctx:
        sb = lambda n, shape: ctx.enter_context(nc.sbuf_tensor("ssd_" + n, shape, F32))
        pb = lambda n, shape: ctx.enter_context(nc.psum_tensor("ssd_" + n, shape, F32))
        ct, bt, bk = sb("ct", [P, T]), sb("bt", [P, T]), sb("bk", [P, NCH, M_STATE])
        row = sb("row", [P, 2, HPG * P])
        m = sb("m", [P, 2, HPG, P])
        cb = sb("cb", [P, 2, P])
        xdt, xdec, yn = sb("xdt", [P, 2, GI]), sb("xdec", [P, 2, GI]), sb("yn", [P, 2, GI])
        off, sdec = sb("off", [P, 2, GI]), sb("sdec", [P, GI])
        s_ctx, s_lat = sb("s_ctx", [P, 2, GI]), sb("s_lat", [P, 2, GI])
        p_cb, p_diag, p_off, p_st = (pb(n, [P, 2, 512]) for n in ("p_cb", "p_diag", "p_off", "p_st"))
        block = ctx.enter_context(nc.Block())
        heads = lambda a: a.rearrange("p (e f) -> p e f", f=HD)
        group_heads = lambda gi, u: bass.ds(HPG * gi + M_HEADS * (u % 2), HPG)
        per_head = lambda n, gi, u: dts[n][:, chunk(u), group_heads(gi, u)].unsqueeze(2).to_broadcast([P, HPG, HD])
        ONE, TWO = 1, 2

        @block.sync
        def _(sp):
            for d in (0, 1):
                sp.dma_start(s_lat[:, d, :], io["ssm_in"][d, 0]).then_inc(s_in[d], 16)

            def rows(gi, us):
                for u in us:
                    sp.wait_ge(dist_done, UNITS * gi + u + 1)
                    src = io["cs_rows"][chunk(u), bass.ds(HPG * gi + M_HEADS * (u % 2), HPG), :]
                    sp.dma_start(row[:, u % 2, :], src.rearrange("e t -> (e t)").unsqueeze(0)
                                 .to_broadcast([P, HPG * P])).then_inc(row_in[u % 2], 16)

            def context_out(gi):
                for d in (0, 1):
                    sp.wait_ge(s_done, 8 * gi + d + 1 + TWO)
                    sp.dma_start(io["ssm_out"][d, bass.ds(gi, 1)].squeeze(0), s_ctx[:, d, :]).then_inc(s_out[d], 16)

            with sp.Fori(0, M_GROUPS - 1) as gi:
                rows(gi, range(0, 5))
                context_out(gi)
                rows(gi, range(5, UNITS))
                sp.wait_ge(off_full, 8 * gi + 8)
                for d in (0, 1):
                    sp.dma_start(s_lat[:, d, :], io["ssm_in"][d, bass.ds(gi + 1, 1)].squeeze(0)).then_inc(s_in[d], 16)
            rows(M_GROUPS - 1, range(0, 5))
            context_out(M_GROUPS - 1)
            rows(M_GROUPS - 1, range(5, UNITS))
            for d in (0, 1):
                sp.wait_ge(s_out[d], 16 * M_GROUPS + 16)

        @block.gpsimd
        def _(pool):
            pool.sem_inc(y_added, TWO)
            with pool.Fori(0, M_GROUPS) as gi:
                pool.wait_ge(diag_full, UNITS * gi + TWO)
                pool.wait_ge(y_new, UNITS * gi + TWO)
                for c in range(NCH):
                    last = pool.tensor_tensor(
                        heads(y_tok[:, c, bass.ds(gi * GI, GI)]), heads(x_tok[:, c, bass.ds(gi * GI, GI)]),
                        g.r("d_skip")[:, bass.ds(gi * HPG, HPG)].unsqueeze(2).to_broadcast([P, HPG, HD]), ALU.mult)
                last.then_inc(y_init, 1)

                def add_y(u):
                    n = UNITS * gi + u
                    pool.wait_ge(y_init, gi + 1)
                    pool.wait_ge(y_new, n + 1 + TWO)
                    pool.wait_ge(y_added, n + TWO)
                    pool.sem_inc(pool_go, 1)
                    y = y_tok[:, chunk(u), bass.ds(gi * GI, GI)]
                    pool.tensor_tensor(y, y, yn[:, u % 2, :], ALU.add).then_inc(y_added, 1)

                for u in range(UNITS):
                    n, d, i = UNITS * gi + u, u % 2, 8 * gi + u
                    pool.wait_ge(diag_full, n + 1)
                    pool.sem_inc(pool_go, 1)
                    x = heads(x_tok[:, chunk(u), bass.ds(gi * GI, GI)])
                    pool.tensor_tensor(heads(xdt[:, d, :]), x, per_head("dt", gi, u), ALU.mult).then_inc(xdt_done, 1)
                    if makes_state(u):
                        pool.tensor_tensor(heads(xdec[:, d, :]), x, per_head("edec", gi, u), ALU.mult).then_inc(xdec_done, 1)
                    if u >= 2:
                        add_y(u - 2)
                add_y(UNITS - 2)
                add_y(UNITS - 1)

        @block.scalar
        def _(act):
            act.sem_inc(dist_done, TWO)
            with act.Fori(0, M_GROUPS) as gi:
                act.wait_ge(diag_full, UNITS * gi + TWO)
                act.activation(ct[:, :], c_chan[:, bass.ds(gi, 1), :].squeeze(1), ACT.Copy)
                act.activation(bt[:, :], b_chan[:, bass.ds(gi, 1), :].squeeze(1), ACT.Copy)
                act.activation(bk[:, :, :], b_tok[:, :, bass.ds(gi * M_STATE, M_STATE)], ACT.Copy)\
                   .then_inc(mats_ready, 1)
                for u in range(UNITS):
                    n = UNITS * gi + u
                    act.wait_ge(row_in[u % 2], 16 * (UNITS // 2) * gi + 16 * (u // 2 + 1))
                    act.wait_ge(diag_full, n + 1)
                    for e in range(HPG):
                        last = act.activation(m[:, u % 2, e, :], row[:, u % 2, P * e:P * e + P], ACT.Relu, scale=-1.0,
                                              bias=dts["cs"][:, chunk(u), bass.ds(HPG * gi + M_HEADS * (u % 2) + e, 1)])
                    last.then_inc(dist_done, 1)
                    act.wait_ge(dist_done, n + 1 + TWO)
                    act.activation(m[:, u % 2, :, :], m[:, u % 2, :, :], ACT.Exp, scale=-1.0)\
                       .then_inc(decay_done, 1)

        @block.tensor
        def _(pe):
            pe.sem_inc(diag_full, TWO)
            with pe.Fori(0, M_GROUPS) as gi:
                pe.wait_ge(mats_ready, gi + 1)

                def products(u):
                    span = slice(P * chunk(u), P * chunk(u) + P)
                    pe.wait_ge(cb_done, UNITS * gi + u + 1)
                    pe.matmul(p_cb[:, u % 2, 0:P], bt[:, span], ct[:, span], start=True, stop=True).then_inc(cb_full, 1)

                products(0)
                for u in range(UNITS):
                    n, d, i = UNITS * gi + u, u % 2, 8 * gi + u
                    span = slice(P * chunk(u), P * chunk(u) + P)
                    if u + 1 < UNITS:
                        products(u + 1)
                    if with_state(u):
                        if u < 4:
                            pe.wait_ge(s_in[d], 16 * gi + 16)
                        else:
                            pe.wait_ge(s_done, i - 1 + TWO)
                        pe.wait_ge(off_done, 8 * gi + u - 2 + 1)
                        pe.matmul(p_off[:, d, :], ct[:, span], s_lat[:, d, :], start=True, stop=True)\
                          .then_inc(off_full, 1)
                    if makes_state(u):
                        pe.wait_ge(xdec_done, i + 1)
                        pe.wait_ge(s_done, i + 1)
                        pe.matmul(p_st[:, d, :], bk[:, chunk(u), :], xdec[:, d, :], start=True, stop=True)\
                          .then_inc(st_full, 1)
                    pe.wait_ge(xdt_done, n + 1)
                    pe.wait_ge(m_done, n + 1)
                    pe.wait_ge(y_new, n + 1)
                    for e in range(HPG):
                        last = pe.matmul(p_diag[:, d, HD * e:HD * e + HD], m[:, d, e, :],
                                         xdt[:, d, HD * e:HD * e + HD], start=True, stop=True)
                    last.then_inc(diag_full, 1)

        @block.vector
        def _(dve):
            dve.sem_inc(cb_done, TWO)
            dve.sem_inc(off_done, TWO)
            dve.sem_inc(s_done, TWO)
            dve.sem_inc(y_new, TWO)
            for d in (0, 1):
                dve.sem_inc(s_out[d], 16)
            with dve.Fori(0, M_GROUPS) as gi:

                def sum_up(u):
                    n, d = UNITS * gi + u, u % 2
                    dve.wait_ge(diag_full, n + 1 + TWO)
                    dve.wait_ge(y_added, n + 1)
                    if with_state(u):
                        dve.wait_ge(off_done, 8 * gi + u - 1 + TWO)
                        dve.tensor_tensor(yn[:, d, :], off[:, d, :], p_diag[:, d, :], ALU.add).then_inc(y_new, 1)
                    else:
                        dve.tensor_copy(yn[:, d, :], p_diag[:, d, :]).then_inc(y_new, 1)

                for u in range(UNITS):
                    n, d, i = UNITS * gi + u, u % 2, 8 * gi + u
                    dve.wait_ge(cb_full, n + 1)
                    dve.wait_ge(y_new, n + 1)
                    dve.tensor_tensor(cb[:, d, :], p_cb[:, d, 0:P], g.tri[:, d, :], ALU.mult).then_inc(cb_done, 1)
                    if makes_state(u) and with_state(u):
                        if u < 4:
                            dve.wait_ge(s_in[d], 16 * gi + 16)
                        dve.wait_ge(s_done, i + TWO)
                        dve.tensor_tensor(heads(sdec[:, :]), heads(s_lat[:, d, :]), per_head("etot", gi, u),
                                          ALU.mult).then_inc(sdec_done, 1)
                    dve.wait_ge(cb_done, n + 1 + TWO)
                    dve.wait_ge(decay_done, n + 1)
                    dve.tensor_tensor(m[:, d, :, :], m[:, d, :, :],
                                      cb[:, d, :].unsqueeze(1).to_broadcast([P, HPG, P]), ALU.mult).then_inc(m_done, 1)
                    if with_state(u):
                        dve.wait_ge(off_full, 8 * gi + u - 1)
                        dve.wait_ge(y_new, n - 2 + TWO + 1)
                        dve.tensor_tensor(heads(off[:, d, :]), heads(p_off[:, d, :]), per_head("ecs", gi, u),
                                          ALU.mult).then_inc(off_done, 1)
                    if makes_state(u):
                        dve.wait_ge(st_full, i + 1)
                        if with_state(u):
                            dve.wait_ge(sdec_done, 6 * gi + u - 1)
                            dve.tensor_tensor(s_lat[:, d, :], sdec[:, :], p_st[:, d, :], ALU.add).then_inc(s_done, 1)
                        else:
                            dve.wait_ge(s_out[d], 16 * gi + 16)
                            dve.tensor_copy(s_ctx[:, d, :], p_st[:, d, :]).then_inc(s_done, 1)
                    if u:
                        sum_up(u - 1)
                sum_up(UNITS - 1)


def phase_m_gate(nc, sem, io, g, y_tok, y_chan, then):
    w_in = [sem("z_w_in0"), sem("z_w_in1")]
    z_full, z_done, gated = sem("z_full"), sem("z_done"), sem("z_gated")
    sum_done, mean_done, root_done, inv_done = sem("z_sum_done"), sem("z_mean_done"), sem("z_root_done"), sem("z_inv")
    normed, tr_full, tr_done = sem("z_normed"), sem("z_tr_full"), sem("z_tr_done")
    SUB = GI // P
    with ExitStack() as ctx:
        sb = lambda n, shape: ctx.enter_context(nc.sbuf_tensor("z_" + n, shape, F32))
        w = sb("w", [P, 2, KD * GI])
        z, sq = sb("z", [P, 2, GI]), sb("sq", [P, GI])
        ms = sb("ms", [P, 2, 1])
        pz = ctx.enter_context(nc.psum_tensor("z_pz", [P, 2, 512], F32))
        pt = ctx.enter_context(nc.psum_tensor("z_pt", [P, 2, 512], F32))
        block = ctx.enter_context(nc.Block())
        units = [(q, c) for q in range(M_GROUPS) for c in range(NCH)]

        @block.sync
        def _(sp):
            for q in range(M_GROUPS):
                if q >= 2:
                    sp.wait_ge(z_full, NCH * (q - 1))
                sp.dma_start(w[:, q % 2, :], io["w_z"][q]).then_inc(w_in[q % 2], 16)
            then.start(sp)

        @block.tensor
        def _(pe):
            def turn(n):
                q, c = units[n]
                pe.wait_ge(normed, n + 1)
                if n >= 2:
                    pe.wait_ge(tr_done, n - 1)
                for j in range(SUB):
                    at = GI * q + P * j
                    last = pe.transpose(pt[:, n % 2, P * j:P * j + P], y_tok[:, c, at:at + P], g.ident)
                last.then_inc(tr_full, 1)

            for n, (q, c) in enumerate(units):
                pe.wait_ge(w_in[q % 2], 16 * (q // 2 + 1))
                if n >= 2:
                    pe.wait_ge(z_done, n - 1)
                for k in range(KD):
                    last = pe.matmul(pz[:, n % 2, :], g.h[:, k, P * c:P * c + P],
                                     w[:, q % 2, GI * k:GI * k + GI], start=(k == 0), stop=(k == KD - 1))
                last.then_inc(z_full, 1)
                if n >= 1:
                    turn(n - 1)
            turn(len(units) - 1)

        @block.scalar
        def _(act):
            for n in range(len(units)):
                act.wait_ge(z_full, n + 1)
                if n >= 2:
                    act.wait_ge(gated, n - 1)
                act.activation(z[:, n % 2, :], pz[:, n % 2, :], ACT.Silu).then_inc(z_done, 1)
                act.wait_ge(inv_done, n + 1)
                act.activation(ms[:, n % 2, :], ms[:, n % 2, :], ACT.Sqrt).then_inc(root_done, 1)

        @block.vector
        def _(dve):
            for n, (q, c) in enumerate(units):
                y = y_tok[:, c, GI * q:GI * q + GI]
                dve.wait_ge(z_done, n + 1)
                dve.tensor_tensor(y, y, z[:, n % 2, :], ALU.mult).then_inc(gated, 1)
                dve.wait_ge(gated, n + 1)
                dve.tensor_tensor_reduce(out=sq[:, :], in0=y, in1=y, scale=1.0, scalar=0.0, op0=ALU.mult,
                                         op1=ALU.add, accum_out=ms[:, n % 2, :]).then_inc(sum_done, 1)
                dve.wait_ge(sum_done, n + 1)
                dve.tensor_scalar(ms[:, n % 2, :], ms[:, n % 2, :], 1.0 / GI, 1e-5, ALU.mult, ALU.add)\
                   .then_inc(mean_done, 1)
                dve.wait_ge(mean_done, n + 1)
                dve.reciprocal(ms[:, n % 2, :], ms[:, n % 2, :]).then_inc(inv_done, 1)
                dve.wait_ge(root_done, n + 1)
                dve.tensor_scalar(y, y, ms[:, n % 2, :], None, ALU.mult).then_inc(normed, 1)
                dve.wait_ge(tr_full, n + 1)
                dve.tensor_tensor(y_chan[:, SUB * q:SUB * q + SUB, P * c:P * c + P],
                                  pt[:, n % 2, :].rearrange("p (j t) -> p j t", t=P),
                                  g.v("m_norm")[:, SUB * q:SUB * q + SUB].unsqueeze(2).to_broadcast([P, SUB, P]),
                                  ALU.mult).then_inc(tr_done, 1)


def phase_m_out(nc, sem, io, g, y, early):
    w_in, w = early.w_in, early.raw
    out_full, gate_full, gate_done, done = sem("m_out_full"), sem("m_gate_full"), sem("m_gate_done"), sem("m_done")
    with ExitStack() as ctx:
        gate = ctx.enter_context(nc.sbuf_tensor("m_gate", [P, 2, T], F32))
        po = ctx.enter_context(nc.psum_tensor("m_po", [P, 2, 1024], F32))
        pg = ctx.enter_context(nc.psum_tensor("m_pg", [P, 2, 1024], F32))
        block = ctx.enter_context(nc.Block())

        @block.sync
        def _(sp):
            stream(sp, KD, lambda it, s: sp.dma_start(w[:, s, :], io["w_m"][2 * it + s]).then_inc(w_in[s], 16),
                   used=out_full)

        @block.tensor
        def _(pe):
            with pe.Fori(0, KD // 2) as it:
                for s in (0, 1):
                    n = 2 * it + s
                    wt = tiles_of(w[:, s, :])
                    pe.wait_ge(w_in[s], 16 * it + 16)
                    pe.wait_ge(gate_done, n + 1)
                    project_halves(pe, pg[:, s, :], wt[:, KI:, :], g.h, KD).then_inc(gate_full, 1)
                    pe.wait_ge(done, n + 1)
                    project_halves(pe, po[:, s, :], wt[:, :KI, :], y, KI).then_inc(out_full, 1)

        @block.scalar
        def _(act):
            act.sem_inc(gate_done, 2)
            with act.Fori(0, KD // 2) as it:
                for s in (0, 1):
                    n = 2 * it + s
                    act.wait_ge(gate_full, n + 1)
                    act.wait_ge(done, n + 1)
                    act.activation(by_half(gate[:, s, :]), halves(pg[:, s, :]), ACT.Sigmoid).then_inc(gate_done, 1)

        @block.vector
        def _(dve):
            dve.sem_inc(done, 2)
            with dve.Fori(0, KD // 2) as it:
                for s in (0, 1):
                    n = 2 * it + s
                    dve.wait_ge(gate_done, n + 3)
                    dve.wait_ge(out_full, n + 1)
                    mix = g.mix[:, bass.ds(n, 1), :].squeeze(1)
                    dve.tensor_tensor(by_half(mix), by_half(gate[:, s, :]), halves(po[:, s, :]), ALU.mult)\
                       .then_inc(done, 1)


def phase_r_out(nc, sem, io, g, y, mix, early, then):
    gate_in = [sem("r_gate_in0"), sem("r_gate_in1")]
    full, done, scaled, rounded = sem("r_full"), sem("r_done"), sem("r_scaled"), sem("r_rounded")
    x_in = sem("r_x_in")
    with ExitStack() as ctx:
        weights = SplitWeights(nc, sem, ctx, "r", KD, KD * P, early.source, early.raw, early)
        gate = g.h
        ps = ctx.enter_context(nc.psum_tensor("r_ps", [P, 2, 1024], F32))
        block = ctx.enter_context(nc.Block())

        @block.sync
        def _(sp):
            for k in (0, 1):
                half = slice(KD // 2 * k, KD // 2 * (k + 1))
                sp.dma_start(gate[:, half, :], io["gate_r"][half].rearrange("k p t -> p k t")).then_inc(gate_in[k], 16)
            then.start(sp)
            weights.load_all(sp)
            sp.dma_start(g.x[:, :, :], io["x_t"].rearrange("k p t -> p k t")).then_inc(x_in, 16)
            sp.wait_ge(x_in, 16)

        @block.gpsimd
        def _(pool):
            weights.low_all(pool)

        @block.scalar
        def _(act):
            for s in (0, 1):
                weights.round_tile(act, 0, s)
            for n in range(KD):
                act.wait_ge(full, n + 1)
                if n + 2 < KD:
                    weights.round_tile(act, n // 2 + 1, n % 2)
                act.wait_ge(done, n + 1)
                act.activation(mix[0][:, n, :], g.mix[:, n, :], ACT.Copy).then_inc(rounded, 1)

        @block.tensor
        def _(pe):
            for n in range(KD):
                parts = weights.tile(pe, n // 2, n % 2)
                if n >= 2:
                    pe.wait_ge(scaled, n - 1)
                project_split(pe, ps[:, n % 2, :], parts, y, KD).then_inc(full, 1)

        @block.vector
        def _(dve):
            for k in (0, 1):
                dve.wait_ge(gate_in[k], 16)
            for n in range(KD):
                dve.wait_ge(full, n + 1)
                dve.tensor_tensor(by_half(gate[:, n, :]), by_half(gate[:, n, :]), halves(ps[:, n % 2, :]),
                                  ALU.mult).then_inc(scaled, 1)
                dve.wait_ge(scaled, n + 1)
                dve.tensor_tensor(g.mix[:, n, :], g.mix[:, n, :], gate[:, n, :], ALU.add).then_inc(done, 1)
                dve.wait_ge(rounded, n + 1)
                dve.tensor_tensor(mix[1][:, n, :], g.mix[:, n, :], mix[0][:, n, :].bitcast(F32), ALU.subtract)


def phase_residual(nc, sem, g, tag, early, rhs, k_tiles, gate_at, then=None, squares=False):
    full, done = sem(tag + "_full"), sem(tag + "_done")
    with ExitStack() as ctx:
        weights = SplitWeights(nc, sem, ctx, tag, KD, k_tiles * P, early.source, early.raw, early)
        if squares:
            total = SquareSum(nc, sem, ctx, tag, g)
        ps = ctx.enter_context(nc.psum_tensor(tag + "_ps", [P, 2, 1024], F32))
        block = ctx.enter_context(nc.Block())

        @block.sync
        def _(sp):
            if then is not None:
                then.start(sp)
            weights.load_all(sp)

        @block.gpsimd
        def _(pool):
            weights.low_all(pool)

        @block.scalar
        def _(act):
            weights.round_tile(act, 0, 0)
            weights.round_tile(act, 0, 1)
            for n in range(KD):
                act.wait_ge(full, n + 1)
                if n + 2 < KD:
                    weights.round_tile(act, n // 2 + 1, n % 2)
                if squares:
                    total.wait_slot(act, n)
                    act.wait_ge(done, n + 1 + 2)
                    act.activation(total.sq[:, n % 2, :], g.x[:, n, :], ACT.Square).then_inc(total.squared, 1)

        @block.tensor
        def _(pe):
            with pe.Fori(0, KD // 2) as it:
                for s in (0, 1):
                    parts = weights.tile(pe, it, s)
                    pe.wait_ge(done, 2 * it + s + 1)
                    project_split(pe, ps[:, s, :], parts, rhs, k_tiles).then_inc(full, 1)

        @block.vector
        def _(dve):
            dve.sem_inc(done, 2)
            if squares:
                total.clear(dve)
            with dve.Fori(0, KD // 2) as it:
                for s in (0, 1):
                    dve.wait_ge(full, 2 * it + s + 1)
                    for c, b, lo, hi in PIECES:
                        x = g.x[:, bass.ds(2 * it + s, 1), lo:hi].squeeze(1)
                        last = dve.scalar_tensor_tensor(
                            out=x, in0=halves(ps[:, s, :])[:, b, lo - HALF * b:hi - HALF * b], in1=x,
                            op0=ALU.mult, op1=ALU.add, scalar=g.mod[:, bass.ds(2 * it + s + gate_at, 1), c])
                    last.then_inc(done, 1)
                    if squares:
                        total.add(dve, 2 * it + s, s)


def phase_up(nc, sem, g, tag, tiles, h, spare, early, hidden, then):
    full, silu_done, done = [sem(tag + "_g_full"), sem(tag + "_u_full")], sem(tag + "_silu_done"), sem(tag + "_done")
    rounded = sem(tag + "_rounded")
    silu, plain = spare
    with ExitStack() as ctx:
        weights = SplitWeights(nc, sem, ctx, tag, 2 * tiles, KD * P, early.source, early.raw, early)
        ps = ctx.enter_context(nc.psum_tensor(tag + "_ps", [P, 2, 2, 1024], F32))
        block = ctx.enter_context(nc.Block())

        @block.sync
        def _(sp):
            if then is not None:
                then.start(sp)
            weights.load_all(sp)

        @block.gpsimd
        def _(pool):
            weights.low_all(pool)

        @block.tensor
        def _(pe):
            for n in range(tiles):
                for s, free in ((0, silu_done), (1, done)):
                    parts = weights.tile(pe, n, s)
                    if n >= 2:
                        pe.wait_ge(free, n - 1)
                    project_split(pe, ps[:, s, n % 2, :], parts, h, KD).then_inc(full[s], 1)

        @block.scalar
        def _(act):
            for s in (0, 1):
                weights.round_tile(act, 0, s)
            for n in range(tiles):
                act.wait_ge(full[0], n + 1)
                if n + 1 < tiles:
                    weights.round_tile(act, n + 1, 0)
                if n >= 2:
                    act.wait_ge(done, n - 1)
                act.activation(by_half(silu[:, n % 2, :]), halves(ps[:, 0, n % 2, :]), ACT.Silu)\
                   .then_inc(silu_done, 1)
                act.wait_ge(full[1], n + 1)
                if n + 1 < tiles:
                    weights.round_tile(act, n + 1, 1)
                act.wait_ge(done, n + 1)
                act.activation(hidden[0][:, n, :], plain[:, n % 2, :], ACT.Copy).then_inc(rounded, 1)

        @block.vector
        def _(dve):
            for n in range(tiles):
                dve.wait_ge(silu_done, n + 1)
                dve.wait_ge(full[1], n + 1)
                dve.tensor_tensor(by_half(plain[:, n % 2, :]), by_half(silu[:, n % 2, :]),
                                  halves(ps[:, 1, n % 2, :]), ALU.mult).then_inc(done, 1)
                dve.wait_ge(rounded, n + 1)
                dve.tensor_tensor(hidden[1][:, n, :], plain[:, n % 2, :], hidden[0][:, n, :].bitcast(F32),
                                  ALU.subtract)


R_TILES, W_TILE, K_TILES, V_TILES, A_TILE, G_TILE = range(0, 8), 8, range(9, 17), range(17, 25), 25, 26


def quarters_of(tiles):
    return sorted({ch // QUARTER for m in tiles for ch in (P * m, P * m + P - 1)})


def shifted_views(q, dst, src):
    before = q % 2 == 0
    far, near = slice(1, CTX), slice(0, CTX - 1)
    context = (dst[:, far], src[:, near]) if before else (dst[:, near], src[:, far])
    if q < 2:
        grid = lambda a: a[:, CTX:T].rearrange("p (r w) -> p r w", w=GRID_W)
        far, near = slice(1, GRID_W), slice(0, GRID_W - 1)
        latent = (grid(dst)[:, :, far], grid(src)[:, :, near]) if before else \
                 (grid(dst)[:, :, near], grid(src)[:, :, far])
    else:
        far, near = slice(CTX + GRID_W, T), slice(CTX, T - GRID_W)
        latent = (dst[:, far], src[:, near]) if before else (dst[:, near], src[:, far])
    return context, latent


def phase_low(nc, sem, io, g, low, then):
    w_in = [sem(f"low_w_in{m}") for m in range(3)]
    full, own, mixed, ready = sem("low_full"), sem("low_own"), sem("low_mixed"), sem("low_ready")
    tiles = (W_TILE, A_TILE, G_TILE)
    with ExitStack() as ctx:
        w = ctx.enter_context(nc.sbuf_tensor("low_w", [P, 3, KD * P], F32))
        ps = ctx.enter_context(nc.psum_tensor("low_ps", [P, 3, 1024], F32))
        block = ctx.enter_context(nc.Block())

        @block.sync
        def _(sp):
            for m in range(3):
                sp.dma_start(w[:, m, :], io["w_low"][m]).then_inc(w_in[m], 16)
            then.start(sp)

        @block.tensor
        def _(pe):
            for m in range(3):
                pe.wait_ge(w_in[m], 16)
                project(pe, ps[:, m, :], tiles_of(w[:, m, :]), g.h, KD).then_inc(full, 1)

        @block.scalar
        def _(act):
            for m, tile in enumerate(tiles):
                act.wait_ge(full, m + 1)
                act.activation(low[:, m, :], ps[:, m, 0:T], ACT.Copy,
                               scale=g.mu_own[:, tile:tile + 1]).then_inc(own, 1)
            act.wait_ge(mixed, 1)
            act.activation(low[:, 0, :], low[:, 0, :], ACT.Tanh)
            act.wait_ge(mixed, 3)
            act.activation(low[:, 2, :], low[:, 2, :], ACT.Sigmoid)

        @block.vector
        def _(dve):
            for m, tile in enumerate(tiles):
                dve.wait_ge(own, m + 1)
                (q,) = quarters_of([tile])
                for dst, src in shifted_views(q, low[:, m, :], ps[:, m, 0:T]):
                    last = dve.scalar_tensor_tensor(out=dst, in0=src, scalar=g.mu_q[:, tile, q:q + 1],
                                                    in1=dst, op0=ALU.mult, op1=ALU.add)
                last.then_inc(mixed, 1)


A_HAT, R_HAT, B_HAT, K_HAT = range(4)


def phase_rwkv_in(nc, sem, io, g, low, bonus, carry, early):
    w_in, w = early.w_in, early.raw
    a_full, a_done = [sem("rw_a_full0"), sem("rw_a_full1")], [sem("rw_a_done0"), sem("rw_a_done1")]
    b_full, b_done = [sem("rw_b_full0"), sem("rw_b_full1")], [sem("rw_b_done0"), sem("rw_b_done1")]
    own, half_mixed = sem("rw_own"), sem("rw_half_mixed")
    sq_done, inv_chain, root_done, kk_done = (sem("rw_sq_done"), sem("rw_inv_chain"), sem("rw_root_done"),
                                              sem("rw_kk_done"))
    cum_done, before_done, g_done, ginv_done, gbef_done = (sem("rw_cum_done"), sem("rw_before_done"),
                                                           sem("rw_g_done"), sem("rw_ginv_done"),
                                                           sem("rw_gbef_done"))
    rate_done, kd_done, kd_sum, kk_a, rk_done = (sem("rw_rate_done"), sem("rw_kd_done"), sem("rw_kd_sum"),
                                                 sem("rw_kk_a"), sem("rw_rk_done"))
    ahat, rhat, bhat, khat = sem("rw_ahat"), sem("rw_rhat"), sem("rw_bhat"), sem("rw_khat")
    turned = sem("rw_turned")
    chan_out, tok_out = sem("rw_chan_out"), sem("rw_tok_out")
    vec_tile, pool_tile = sem("rw_vec_tile"), sem("rw_pool_tile")
    roles = (R_TILES, K_TILES, V_TILES)
    TURNS = ((0, B_HAT), (0, K_HAT), (1, B_HAT), (1, K_HAT), None)
    A_USES, B_USES = 3, 6 + len(TURNS)
    TWO = 2

    def a_use(it, s, x):
        return (A_USES * s + x) % 2, A_USES * it + (A_USES * s + x) // 2

    def b_use(it, s, x):
        return (B_USES * s + x) % 2, B_USES * it + (B_USES * s + x) // 2

    with ExitStack() as ctx:
        sb = lambda n, shape: ctx.enter_context(nc.sbuf_tensor("rw_" + n, shape, F32))
        rkv = sb("rkv", [P, 2, 3, T])
        dec, rate = sb("dec", [P, 2, T]), sb("rate", [P, 2, T])
        cum, gg = sb("cum", [P, 2, T]), sb("gg", [P, 2, T])
        kd = sb("kd", [P, 2, T])
        kk, inv, kds = sb("kk", [P, T]), sb("inv", [P, T]), sb("kds", [P, T])
        hat = sb("hat", [P, 2, 4, T])
        tb = sb("tb", [P, len(TURNS), T])
        pa = ctx.enter_context(nc.psum_tensor("rw_pa", [P, 2, 1024], F32))
        pb = ctx.enter_context(nc.psum_tensor("rw_pb", [P, 2, 1024], F32))
        block = ctx.enter_context(nc.Block())
        one = lambda base, n: bass.ds(n + base, 1)

        @block.sync
        def _(sp):
            def store(it, s):
                n = 2 * it + s
                chan = io["chan"].rearrange("d c p (q j t) -> d q j p c t", q=4, j=PAIRS)
                for d in (0, 1):
                    for q, made in ((A_HAT, ahat), (R_HAT, rhat), (B_HAT, bhat), (K_HAT, khat)):
                        sp.wait_ge(made, 2 * n + d + 1)
                        sp.dma_start(chan[d, q, bass.ds(n, 1)].squeeze(0),
                                     hat[:, d, q, :].rearrange("p (c t) -> p c t", t=WC)).then_inc(chan_out, 16)
                tok = io["tok"].rearrange("d (c p) (q j m) -> d q j p c m", p=P, q=2, m=P)
                val = io["val"].rearrange("(c p) (j m) -> j p c m", p=P, m=P)
                for x, turn in enumerate(TURNS):
                    sp.wait_ge(turned, len(TURNS) * n + x + 1)
                    dst = val[bass.ds(n, 1)] if turn is None else tok[turn[0], turn[1] - B_HAT, bass.ds(n, 1)]
                    sp.dma_start(dst.squeeze(0), tb[:, x, :].rearrange("p (c m) -> p c m", m=P)).then_inc(tok_out, 16)

            with sp.Fori(0, PAIRS // 2 - 1) as it:
                for s in (0, 1):
                    store(it, s)
            for s in (0, 1):
                store(PAIRS // 2 - 1, s)
            sp.wait_ge(chan_out, 16 * 8 * (PAIRS + 1))
            sp.wait_ge(tok_out, 16 * len(TURNS) * (PAIRS + 1))

        @block.tensor
        def _(pe):
            def proj(it, s, x):
                slot, before = a_use(it, s, x)
                if x == 0:
                    pe.wait_ge(w_in[s], 16 * it + 16)
                pe.wait_ge(a_done[slot], before + 1)
                wt = tiles_of(w[:, s, :])
                project(pe, pa[:, slot, :], wt[:, KD * x:KD * x + KD, :], g.h, KD).then_inc(a_full[slot], 1)

            def small(it, s, x, lhs, rhs, ready=None):
                slot, before = b_use(it, s, x)
                if ready is not None:
                    pe.wait_ge(*ready)
                pe.wait_ge(b_done[slot], before + 1)
                for lo, hi in BANKS:
                    last = pe.matmul(pb[:, slot, lo:hi], lhs, rhs[:, lo:hi], start=True, stop=True)
                last.then_inc(b_full[slot], 1)

            def finish(it, s, ahead):
                n = 2 * it + s
                wt = tiles_of(w[:, s, :])
                proj(it, s, 2)
                for x, tile in ((0, 0), (2, 1)):
                    for d in (0, 1):
                        rows = slice(64 * d, 64 * d + 64)
                        small(it, s, x + d, wt[rows, 3 * KD + tile, :], low[rows, tile, :])
                if ahead is not None:
                    proj(*ahead, 0)
                small(it, s, 4, g.head_ones, inv, (sq_done, n + 1))
                if ahead is not None:
                    proj(*ahead, 1)
                small(it, s, 5, g.head_ones, kds, (rk_done, n + 1))
                for x, turn in enumerate(TURNS):
                    slot, before = b_use(it, s, 6 + x)
                    if turn is None:
                        src = rkv[:, s, 2, :]
                    else:
                        src = hat[:, turn[0], turn[1], :]
                        pe.wait_ge(bhat if turn[1] == B_HAT else khat, 2 * n + turn[0] + 1)
                    pe.wait_ge(b_done[slot], before + 1)
                    for c in range(NCH):
                        last = pe.transpose(pb[:, slot, P * c:P * c + P], src[:, P * c:P * c + P], g.ident)
                    last.then_inc(b_full[slot], 1)

            proj(0, 0, 0)
            proj(0, 0, 1)
            with pe.Fori(0, PAIRS // 2 - 1) as it:
                finish(it, 0, (it, 1))
                finish(it, 1, (it + 1, 0))
            finish(PAIRS // 2 - 1, 0, (PAIRS // 2 - 1, 1))
            finish(PAIRS // 2 - 1, 1, None)

        def mixed(eng, it, s, x):
            slot, before = a_use(it, s, x)
            eng.wait_ge(a_done[slot], before + 2)

        @block.scalar
        def _(act):
            def take(it, s, xs):
                n = 2 * it + s
                if 0 in xs:
                    act.wait_ge(vec_tile, n + 1)
                    act.wait_ge(pool_tile, n + 1)
                for x in xs:
                    slot, before = a_use(it, s, x)
                    act.wait_ge(a_full[slot], before + 1)
                    act.activation(rkv[:, s, x, :], pa[:, slot, 0:T], ACT.Copy,
                                   scale=g.mu_own[:, one(roles[x][0], n)]).then_inc(own, 1)

            def tile(it, s, ahead, loads):
                n = 2 * it + s
                take(it, s, (2,))
                act.wait_ge(vec_tile, n + 2)
                act.wait_ge(pool_tile, n + 2)
                for x, bias, dst in ((0, "w0", dec), (2, "a0", rate)):
                    for d in (0, 1):
                        slot, before = b_use(it, s, x + d)
                        act.wait_ge(b_full[slot], before + 1)
                        act.activation(dst[:, d, :], pb[:, slot, 0:T], ACT.Sigmoid,
                                       bias=g.v(bias)[:, one(KD * d, n)]).then_inc(b_done[slot], 1)
                if loads:
                    act.dma_start(w[:, s, :], io["w_rkv"][n + 2]).then_inc(w_in[s], 16)
                mixed(act, it, s, 1)
                act.activation(inv[:, :], rkv[:, s, 1, :], ACT.Square,
                               scale=g.v("k_k")[:, one(0, n)]).then_inc(sq_done, 1)
                act.wait_ge(chan_out, 16 * 8 * n + 16 * 8)
                for d in (0, 1):
                    act.wait_ge(before_done, 2 * n + d + 1)
                    act.activation(gg[:, d, :], cum[:, d, :], ACT.Exp, scale=-LOG_DECAY).then_inc(g_done, 1)
                    act.activation(dec[:, d, :], dec[:, d, :], ACT.Exp, scale=-LOG_DECAY).then_inc(gbef_done, 1)
                    act.activation(cum[:, d, :], cum[:, d, :], ACT.Exp, scale=LOG_DECAY).then_inc(ginv_done, 1)
                act.wait_ge(inv_chain, 2 * n + 2)
                act.activation(inv[:, :], inv[:, :], ACT.Sqrt).then_inc(root_done, 1)
                for d in (0, 1):
                    end = WC - 1 if d == 0 else 0
                    act.wait_ge(g_done, 2 * n + d + 1)
                    act.activation(carry[:, d, :, one(0, n)].squeeze(2), gg[:, d, end:T:WC], ACT.Copy)
                if ahead is not None:
                    take(*ahead, (0, 1))
                act.wait_ge(tok_out, 16 * len(TURNS) * n + 16 * len(TURNS))
                for x in range(len(TURNS)):
                    slot, before = b_use(it, s, 6 + x)
                    act.wait_ge(b_full[slot], before + 1)
                    act.activation(tb[:, x, :], pb[:, slot, 0:T], ACT.Copy).then_inc(turned, 1)
                    act.wait_ge(turned, len(TURNS) * n + x + 1)
                    act.sem_inc(b_done[slot], 1)

            take(0, 0, (0, 1))
            with act.Fori(0, PAIRS // 2 - 1) as it:
                tile(it, 0, (it, 1), True)
                tile(it, 1, (it + 1, 0), True)
            tile(PAIRS // 2 - 1, 0, (PAIRS // 2 - 1, 1), False)
            tile(PAIRS // 2 - 1, 1, None, False)

        @block.gpsimd
        def _(pool):
            pool.sem_inc(pool_tile, TWO)
            with pool.Fori(0, PAIRS // 2) as it:
                for s in (0, 1):
                    n = 2 * it + s
                    r, k = rkv[:, s, 0, :], rkv[:, s, 1, :]
                    for d in (0, 1):
                        pool.wait_ge(cum_done, 2 * n + d + 1)
                        pool.tensor_tensor(dec[:, d, :], cum[:, d, :], dec[:, d, :], ALU.subtract)\
                            .then_inc(before_done, 1)
                    for d in (0, 1):
                        pool.wait_ge(rate_done, 2 * n + d + 1)
                        if d == 0:
                            mixed(pool, it, s, 1)
                        pool.tensor_tensor(kd[:, d, :], kd[:, d, :], k, ALU.mult).then_inc(kd_done, 1)
                    pool.wait_ge(kd_done, 2 * n + 2)
                    pool.wait_ge(vec_tile, n + 2)
                    pool.tensor_tensor(kds[:, :], kd[:, 0, :], kd[:, 1, :], ALU.add).then_inc(kd_sum, 1)
                    for d in (0, 1):
                        pool.wait_ge(kk_done, n + 1)
                        pool.tensor_tensor(rate[:, d, :], rate[:, d, :], kk[:, :], ALU.mult).then_inc(kk_a, 1)
                    mixed(pool, it, s, 0)
                    for d in (0, 1):
                        pool.wait_ge(g_done, 2 * n + d + 1)
                        pool.tensor_tensor(hat[:, d, R_HAT, :], gg[:, d, :], r, ALU.mult).then_inc(rhat, 1)
                    pool.wait_ge(rhat, 2 * n + 2)
                    pool.sem_inc(pool_tile, 1)

        @block.vector
        def _(dve):
            dve.sem_inc(vec_tile, TWO)
            dve.sem_inc(a_done[0], 1)
            dve.sem_inc(a_done[1], 1)
            dve.sem_inc(b_done[0], 1)
            dve.sem_inc(b_done[1], 1)
            dve.sem_inc(chan_out, 16 * 8)
            dve.sem_inc(tok_out, 16 * len(TURNS))
            with dve.Fori(0, PAIRS // 2) as it:
                for s in (0, 1):
                    n = 2 * it + s
                    r, k, v = (rkv[:, s, x, :] for x in range(3))
                    for x, role in enumerate(roles):
                        slot, before = a_use(it, s, x)
                        dve.wait_ge(own, 3 * n + x + 1)
                        qa, qb = quarters_of(role)
                        for q in (qa, qb):
                            for dst, src in shifted_views(q, rkv[:, s, x, :], pa[:, slot, 0:T]):
                                last = dve.scalar_tensor_tensor(
                                    out=dst, in0=src, scalar=g.mu_q[:, one(role[0], n), q], in1=dst,
                                    op0=ALU.mult, op1=ALU.add)
                            if q == qa:
                                last.then_inc(half_mixed, 1)
                                dve.wait_ge(half_mixed, 3 * n + x + 1)
                        last.then_inc(a_done[slot], 1)
                    for d in (0, 1):
                        slot, before = b_use(it, s, d)
                        dve.wait_ge(b_done[slot], before + 2)
                        flow = (lambda a: a) if d == 0 else (lambda a: a[:, ::-1])
                        dve.tensor_tensor_scan(flow(cum[:, d, :]), flow(g.reset[:, d, :]), flow(dec[:, d, :]),
                                               0.0, ALU.mult, ALU.add).then_inc(cum_done, 1)
                    for d in (0, 1):
                        slot, before = b_use(it, s, 2 + d)
                        dve.wait_ge(b_done[slot], before + 2)
                        dve.tensor_scalar(kd[:, d, :], rate[:, d, :], g.v("k_a")[:, one(0, n)],
                                          g.k_a_c[:, one(0, n)], ALU.mult, ALU.add).then_inc(rate_done, 1)
                    slot, before = b_use(it, s, 4)
                    dve.wait_ge(b_full[slot], before + 1)
                    dve.tensor_scalar(inv[:, :], pb[:, slot, 0:T], 1e-12, None, ALU.add).then_inc(inv_chain, 1)
                    dve.wait_ge(inv_chain, 2 * n + 1)
                    dve.sem_inc(b_done[slot], 1)
                    dve.reciprocal(inv[:, :], inv[:, :]).then_inc(inv_chain, 1)
                    mixed(dve, it, s, 0)
                    dve.wait_ge(kd_sum, n + 1)
                    dve.scalar_tensor_tensor(out=kds[:, :], in0=r, scalar=g.v("r_k")[:, one(0, n)], in1=kds[:, :],
                                             op0=ALU.mult, op1=ALU.mult).then_inc(rk_done, 1)
                    dve.wait_ge(root_done, n + 1)
                    dve.scalar_tensor_tensor(out=kk[:, :], in0=k, scalar=g.v("k_k")[:, one(0, n)], in1=inv[:, :],
                                             op0=ALU.mult, op1=ALU.mult).then_inc(kk_done, 1)
                    for d in (0, 1):
                        dve.wait_ge(ginv_done, 2 * n + d + 1)
                        dve.tensor_tensor(hat[:, d, K_HAT, :], kd[:, d, :], cum[:, d, :], ALU.mult).then_inc(khat, 1)
                    dve.wait_ge(kk_done, n + 1)
                    for d in (0, 1):
                        dve.wait_ge(gbef_done, 2 * n + d + 1)
                        dve.scalar_tensor_tensor(out=hat[:, d, A_HAT, :], in0=kk[:, :], scalar=-1.0,
                                                 in1=dec[:, d, :], op0=ALU.mult, op1=ALU.mult).then_inc(ahat, 1)
                    for d in (0, 1):
                        dve.wait_ge(kk_a, 2 * n + d + 1)
                        dve.tensor_tensor(hat[:, d, B_HAT, :], rate[:, d, :], cum[:, d, :], ALU.mult).then_inc(bhat, 1)
                    slot, before = b_use(it, s, 5)
                    dve.wait_ge(b_full[slot], before + 1)
                    mixed(dve, it, s, 2)
                    dve.scalar_tensor_tensor(out=bonus[:, one(0, n), :].squeeze(1), in0=pb[:, slot, 0:T],
                                             scalar=0.5, in1=v, op0=ALU.mult, op1=ALU.mult)\
                       .then_inc(b_done[slot], 1)
                    dve.wait_ge(b_done[slot], before + 2)
                    dve.sem_inc(vec_tile, 1)


def phase_blocks(nc, sem, io):
    loaded = [sem("bl_in0"), sem("bl_in1")]
    full, copied = [sem("bl_full0"), sem("bl_full1")], [sem("bl_copied0"), sem("bl_copied1")]
    out = [sem("bl_out0"), sem("bl_out1")]
    go, sp_go = sem("bl_pe_go"), sem("bl_sp_go")
    with ExitStack() as ctx:
        ab = ctx.enter_context(nc.sbuf_tensor("bl_ab", [P, 2, 2, 2, PAIRS, WC], F32))
        m = ctx.enter_context(nc.sbuf_tensor("bl_m", [P, 2, 2, PAIRS, WC], F32))
        ps = ctx.enter_context(nc.psum_tensor("bl_ps", [P, 2, 2, 512], F32))
        block = ctx.enter_context(nc.Block())

        @block.sync
        def _(sp):
            def load(it, s):
                for d in (0, 1):
                    src = io["chan"][d, bass.ds(2 * it + s, 1)].squeeze(0).rearrange("p (q f) -> p q f", q=4)
                    sp.dma_start(ab[:, s, d, :, :, :].rearrange("p q j t -> p q (j t)"),
                                 src[:, A_HAT:B_HAT + 1:B_HAT, :]).then_inc(loaded[s], 16)

            def store(it, s):
                for d in (0, 1):
                    sp.wait_ge(copied[d], 2 * it + s + 2 + 1)
                sp.sem_inc(sp_go, 1)
                dst = io["blk_m"][bass.ds(2 * it + s, 1)].squeeze(0)
                for hb in range(4):
                    rows, cols = slice(QB * hb, QB * hb + QB), slice(QB * (hb % 2), QB * (hb % 2) + QB)
                    sp.dma_start(dst[hb].rearrange("d j (r c) -> r (d j) c", c=QB),
                                 m[rows, s, :, :, cols].rearrange("r d j c -> r (d j) c")).then_inc(out[s], 16)

            load(0, 0)
            load(0, 1)
            with sp.Fori(0, NWC // 2 - 1) as it:
                for s in (0, 1):
                    store(it, s)
                    load(it + 1, s)
            for s in (0, 1):
                store(NWC // 2 - 1, s)
            for s in (0, 1):
                sp.wait_ge(out[s], 16 * 4 * (NWC // 2 + 1))

        @block.tensor
        def _(pe):
            with pe.Fori(0, NWC // 2) as it:
                for s in (0, 1):
                    pe.wait_ge(loaded[s], 32 * it + 32)
                    for d in (0, 1):
                        pe.wait_ge(copied[d], 2 * it + s + 1)
                        pe.sem_inc(go, 1)
                        for j in range(PAIRS):
                            for rows in (slice(0, 64), slice(64, 128)):
                                last = pe.matmul(ps[rows, s, d, WC * j:WC * j + WC], ab[rows, s, d, 1 - d, j, :],
                                                 ab[rows, s, d, d, j, :], start=True, stop=True)
                        last.then_inc(full[d], 1)

        def copy(eng, d, instruction):
            for s in (0, 1):
                eng.sem_inc(out[s], 16 * 2)
            eng.sem_inc(copied[d], 2)
            with eng.Fori(0, NWC // 2) as it:
                for s in (0, 1):
                    eng.wait_ge(full[d], 2 * it + s + 1)
                    eng.wait_ge(out[s], 16 * 4 * it + 16 * 4)
                    instruction(m[:, s, d, :, :], ps[:, s, d, :].rearrange("p (j w) -> p j w", w=WC))\
                        .then_inc(copied[d], 1)

        @block.scalar
        def _(act):
            copy(act, 0, lambda o, i: nc.scalar.activation(o, i, ACT.Copy))

        @block.vector
        def _(dve):
            copy(dve, 1, lambda o, i: nc.vector.tensor_copy(o, i))


def phase_solve(nc, sem, io, g):
    w_in, w_used = [sem("so_w_in0"), sem("so_w_in1")], sem("so_w_used")
    gate_done, gate_out = sem("so_gate_done"), [sem("so_gate_out0"), sem("so_gate_out1")]
    u_in, w_out = sem("so_u_in"), sem("so_w_out")
    prepared, zeroed = sem("so_prepared"), sem("so_zeroed")
    SHARES = (("so_v0", 0, 2), ("so_v1", 2, 4), ("so_p", 4, BLOCK_GROUPS))
    product = [sem(n + "_product") for n, _, _ in SHARES]
    summed = [sem(n + "_summed") for n, _, _ in SHARES]
    turned = [sem(n + "_turned") for n, _, _ in SHARES]
    with ExitStack() as ctx:
        sb = lambda n, shape: ctx.enter_context(nc.sbuf_tensor("so_" + n, shape, F32))
        u, w, wt = (sb(n, [P, BLOCK_GROUPS, QB, QB]) for n in ("u", "w", "wt"))
        part = sb("part", [P, BLOCK_GROUPS, (QB // 2) ** 2])
        gw, gate = sb("gw", [P, 2, KD * P]), sb("gate", [P, 2, T])
        ps = ctx.enter_context(nc.psum_tensor("so_ps", [P, 2, 1024], F32))
        block = ctx.enter_context(nc.Block())

        def flat(t):
            return t.rearrange("p g i k -> p g (i k)")

        @block.sync
        def _(sp):
            src = io["blk_m"].rearrange("c h d j e -> (c h d j) e").rearrange("(g p) e -> p g e", p=P)
            sp.dma_start(flat(u[:, :, :, :]), src).then_inc(u_in, 16)

            def load(j):
                sp.dma_start(gw[:, j % 2, :], io["w_r_gate"][j]).then_inc(w_in[j % 2], 16)

            load(0)
            load(1)
            dst = io["blk_w"].rearrange("c h d k j e -> k (c h d) j e").rearrange("k (g q) j e -> k g q j e", g=BLOCK_GROUPS)

            def store(share):
                _, lo, hi = SHARES[share]
                for kind, src, ready in ((0, w, (summed[share], QB - 1)), (1, wt, (turned[share], 1))):
                    sp.wait_ge(*ready)
                    for gr in range(lo, hi):
                        sp.dma_start(dst[kind, gr], flat(src[:, :, :, :])[:, gr, :]).then_inc(w_out, 16)

            for j in range(KD):
                sp.wait_ge(gate_done, j + 1)
                sp.dma_start(io["gate_r"][j], gate[:, j % 2, :]).then_inc(gate_out[j % 2], 16)
                if j + 2 < KD:
                    load(j + 2)
                if j == KD // 2:
                    store(0)
                    store(2)
            for s in (0, 1):
                sp.wait_ge(gate_out[s], 16 * KD // 2)
            store(1)
            sp.wait_ge(w_out, 16 * 2 * BLOCK_GROUPS)

        def solve(eng, share):
            _, lo, hi = SHARES[share]
            n = hi - lo
            eng.wait_ge(u_in, 16)
            eng.wait_ge(prepared, 1)
            for step, k in enumerate(range(QB - 1, 0, -1)):
                shape = [P, n, k, QB - k]
                p = part[:, lo:hi, 0:k * (QB - k)].rearrange("p g (i c) -> p g i c", c=QB - k)
                col, row, acc = u[:, lo:hi, 0:k, k:k + 1], w[:, lo:hi, k:k + 1, k:QB], w[:, lo:hi, 0:k, k:QB]
                if step > 0:
                    eng.wait_ge(summed[share], step)
                eng.tensor_tensor(p, col.to_broadcast(shape), row.to_broadcast(shape), ALU.mult)\
                   .then_inc(product[share], 1)
                eng.wait_ge(product[share], step + 1)
                eng.tensor_tensor(acc, acc, p, ALU.add).then_inc(summed[share], 1)
            eng.wait_ge(summed[share], QB - 1)
            eng.tensor_copy(wt[:, lo:hi, :, :], w[:, lo:hi, :, :].rearrange("p g i k -> p g k i"))\
               .then_inc(turned[share], 1)

        @block.tensor
        def _(pe):
            for j in range(KD):
                pe.wait_ge(w_in[j % 2], 16 * (j // 2 + 1))
                if j >= 2:
                    pe.wait_ge(gate_done, j - 1)
                project_halves(pe, ps[:, j % 2, :], tiles_of(gw[:, j % 2, :]), g.h, KD).then_inc(w_used, 1)

        @block.scalar
        def _(act):
            for j in range(KD):
                act.wait_ge(w_used, j + 1)
                if j >= 2:
                    act.wait_ge(gate_out[j % 2], 16 * (j // 2))
                act.activation(by_half(gate[:, j % 2, :]), halves(ps[:, j % 2, :]), ACT.Sigmoid)\
                   .then_inc(gate_done, 1)

        @block.vector
        def _(dve):
            solve(dve, 0)
            solve(dve, 1)

        @block.gpsimd
        def _(pool):
            pool.memset(w[:, :, :, :], 0.0).then_inc(zeroed, 1)
            pool.wait_ge(zeroed, 1)
            pool.memset(flat(w[:, :, :, :])[:, :, 0:QB * QB:QB + 1], 1.0).then_inc(prepared, 1)
            solve(pool, 2)


PE_STEPS = ["MB", "MK", "Z", "T", "X", "U", "Y", "S"]
DVE_STEPS = ["MB", "MK", "Z", "T", "S"]
ACT_STEPS = ["X", "U", "Y"]


def phase_wkv(nc, sem, io, g, carry, diagonal, first, n_chunks, state_in, state_out, tag):
    count = lambda steps, i, name: len(steps) * i + steps.index(name) + 1
    loaded = [[sem(f"{tag}_in{d}{s}") for s in (0, 1)] for d in (0, 1)]
    ar_in = [[sem(f"{tag}_ar_in{d}{s}") for s in (0, 1)] for d in (0, 1)]
    bk_in = [sem(f"{tag}_bk_in{d}") for d in (0, 1)]
    y_out = [[sem(f"{tag}_y_out{d}{s}") for s in (0, 1)] for d in (0, 1)]
    pe_done, dve_done, act_done = ([sem(f"{tag}_{e}_done{d}") for d in (0, 1)] for e in ("pe", "dve", "act"))
    summed = [sem(f"{tag}_summed{d}") for d in (0, 1)]
    pe_ready, dve_ready, sp_ready = sem(tag + "_pe_go"), sem(tag + "_dve_go"), sem(tag + "_sp_go")
    state_ready, state_stored, zeroed = sem(tag + "_state_ready"), sem(tag + "_state_stored"), sem(tag + "_zeroed")
    STEP_LOADS = 8
    with ExitStack() as ctx:
        sb = lambda n, shape: ctx.enter_context(nc.sbuf_tensor(f"{tag}_{n}", shape, F32))
        ar = sb("ar", [P, 2, 2, 2, PAIRS, WC])
        bk, ww = diagonal
        tk = sb("tk", [P, 2, 2, 2, PAIRS, HD])
        vv = sb("vv", [P, 2, 2, PAIRS, HD])
        mb, mk = sb("mb", [P, 2, PAIRS, 2, WC]), sb("mk", [P, 2, PAIRS, 2, WC])
        z, tt = sb("z", [P, 2, PAIRS, WC]), sb("tt", [P, 2, PAIRS, WC])
        x_, u_, st = sb("x", [P, 2, PAIRS, HD]), sb("u", [P, 2, PAIRS, HD]), sb("st", [P, 2, PAIRS, HD])
        y_ = sb("y", [P, 2, 2, PAIRS, HD])
        p0 = ctx.enter_context(nc.psum_tensor(tag + "_p0", [P, 2, 2, 512], F32))
        p1 = ctx.enter_context(nc.psum_tensor(tag + "_p1", [P, 2, 2, 512], F32))
        block = ctx.enter_context(nc.Block())
        narrow = lambda p: p.rearrange("p (j w) -> p j w", w=WC)
        wide = lambda p: p.rearrange("p b (j f) -> p (b j) f", f=2 * WC)
        over_heads = lambda m: m.unsqueeze(1).to_broadcast([P, PAIRS, WC])
        chunk = lambda d, i: i + first if d == 0 else first + n_chunks - 1 - i
        plain = lambda s, d: ww[:, s, d, 1 - d]
        turned = lambda s, d: ww[:, s, d, d]
        ITERS = n_chunks // 2

        @block.sync
        def _(sp):
            if state_in is not None:
                sp.dma_start(st[:, :, :, :], state_in.rearrange("d p (j w) -> p d j w", w=HD)).then_inc(state_ready, 16)

            def load_bk(it, s):
                for d in (0, 1):
                    src = io["chan"][d, bass.ds(chunk(d, 2 * it + s), 1)].squeeze(0)\
                        .rearrange("p (q t) -> p q t", t=WC)
                    for h in (0, 1):
                        rows = slice(64 * h, 64 * h + 64)
                        sp.dma_start(bk[rows, d, :, :, rows].rearrange("p q j t -> p (q j) t"),
                                     src[rows, B_HAT * PAIRS:, :]).then_inc(bk_in[d], 16)

            def load_blocks(it, s):
                for d in (0, 1):
                    c = chunk(d, 2 * it + s)
                    for hb in range(4):
                        rows, cols = slice(QB * hb, QB * hb + QB), slice(QB * (hb % 2), QB * (hb % 2) + QB)
                        src = io["blk_w"][bass.ds(c, 1)].squeeze(0)[hb, d]
                        sp.dma_start(ww[rows, s, d, :, :, cols].rearrange("p k j e -> p (k j) e"),
                                     src.rearrange("k j (r e) -> r (k j) e", e=QB)).then_inc(loaded[d][s], 16)

            def load_ar(it, s):
                for d in (0, 1):
                    c = chunk(d, 2 * it + s)
                    sp.dma_start(ar[:, s, d, :, :, :].rearrange("p q j t -> p (q j t)"),
                                 io["chan"][d, bass.ds(c, 1)].squeeze(0)[:, 0:B_HAT * PAIRS * WC])\
                      .then_inc(ar_in[d][s], 16)

            def load(it, s):
                for d in (0, 1):
                    c = chunk(d, 2 * it + s)
                    for h in (0, 1):
                        rows = slice(64 * h, 64 * h + 64)
                        tok = io["tok"][d, bass.ds(c * WC, WC), :].rearrange("t (n h m) -> h t n m", h=2, m=HD)
                        val = io["val"][bass.ds(c * WC, WC), :].rearrange("t (n h m) -> h t n m", h=2, m=HD)
                        sp.dma_start(tk[rows, s, d, :, :, :].rearrange("p q j m -> p (q j) m"), tok[h])\
                          .then_inc(loaded[d][s], 16)
                        sp.dma_start(vv[rows, s, d, :, :], val[h]).then_inc(loaded[d][s], 16)

            def store(it, s):
                for d in (0, 1):
                    i = 2 * it + s
                    sp.wait_ge(act_done[d], count(ACT_STEPS, i, "Y") + 1)
                    sp.sem_inc(sp_ready, 1)
                    dst = io["wkv_y"][d, bass.ds(chunk(d, i), 1)].squeeze(0).rearrange("p (j w) -> p j w", w=HD)
                    sp.dma_start(dst, y_[:, s, d, :, :]).then_inc(y_out[d][s], 16)

            def next_bk(it, s):
                for d in (0, 1):
                    sp.wait_ge(pe_done[d], count(PE_STEPS, 2 * it + s, "MK"))
                sp.sem_inc(sp_ready, 1)
                load_bk(it + s, 1 - s)

            load_ar(0, 0)
            if state_in is None:
                sp.wait_ge(zeroed, 2)
            load_bk(0, 0)
            load_blocks(0, 0)
            load(0, 0)
            load_ar(0, 1)
            load_blocks(0, 1)
            load(0, 1)
            if ITERS > 1:
                with sp.Fori(0, ITERS - 1) as it:
                    for s in (0, 1):
                        next_bk(it, s)
                        store(it, s)
                        for d in (0, 1):
                            sp.wait_ge(pe_done[d], len(PE_STEPS) * (2 * it + s + 1))
                        sp.sem_inc(sp_ready, 1)
                        load_ar(it + 1, s)
                        load_blocks(it + 1, s)
                        load(it + 1, s)
            next_bk(ITERS - 1, 0)
            for s in (0, 1):
                store(ITERS - 1, s)
            for d in (0, 1):
                for s in (0, 1):
                    sp.wait_ge(y_out[d][s], 16 * ITERS + 16)
            if state_out is not None:
                for d in (0, 1):
                    sp.wait_ge(dve_done[d], len(DVE_STEPS) * n_chunks + 1)
                sp.dma_start(state_out.rearrange("d p (j w) -> p d j w", w=HD), st[:, :, :, :]).then_inc(state_stored, 16)
                sp.wait_ge(state_stored, 16)

        @block.gpsimd
        def _(pool):
            if state_in is None:
                pool.memset(st[:, :, :, :], 0.0).then_inc(state_ready, 16)
            for d in (0, 1):
                for s in (0, 1):
                    pool.sem_inc(y_out[d][s], 16)

        @block.tensor
        def _(pe):
            pe.wait_ge(state_ready, 16)
            halves = (slice(0, 64), slice(64, 128))

            def stage(d, products, waits, rows_of=halves):
                for s, v in waits:
                    pe.wait_ge(s, v)
                pe.sem_inc(pe_ready, 1)
                for j in range(PAIRS):
                    for rows in rows_of:
                        for out, lhs, rhs, starts, stops in products(j):
                            last = pe.matmul(out[rows], lhs[rows], rhs[rows], start=starts, stop=stops)
                last.then_inc(pe_done[d], 1)

            def alone(out, lhs, rhs):
                return [(out, lhs, rhs, True, True)]

            def total(out, *pairs):
                return [(out, l, r, n == 0, n == len(pairs) - 1) for n, (l, r) in enumerate(pairs)]

            def step(it, s, final=False):
                i = 2 * it + s
                dve = lambda d, name, at=i: (dve_done[d], count(DVE_STEPS, at, name) + 1)
                act = lambda d, name, at=i: (act_done[d], count(ACT_STEPS, at, name) + 1)
                both_heads = (slice(0, P),)
                for d in (0, 1):
                    stage(d, lambda j: alone(wide(p0[:, d])[:, j], bk[:, d, 0, j, :], ar[:, s, d, :, j, :]),
                          [(bk_in[d], 32 * i + 32), (ar_in[d][s], 16 * it + 16),
                           (act_done[d], len(ACT_STEPS) * i + 1)], both_heads)
                for d in (0, 1):
                    stage(d, lambda j: alone(wide(p1[:, d])[:, j], bk[:, d, 1, j, :], ar[:, s, d, :, j, :]),
                          [(dve_done[d], len(DVE_STEPS) * i + 1)], both_heads)
                for d in (0, 1):
                    stage(d, lambda j: alone(narrow(p0[:, d, 0])[:, j], mb[:, d, j, 0, :], plain(s, d)[:, j]),
                          [dve(d, "MB"), (loaded[d][s], 16 * STEP_LOADS * (it + 1))])
                for d in (0, 1):
                    stage(d, lambda j: alone(narrow(p1[:, d, 1])[:, j], z[:, d, j, :], turned(s, d)[:, j]),
                          [dve(d, "Z")])
                for d in (0, 1):
                    stage(d, lambda j: total(narrow(p0[:, d, 0])[:, j], (ar[:, s, d, 0, j, :], st[:, d, j, :]),
                                             (mk[:, d, j, 0, :], vv[:, s, d, j, :])), [])
                for d in (0, 1):
                    stage(d, lambda j: alone(narrow(p0[:, d, 1])[:, j], tt[:, d, j, :], x_[:, d, j, :]),
                          [act(d, "X"), dve(d, "T")])
                for d in (0, 1):
                    stage(d, lambda j: total(narrow(p1[:, d, 0])[:, j], (ar[:, s, d, 1, j, :], st[:, d, j, :]),
                                             (mb[:, d, j, 1, :], u_[:, d, j, :]),
                                             (mk[:, d, j, 1, :], vv[:, s, d, j, :])), [act(d, "U")])
                    if final and state_out is None:
                        continue
                    stage(d, lambda j: total(narrow(p1[:, d, 1])[:, j], (tk[:, s, d, 0, j, :], u_[:, d, j, :]),
                                             (tk[:, s, d, 1, j, :], vv[:, s, d, j, :])), [])

            if ITERS > 1:
                with pe.Fori(0, ITERS - 1) as it:
                    step(it, 0)
                    step(it, 1)
            step(ITERS - 1, 0)
            step(ITERS - 1, 1, final=True)

        @block.scalar
        def _(act):
            for d in (0, 1):
                act.sem_inc(act_done[d], 1)
            with act.Fori(0, ITERS) as it:
                for s in (0, 1):
                    i = 2 * it + s
                    for name, src, dst in (("X", lambda d: p0[:, d, 0, :], lambda d: x_[:, d]),
                                           ("U", lambda d: p0[:, d, 1, :], lambda d: u_[:, d]),
                                           ("Y", lambda d: p1[:, d, 0, :], lambda d: y_[:, s, d])):
                        for d in (0, 1):
                            act.wait_ge(pe_done[d], count(PE_STEPS, i, name))
                            if name == "Y":
                                act.wait_ge(y_out[d][s], 16 * it + 16)
                            act.activation(dst(d), narrow(src(d)), ACT.Copy).then_inc(act_done[d], 1)

        @block.vector
        def _(dve):
            if state_in is None:
                dve.memset(bk[:, :, :, :, :], 0.0).then_inc(zeroed, 1)
                dve.memset(ww[:, :, :, :, :, :], 0.0).then_inc(zeroed, 1)
            for d in (0, 1):
                dve.sem_inc(dve_done[d], 1)

            def step(it, s, final=False):
                i = 2 * it + s
                pairs = lambda d: g.wmask[:, d, STRICT:UPTO + 1, :].rearrange("p l w -> p (l w)")\
                    .unsqueeze(1).to_broadcast([P, PAIRS, 2 * WC])
                flat = lambda m: m.rearrange("p j q w -> p j (q w)")
                for d in (0, 1):
                    dve.wait_ge(pe_done[d], count(PE_STEPS, i, "MB"))
                    dve.tensor_tensor(flat(mb[:, d]), wide(p0[:, d]), pairs(d), ALU.mult).then_inc(dve_done[d], 1)
                for d in (0, 1):
                    dve.wait_ge(pe_done[d], count(PE_STEPS, i, "MK"))
                    dve.tensor_tensor(flat(mk[:, d]), wide(p1[:, d]), pairs(d), ALU.mult).then_inc(dve_done[d], 1)
                for d in (0, 1):
                    dve.wait_ge(pe_done[d], count(PE_STEPS, i, "Z"))
                    dve.tensor_tensor(z[:, d], narrow(p0[:, d, 0]), over_heads(g.wmask[:, d, BETWEEN, :]),
                                      ALU.mult).then_inc(dve_done[d], 1)
                for d in (0, 1):
                    dve.wait_ge(pe_done[d], count(PE_STEPS, i, "T"))
                    dve.tensor_tensor(tt[:, d], turned(s, d), narrow(p1[:, d, 1]), ALU.add)\
                       .then_inc(dve_done[d], 1)
                for d in (0, 1):
                    if final and state_out is None:
                        continue
                    dve.wait_ge(pe_done[d], count(PE_STEPS, i, "S"))
                    dve.tensor_tensor(st[:, d], st[:, d], narrow(p1[:, d, 1]), ALU.add).then_inc(summed[d], 1)
                    dve.wait_ge(summed[d], i + 1)
                    dve.sem_inc(dve_ready, 1)
                    end = carry[:, d, bass.ds(chunk(d, i), 1), :].squeeze(1)
                    dve.tensor_tensor(st[:, d], st[:, d], end.unsqueeze(2).to_broadcast([P, PAIRS, HD]),
                                      ALU.mult).then_inc(dve_done[d], 1)

            if ITERS > 1:
                with dve.Fori(0, ITERS - 1) as it:
                    step(it, 0)
                    step(it, 1)
            step(ITERS - 1, 0)
            step(ITERS - 1, 1, final=True)


def phase_wkv_out(nc, sem, io, g, low, bonus, y_r, split, then):
    y_in = [sem(f"wo_y_in{b}") for b in range(NWC // 2)]
    added, centred, squared, summed, scaled = (sem("wo_added"), sem("wo_centred"), sem("wo_squared"),
                                               sem("wo_summed"), sem("wo_scaled"))
    inverse, root_done, normed = sem("wo_inverse"), sem("wo_root_done"), sem("wo_normed")
    tr_full, affine, tr_done = sem("wo_tr_full"), sem("wo_affine"), sem("wo_tr_done")
    g_in, g_full, g_done, rounded = sem("wo_g_in"), sem("wo_g_full"), sem("wo_g_done"), sem("wo_rounded")
    BATCH = 2
    N = NWC // BATCH
    ROWS = BATCH * PAIRS
    with ExitStack() as ctx:
        sb = lambda n, shape: ctx.enter_context(nc.sbuf_tensor("wo_" + n, shape, F32))
        y = sb("y", [P, N, 2, ROWS, HD])
        sq = sb("sq", [P, ROWS, HD])
        mean, var = sb("mean", [P, 2, ROWS]), sb("var", [P, 2, ROWS])
        g2 = sb("g2", [P, D])
        ps = ctx.enter_context(nc.psum_tensor("wo_ps", [P, 2, PAIRS, BATCH * WC], F32))
        pg = ctx.enter_context(nc.psum_tensor("wo_pg", [P, 2, 1024], F32))
        block = ctx.enter_context(nc.Block())
        per_row = lambda a: a.unsqueeze(2).to_broadcast([P, ROWS, HD])
        span = lambda b: slice(BATCH * WC * b, BATCH * WC * (b + 1))

        @block.sync
        def _(sp):
            sp.dma_start(g2[:, :], io["g2"]).then_inc(g_in, 16)
            for b in range(N):
                for d in (0, 1):
                    for c in range(BATCH):
                        sp.dma_start(y[:, b, d, PAIRS * c:PAIRS * (c + 1), :].rearrange("p j w -> p (j w)"),
                                     io["wkv_y"][d, BATCH * b + c]).then_inc(y_in[b], 16)
            then.start(sp)

        @block.tensor
        def _(pe):
            def gate(j):
                for lo, hi in BANKS:
                    last = pe.matmul(pg[:, j % 2, lo:hi], g2[:, P * j:P * j + P], low[:, 2, lo:hi],
                                     start=True, stop=True)
                last.then_inc(g_full, 1)

            pe.wait_ge(g_in, 16)
            gate(0)
            gate(1)
            for b in range(N):
                pe.wait_ge(normed, b + 1)
                if b >= 2:
                    pe.wait_ge(affine, b - 1)
                for j in range(PAIRS):
                    for c in range(BATCH):
                        for rows in (slice(0, 64), slice(64, 128)):
                            last = pe.matmul(ps[rows, b % 2, j, WC * c:WC * c + WC], y[rows, b, 0, PAIRS * c + j, :],
                                             g.ident_w[rows], start=True, stop=True)
                last.then_inc(tr_full, 1)
            for j in range(2, PAIRS):
                pe.wait_ge(g_done, j - 1)
                gate(j)

        @block.gpsimd
        def _(pool):
            def add_bonus(b):
                pool.wait_ge(affine, b + 1)
                pool.tensor_tensor(y_r[:, :, span(b)], y_r[:, :, span(b)], bonus[:, :, span(b)], ALU.add)\
                    .then_inc(tr_done, 1)

            for b in range(N):
                pool.wait_ge(y_in[b], 16 * 2 * BATCH)
                pool.tensor_tensor(y[:, b, 0], y[:, b, 0], y[:, b, 1], ALU.add).then_inc(added, 1)
            for b in range(N):
                add_bonus(b)

        @block.scalar
        def _(act):
            def turn(b):
                act.wait_ge(tr_full, b + 1)
                for j in range(PAIRS):
                    last = act.activation(y_r[:, j, span(b)], ps[:, b % 2, j, :], ACT.Identity,
                                          scale=g.v("lnx_w")[:, j:j + 1], bias=g.v("lnx_b")[:, j:j + 1])
                last.then_inc(affine, 1)

            for b in range(N):
                act.wait_ge(centred, b + 1)
                if b > 0:
                    act.wait_ge(summed, 2 * b)
                act.activation(sq[:, :, :], y[:, b, 0], ACT.Square).then_inc(squared, 1)
                act.wait_ge(inverse, b + 1)
                act.activation(var[:, b % 2, :], var[:, b % 2, :], ACT.Sqrt).then_inc(root_done, 1)
                if b > 0:
                    turn(b - 1)
            turn(N - 1)
            for j in range(PAIRS):
                act.wait_ge(g_done, j + 1)
                act.activation(split[0][:, j, :], y_r[:, j, :], ACT.Copy).then_inc(rounded, 1)

        @block.vector
        def _(dve):
            def normalise(b):
                dve.wait_ge(root_done, b + 1)
                dve.tensor_tensor(y[:, b, 0], y[:, b, 0], per_row(var[:, b % 2, :]), ALU.mult).then_inc(normed, 1)

            for b in range(N):
                yy, m, v = y[:, b, 0], mean[:, b % 2, :], var[:, b % 2, :]
                dve.wait_ge(added, b + 1)
                dve.tensor_reduce(m, yy, AX.X, ALU.add).then_inc(summed, 1)
                dve.wait_ge(summed, 2 * b + 1)
                dve.tensor_scalar(m, m, 1.0 / HD, None, ALU.mult).then_inc(scaled, 1)
                dve.wait_ge(scaled, 2 * b + 1)
                dve.tensor_tensor(yy, yy, per_row(m), ALU.subtract).then_inc(centred, 1)
                if b > 0:
                    normalise(b - 1)
                dve.wait_ge(squared, b + 1)
                dve.tensor_reduce(v, sq[:, :, :], AX.X, ALU.add).then_inc(summed, 1)
                dve.wait_ge(summed, 2 * b + 2)
                dve.tensor_scalar(v, v, 1.0 / HD, 64e-5, ALU.mult, ALU.add).then_inc(scaled, 1)
                dve.wait_ge(scaled, 2 * b + 2)
                dve.reciprocal(v, v).then_inc(inverse, 1)
            normalise(N - 1)

            def low_part(j):
                dve.wait_ge(rounded, j + 1)
                dve.tensor_tensor(split[1][:, j, :], y_r[:, j, :], split[0][:, j, :].bitcast(F32), ALU.subtract)

            dve.wait_ge(tr_done, N)
            for j in range(PAIRS):
                dve.wait_ge(g_full, j + 1)
                dve.tensor_tensor(y_r[:, j, :], y_r[:, j, :], pg[:, j % 2, 0:T], ALU.mult).then_inc(g_done, 1)
                if j > 0:
                    low_part(j - 1)
            low_part(PAIRS - 1)


def build(nc, io):
    with ExitStack() as ctx:
        serial, kept = [0], []

        def early(tag, source, raw):
            loads = EarlyLoads(nc, tag, source, raw)
            kept.extend(loads.w_in)
            return loads

        def run(phase, *args, **kw):
            used = []
            serial[0] += 1

            def sem(name):
                used.append(nc.alloc_semaphore(f"p{serial[0]}_{name}"))
                return used[-1]

            phase(nc, sem, *args, **kw)
            nc.all_engine_barrier()
            nc.clear_and_free_semaphores(used)
            nc.all_engine_barrier()

        def sb(scope, name, shape):
            return scope.enter_context(nc.sbuf_tensor(name, shape, F32))

        g = Resident()
        g.h = sb(ctx, "h", [P, KD, T])
        g.squares = sb(ctx, "squares", [P, T])
        g.mod = sb(ctx, "mod", [P, 6 * KD, 2])
        g.cst, g.vec, g.row = sb(ctx, "cst", [P, CST_N]), sb(ctx, "vec", [P, VEC_N]), sb(ctx, "row", [P, ROW_N])
        g.mu_q, g.mu_own = sb(ctx, "mu_q", [P, 27, 4]), sb(ctx, "mu_own", [P, 27])
        g.k_a_c, g.neg_a = sb(ctx, "k_a_c", [P, KD]), sb(ctx, "neg_a", [P, 64])
        g.v = lambda name: g.vec[:, VEC_AT[name][0]:VEC_AT[name][1]]
        g.r = lambda name: g.row[:, ROW_AT[name][0]:ROW_AT[name][1]]
        c = lambda name: g.cst[:, CST_AT[name][0]:CST_AT[name][1]]
        g.ident, g.ones, g.head_ones, g.ident_w = c("ident"), c("ones"), c("head_ones"), c("ident_w")
        g.sel = c("sel")
        g.tri = c("tri").rearrange("p (d f) -> p d f", d=2)
        g.wmask = c("wmask").rearrange("p (d l f) -> p d l f", d=2, f=WC)
        g.reset = c("reset").rearrange("p (d t) -> p d t", d=2)
        g.qmask = c("qmask").rearrange("p (m q) -> p m q", q=4)

        pair = lambda scope, name, tiles: tuple(
            scope.enter_context(nc.sbuf_tensor(f"{name}_{part}", [P, tiles, T], F32R)) for part in ("hi", "lo"))
        run(phase_load, io, g)
        run(phase_modulation, io, g)
        with ExitStack() as mixers:
            g.mix = sb(mixers, "mix", [P, KD, T])
            with ExitStack() as mamba:
                y_tok = sb(mamba, "y_tok", [P, NCH, M_INNER])
                with ExitStack() as scan:
                    xb_tok = sb(scan, "xb_tok", [P, NCH, M_INNER + M_GROUPS * M_STATE])
                    x_tok, b_tok = xb_tok[:, :, 0:M_INNER], xb_tok[:, :, M_INNER:]
                    b_chan, c_chan = g.mix[:, 0:M_GROUPS, :], g.mix[:, M_GROUPS:2 * M_GROUPS, :]
                    with ExitStack() as conv:
                        h = pair(conv, "h1", KD)
                        spare = y_tok[:, :, :].rearrange("p c m -> p (c m)")
                        g.x = g.h
                        xbc = early("w_xbc", lambda t: io["w_xbc"][t], conv_rooms(spare)[0])
                        run(phase_norm, g, "norm1", g.v("norm1"), 0, g.h, h, keep=True, then=xbc)
                        run(phase_conv, io, g, h, spare, xbc, g.mix, xb_tok)
                    dts = {n: sb(scan, n, [P, NCH, 64]) for n in DT_PARTS}
                    run(phase_dt, io, g, dts)
                    run(phase_ssd, io, g, dts, x_tok, b_chan, c_chan, b_tok, y_tok)
                y_chan = sb(mamba, "y_chan", [P, KI, T])
                m_load = early("w_m", lambda t: io["w_m"][t], sb(mamba, "m_w", [P, 2, (KI + KD) * P]))
                run(phase_m_gate, io, g, y_tok, y_chan, m_load)
                run(phase_m_out, io, g, y_chan, m_load)
            g.x = sb(mixers, "x_again", [P, KD, T])
            with ExitStack() as rwkv:
                low = sb(rwkv, "low", [P, 3, T])
                bonus = g.x
                carry = sb(rwkv, "carry", [P, 2, NWC, PAIRS])
                with ExitStack() as inputs:
                    w = sb(inputs, "rkv_w", [P, 2, (3 * KD + 2) * P])
                    rkv_load = early("w_rkv", lambda t: io["w_rkv"][t], w)
                    run(phase_low, io, g, low, rkv_load)
                    run(phase_rwkv_in, io, g, low, bonus, carry, rkv_load)
                run(phase_blocks, io)
                run(phase_solve, io, g)
                with ExitStack() as scan:
                    diagonal = (sb(scan, "bk", [P, 2, 2, PAIRS, P]), sb(scan, "ww", [P, 2, 2, 2, PAIRS, WC]))
                    run(phase_wkv, io, g, carry, diagonal, 0, CTX // WC, None, io["wkv_out"], "wc")
                    run(phase_wkv, io, g, carry, diagonal, CTX // WC, LAT // WC, io["wkv_in"], None, "wl")
                room = sb(rwkv, "raw", [P, 2, 2, KD * P])
                y = pair(rwkv, "y_parts", KD)
                r_load = early("w_r", lambda n: io["w_r"][n], room[:, 0])
                o_load = early("w_o", lambda n: io["w_o"][n], room[:, 1])
                run(phase_wkv_out, io, g, low, bonus, g.h, y, r_load)
                mix = pair(rwkv, "mix", KD)
                run(phase_r_out, io, g, y, mix, r_load, o_load)
                run(phase_residual, g, "w_o", o_load, mix, KD, 2 * KD, squares=True)
            with ExitStack() as ffn:
                h = pair(ffn, "h2", KD)
                part = KF // 2
                room = g.mix[:, :, :].rearrange("p k t -> p (k t)")
                spare = g.mix[:, 0:2, :], g.mix[:, 2:4, :]
                raw_up = room[:, 4 * T:4 * T + 2 * D].rearrange("p (s w) -> p s w", s=2)
                raw_down = g.h[:, :, :].rearrange("p k t -> p (k t)")[:, 0:2 * part * P]\
                    .rearrange("p (s w) -> p s w", s=2)
                ups, downs = [], []
                for n in range(KF // part):
                    ups.append(early(f"up{n}", lambda t, at=2 * n * part: io["w_gu"][t + at], raw_up))
                    downs.append(early(f"down{n}", lambda t, w=io["w_down"][n]: w[t], raw_down))
                run(phase_norm, g, "norm2", g.v("norm2"), 3 * KD, g.h, h, then=ups[0])
                hidden = pair(ffn, "hidden", part)
                for n in range(KF // part):
                    run(phase_up, g, f"up{n}", part, h, spare, ups[n], hidden, downs[n])
                    last = n + 1 == KF // part
                    run(phase_residual, g, f"down{n}", downs[n], hidden, part, 5 * KD,
                        None if last else ups[n + 1], squares=last)
            run(phase_norm, g, "final", g.v("final"), None, g.h, store=io["y"])
        nc.clear_and_free_semaphores(kept)
        nc.all_engine_barrier()


def _tiles(w):
    k, m = w.shape
    return np.ascontiguousarray(w.reshape(k // P, P, m // P, P).transpose(2, 1, 0, 3).reshape(m // P, P, k))


def _cols(v):
    return np.ascontiguousarray(v.reshape(-1, P).T)


def _constants():
    f32 = np.float32
    i, f = np.arange(P)[:, None], np.arange(P)[None, :]
    r, w = np.arange(P)[:, None] % WC, np.arange(WC)[None, :]
    masks = []
    for d in (0, 1):
        a, b = (r, w) if d == 0 else (w, r)
        masks += [b > a, b >= a]
        masks.append((a >= QB) & (b < QB))
    t = np.arange(T)
    ch = (np.arange(27)[None, :, None] * P + np.arange(P)[:, None, None]) // QUARTER
    parts = dict(
        ident=np.eye(P), ones=np.ones((P, P)), head_ones=(i // HD == f // HD),
        tri=np.concatenate([f >= i, f <= i], 1), wmask=np.concatenate(masks, 1),
        reset=np.repeat(np.concatenate([t % WC != 0, t % WC != WC - 1])[None], P, 0),
        qmask=(ch == np.arange(4)[None, None, :]).reshape(P, -1), ident_w=(r == w),
        sel=(np.arange(P)[:, None] % 2 == np.arange(2)[None, :]))
    return np.ascontiguousarray(np.concatenate([parts[n].astype(f32) for n in CST], 1))


def _lay_out(i):
    a = {n: np.asarray(v) for n, v in i.items()}
    l = {n: a[n][0] for n in a if n not in ("c_ctx", "final_norm_w")}
    w_in = l["w_in"]
    o1, o2 = M_INNER, M_INNER + M_INNER + 2 * M_GROUPS * M_STATE
    o3 = o2 + 2 * M_HEADS
    o4 = o3 + R_COLS
    z, xbc, dt, rw, gates = w_in[:, :o1], w_in[:, o1:o2], w_in[:, o2:o3], w_in[:, o3:o4], w_in[:, o4:]
    rt, gt = _tiles(rw), _tiles(gates)
    low_w = rt[[8, 25, 26]]
    up = np.stack([l["w2"].reshape(P, D), l["a2"].reshape(P, D)])
    up = up.reshape(2, P, KD, P).transpose(2, 1, 0, 3).reshape(KD, P, 2 * P)
    rkv_w = np.concatenate([rt[0:8], rt[9:17], rt[17:25], up], 2)
    vec = dict(norm1=l["norm1_w"], norm2=l["norm2_w"], final=a["final_norm_w"],
               conv_b=l["conv_b"], m_norm=l["m_norm_w"], mu=l["mu_shift"], w0=l["w0"], a0=l["a0"],
               k_k=l["k_k"], k_a=l["k_a"], r_k=l["r_k"], lnx_w=l["lnx_w"], lnx_b=l["lnx_b"])
    vec = {n: _cols(v) for n, v in vec.items()}
    vec["b_ada"] = np.repeat(_cols(l["b_ada"]), 2, 1)
    vec["conv_w"] = l["conv_w"].reshape(M_CONV, 24, P).transpose(2, 1, 0).reshape(P, -1)
    row = dict(dt_bias=l["dt_bias"], a_log=l["a_log"], d_skip=l["d_skip"])
    row = np.concatenate([np.repeat(row[n].reshape(1, -1), P, 0) for n in ROW], 1)
    gu = _tiles(l["w_gu"])
    ssm = np.stack([l["state_ssm_fwd"], l["state_ssm_bwd"]])
    ssm = ssm.reshape(2, M_GROUPS, GI, M_STATE).transpose(0, 1, 3, 2)
    wkv = np.stack([l["state_wkv_fwd"], l["state_wkv_bwd"]])
    wkv = wkv.reshape(2, PAIRS, 2, HD, HD).transpose(0, 2, 4, 1, 3).reshape(2, P, PAIRS * HD)
    x = np.concatenate([a["x_prompt"][0], a["x_sample"][0]], 0)
    out = dict(
        x_t=x.T.reshape(KD, P, T), cond=np.stack([_cols(a["c_ctx"]), _cols(a["c"])], 2), cst=_constants(),
        vec=np.concatenate([vec[n] for n in VEC], 1), row=row,
        w_ada=l["w_ada"].reshape(KD, P, 12, 512).transpose(2, 1, 0, 3).reshape(12, P, KD * 512),
        w_xbc=_tiles(xbc), w_dt=dt.reshape(KD, P, 64).transpose(1, 0, 2).reshape(P, -1),
        w_z=z.reshape(KD, P, M_GROUPS, GI).transpose(2, 1, 0, 3).reshape(M_GROUPS, P, -1),
        w_m=np.concatenate([_tiles(l["w_m_out"]), gt[:KD]], 2), w_low=low_w, w_rkv=rkv_w,
        w_r=_tiles(l["w_r_out"]), w_r_gate=gt[KD:], w_o=_tiles(l["w_o"]),
        w_gu=np.stack([gu[:KF], gu[KF:]], 1).reshape(2 * KF, P, D),
        w_down=np.stack(np.split(_tiles(l["w_down"]), 2, 2)), g2=l["g2"], ssm_in=ssm, wkv_in=wkv)
    return {n: np.ascontiguousarray(v) for n, v in out.items()}


OUTS = dict(y=[KD, P, T], ssm_out=[2, M_GROUPS, M_STATE, GI], wkv_out=[2, P, PAIRS * HD])
SCRATCH = dict(chan=[2, NWC, P, 4 * PAIRS * WC], tok=[2, T, 2 * D], val=[T, D], wkv_y=[2, NWC, P, PAIRS * HD],
               cs_rows=[NCH, 64, P],
               blk_m=[NWC, 4, 2, PAIRS, QB * QB], blk_w=[NWC, 4, 2, 2, PAIRS, QB * QB],
               gate_r=[KD, P, T])


def declare(nc, arrays):
    io = {}
    for name, a in arrays.items():
        io[name] = nc.dram_tensor("in_" + name, a.shape, F32, kind="ExternalInput").ap()
    for name, shape in OUTS.items():
        io[name] = nc.dram_tensor("out_" + name, shape, F32, kind="ExternalOutput").ap()
    for name, shape in SCRATCH.items():
        io[name] = nc.dram_tensor("scratch_" + name, shape, F32, kind="Internal").ap()
    return io


def kernel(**inputs):
    import concourse.bacc as bacc
    from concourse.bass_utils import run_bass_kernel_spmd

    nc = bacc.Bacc("TRN2", target_bir_lowering=False, num_devices=1)
    arrays = _lay_out(inputs)
    build(nc, declare(nc, arrays))
    sent = {"in_" + name: a for name, a in arrays.items()}
    got = run_bass_kernel_spmd(nc, [sent], core_ids=[0]).results[0]
    y = np.asarray(got["out_y"]).reshape(D, T).T
    ssm = np.asarray(got["out_ssm_out"]).transpose(0, 1, 3, 2).reshape(2, 1, 1, M_HEADS, HD, M_STATE)
    wkv = np.asarray(got["out_wkv_out"]).reshape(2, 2, HD, PAIRS, HD).transpose(0, 3, 1, 4, 2)
    wkv = wkv.reshape(2, 1, 1, R_HEADS, HD, HD)
    return y[None, :CTX], y[None, CTX:], ssm[0], ssm[1], wkv[0], wkv[1]
```
